# Optimizing a Trainium2 kernel written in Bass

```python
import math
import jax
import jax.numpy as jnp
from jax import lax
import numpy as np
import jax, jax.numpy as jnp

D_MODEL = 2048
BATCH = 1
SEQ = 256
DEPTH = 1

N_MIXERS = 3
PLE_DIM = 256
NORM_EPS = 1e-6
NEG_INF = -1e30
TINY = 1e-30
Q_BLOCK = 128

N_BUCKETS = 32
BUCKET_MAX_DIST = 2048
N_BIAS_HEADS = 16

LRU_WIDTH = D_MODEL
LRU_BLOCKS = 8
LRU_BLOCK_W = LRU_WIDTH // LRU_BLOCKS
CONV_W = 4
LRU_C = 8.0

DIL_PATTERNS = ((128, 1), (512, 4), (2048, 16))
N_DIL = len(DIL_PATTERNS)
DIL_HEADS = 16
DIL_HEAD_DIM = 64
DIL_WIDTH = DIL_HEADS * DIL_HEAD_DIM
DIL_IN_COLS = N_DIL * 3 * DIL_WIDTH + DIL_WIDTH

NSA_HEADS = 16
NSA_KV_GROUPS = 4
NSA_REP = NSA_HEADS // NSA_KV_GROUPS
NSA_HEAD_DIM = 128
NSA_WIDTH = NSA_HEADS * NSA_HEAD_DIM
NSA_KV_WIDTH = NSA_KV_GROUPS * NSA_HEAD_DIM
CMP_BLOCK = 32
CMP_STRIDE = 16
CMP_HIDDEN = 512
SEL_BLOCK = 64
SEL_TOPK = 16
WIN = 512
SEL_QCHUNK = 16
FORCE_BONUS = 1e4
NSA_SPLITS = (NSA_WIDTH,) + (NSA_KV_WIDTH,) * 6 + (3 * NSA_HEADS, NSA_WIDTH)
NSA_IN_COLS = sum(NSA_SPLITS)


def _rmsnorm(x, g):
    xf = x.astype(jnp.float32)
    y = xf * lax.rsqrt(jnp.mean(xf * xf, axis=-1, keepdims=True) + NORM_EPS)
    return (y * g.astype(jnp.float32)).astype(x.dtype)

def _t5_bucket(dist):
    n = jnp.maximum(dist, 0)
    max_exact = N_BUCKETS // 2
    nf = jnp.maximum(n, max_exact).astype(jnp.float32)
    large = max_exact + (jnp.log(nf / max_exact) / math.log(BUCKET_MAX_DIST / max_exact)
                         * (N_BUCKETS - max_exact)).astype(jnp.int32)
    return jnp.where(n < max_exact, n, jnp.minimum(large, N_BUCKETS - 1))

def _masked_softmax(logits, mask):
    l = jnp.where(mask, logits, NEG_INF)
    m = jnp.max(l, axis=-1, keepdims=True)
    e = jnp.where(mask, jnp.exp(l - m), 0.0)
    s = jnp.sum(e, axis=-1, keepdims=True)
    return e / jnp.maximum(s, TINY), m[..., 0], s[..., 0]

def _unblock(t, length):
    nb, n, qb = t.shape[:3]
    t = jnp.moveaxis(t, 0, 1).reshape((n, nb * qb) + t.shape[3:])
    return t[:, :length]

def _banded_attention(q, k, v, rel_bias, lookback, max_delta, dilation):
    n, length, G, R, dh = q.shape
    nb = -(-length // Q_BLOCK)
    lp = nb * Q_BLOCK
    qp = jnp.pad(q, ((0, 0), (0, lp - length), (0, 0), (0, 0), (0, 0)))
    kp = jnp.pad(k, ((0, 0), (lookback, lp - length), (0, 0), (0, 0)))
    vp = jnp.pad(v, ((0, 0), (lookback, lp - length), (0, 0), (0, 0)))
    table = rel_bias.reshape(N_BUCKETS, G, R)
    span = Q_BLOCK + lookback
    scale = dh ** -0.5

    def block(b):
        q0 = b * Q_BLOCK
        qs = lax.dynamic_slice_in_dim(qp, q0, Q_BLOCK, axis=1)
        ks = lax.dynamic_slice_in_dim(kp, q0, span, axis=1)
        vs = lax.dynamic_slice_in_dim(vp, q0, span, axis=1)
        qpos = q0 + jnp.arange(Q_BLOCK)
        kpos = q0 - lookback + jnp.arange(span)
        delta = qpos[:, None] - kpos[None, :]
        mask = (delta >= 0) & (delta <= max_delta) & (kpos[None, :] >= 0)
        bias = jnp.transpose(table[_t5_bucket(delta * dilation)], (2, 3, 0, 1)).astype(jnp.float32)
        logits = jnp.einsum('nqgrd,nkgd->ngrqk', qs, ks).astype(jnp.float32) * scale + bias
        prob, m, s = _masked_softmax(logits, mask)
        o = jnp.einsum('ngrqk,nkgd->nqgrd', prob, vs.astype(jnp.float32))
        return o, jnp.transpose(m, (0, 3, 1, 2)), jnp.transpose(s, (0, 3, 1, 2))

    o, m, s = lax.map(block, jnp.arange(nb))
    return _unblock(o, length), _unblock(m, length), _unblock(s, length)

def _to_strided(t, d):
    bn, s = t.shape[:2]
    rest = t.shape[2:]
    t = jnp.swapaxes(t.reshape((bn, s // d, d) + rest), 1, 2)
    return t.reshape((bn * d, s // d) + rest)

def _from_strided(t, d, bn):
    n, length = t.shape[:2]
    rest = t.shape[2:]
    t = jnp.swapaxes(t.reshape((bn, d, length) + rest), 1, 2)
    return t.reshape((bn, length * d) + rest)

def _rglru_mixer(u, w_in, conv_w, conv_b, w_r, b_r, w_i, b_i, lam, w_out):
    bn, s, _ = u.shape
    proj = u @ w_in
    xb, gate = proj[..., :LRU_WIDTH], proj[..., LRU_WIDTH:]
    xc = lax.conv_general_dilated(xb, conv_w[:, None, :], window_strides=(1,),
                                  padding=((CONV_W - 1, 0),),
                                  dimension_numbers=('NWC', 'WIO', 'NWC'),
                                  feature_group_count=LRU_WIDTH) + conv_b
    xblk = xc.reshape(bn, s, LRU_BLOCKS, LRU_BLOCK_W)
    r = jax.nn.sigmoid(jnp.einsum('bsnc,ncd->bsnd', xblk, w_r) + b_r).reshape(bn, s, LRU_WIDTH)
    i = jax.nn.sigmoid(jnp.einsum('bsnc,ncd->bsnd', xblk, w_i) + b_i).reshape(bn, s, LRU_WIDTH)
    log_a = -LRU_C * r.astype(jnp.float32) * jax.nn.softplus(-lam.astype(jnp.float32))
    a = jnp.exp(log_a)
    bterm = jnp.sqrt(-jnp.expm1(2.0 * log_a)) * (i * xc).astype(jnp.float32)

    def combine(e1, e2):
        a1, b1 = e1
        a2, b2 = e2
        return a1 * a2, a2 * b1 + b2

    _, h = lax.associative_scan(combine, (a, bterm), axis=1)
    y = h.astype(u.dtype) * jax.nn.silu(gate)
    return y @ w_out

def _dilated_mixer(u, w_in, w_out, rel_bias):
    bn, s, _ = u.shape
    proj = u @ w_in
    qkv = proj[..., :N_DIL * 3 * DIL_WIDTH].reshape(bn, s, N_DIL, 3, DIL_HEADS, 1, DIL_HEAD_DIM)
    gate = proj[..., N_DIL * 3 * DIL_WIDTH:]
    outs, maxes, dens = [], [], []
    for gi, (window, dil) in enumerate(DIL_PATTERNS):
        q = _to_strided(qkv[:, :, gi, 0], dil)
        k = _to_strided(qkv[:, :, gi, 1, :, 0], dil)
        v = _to_strided(qkv[:, :, gi, 2, :, 0], dil)
        o, m, den = _banded_attention(q, k, v, rel_bias, window // dil, window // dil, dil)
        outs.append(_from_strided(o[:, :, :, 0], dil, bn))
        maxes.append(_from_strided(m[:, :, :, 0], dil, bn))
        dens.append(_from_strided(den[:, :, :, 0], dil, bn))
    o = jnp.stack(outs)
    m = jnp.stack(maxes)
    den = jnp.stack(dens)
    wts = den * jnp.exp(m - jnp.max(m, axis=0, keepdims=True))
    o = jnp.sum(wts[..., None] * o, axis=0) / jnp.sum(wts, axis=0)[..., None]
    y = o.reshape(bn, s, DIL_WIDTH).astype(u.dtype) * jax.nn.silu(gate)
    return y @ w_out

def _compress(t, cidx, pos, w1, w2):
    bn, nc = t.shape[0], cidx.shape[0]
    blk = t[:, cidx] + pos[None, None, :, None, :]
    blk = jnp.swapaxes(blk, 2, 3).reshape(bn, nc, NSA_KV_GROUPS, CMP_BLOCK * NSA_HEAD_DIM)
    return jax.nn.gelu(blk @ w1) @ w2

def _nsa_mixer(u, w_in, pos_k, w1_k, w2_k, pos_v, w1_v, w2_v, w_out, rel_bias):
    bn, s, _ = u.shape
    G, R, dh = NSA_KV_GROUPS, NSA_REP, NSA_HEAD_DIM
    scale = dh ** -0.5
    proj = u @ w_in
    offs = np.cumsum(NSA_SPLITS)[:-1].tolist()
    q, kc, vc, ksl, vsl, kw, vw, bgate, gpath = jnp.split(proj, offs, axis=-1)
    q = q.reshape(bn, s, G, R, dh)
    kc, vc, ksl, vsl, kw, vw = [t.reshape(bn, s, G, dh) for t in (kc, vc, ksl, vsl, kw, vw)]

    nc = (s - CMP_BLOCK) // CMP_STRIDE + 1
    cidx = np.arange(nc)[:, None] * CMP_STRIDE + np.arange(CMP_BLOCK)[None, :]
    cend = cidx[:, -1]
    kcmp = _compress(kc, cidx, pos_k, w1_k, w2_k)
    vcmp = _compress(vc, cidx, pos_v, w1_v, w2_v)
    nsel = s // SEL_BLOCK
    topk = min(SEL_TOPK, nsel)
    sel_start = np.arange(nsel) * SEL_BLOCK
    cover = jnp.asarray(((cidx[:, :1] < sel_start[None, :] + SEL_BLOCK)
                         & (cidx[:, -1:] >= sel_start[None, :])).astype(np.float32))
    blk_ids = jnp.arange(nsel)

    def cmp_block(b):
        q0 = b * Q_BLOCK
        qs = lax.dynamic_slice_in_dim(q, q0, Q_BLOCK, axis=1)
        t = q0 + jnp.arange(Q_BLOCK)
        mask = cend[None, :] <= t[:, None]
        logits = jnp.einsum('bqgrd,bcgd->bgrqc', qs, kcmp).astype(jnp.float32) * scale
        prob, _, _ = _masked_softmax(logits, mask)
        o = jnp.einsum('bgrqc,bcgd->bqgrd', prob, vcmp.astype(jnp.float32))
        imp = jnp.einsum('bgrqc,cn->bgqn', prob, cover)
        cur = t // SEL_BLOCK
        forced = ((blk_ids[None, :] == 0) | (blk_ids[None, :] == cur[:, None])
                  | (blk_ids[None, :] == cur[:, None] - 1)).astype(jnp.float32)
        valid = blk_ids[None, :] * SEL_BLOCK <= t[:, None]
        imp = jnp.where(valid, imp + FORCE_BONUS * forced, NEG_INF)
        _, idx = lax.top_k(imp, topk)
        return o, jnp.transpose(idx, (0, 2, 1, 3))

    o_cmp, sel_idx = lax.map(cmp_block, jnp.arange(s // Q_BLOCK))
    o_cmp = _unblock(o_cmp, s)
    sel_idx = _unblock(sel_idx, s)

    ksT = jnp.swapaxes(ksl, 1, 2)
    vsT = jnp.swapaxes(vsl, 1, 2)
    nkeys = topk * SEL_BLOCK
    tgr = jnp.transpose(rel_bias.reshape(N_BUCKETS, G, R), (1, 2, 0))
    g_ix = jnp.arange(G)[None, :, None, None, None]
    r_ix = jnp.arange(R)[None, None, :, None, None]
    gather = jax.vmap(jax.vmap(lambda a, ix: a[ix]))

    def sel_chunk(c):
        q0 = c * SEL_QCHUNK
        qs = lax.dynamic_slice_in_dim(q, q0, SEL_QCHUNK, axis=1)
        idx = lax.dynamic_slice_in_dim(sel_idx, q0, SEL_QCHUNK, axis=1)
        tok = idx[..., None] * SEL_BLOCK + jnp.arange(SEL_BLOCK)
        tok = jnp.transpose(tok.reshape(bn, SEL_QCHUNK, G, nkeys), (0, 2, 1, 3))
        flat = tok.reshape(bn, G, SEL_QCHUNK * nkeys)
        kg = gather(ksT, flat).reshape(bn, G, SEL_QCHUNK, nkeys, dh)
        vg = gather(vsT, flat).reshape(bn, G, SEL_QCHUNK, nkeys, dh)
        t = q0 + jnp.arange(SEL_QCHUNK)
        delta = t[None, None, :, None] - tok
        bias = tgr[g_ix, r_ix, _t5_bucket(delta)[:, :, None]].astype(jnp.float32)
        logits = jnp.einsum('bqgrd,bgqnd->bgrqn', qs, kg).astype(jnp.float32) * scale + bias
        prob, _, _ = _masked_softmax(logits, (delta >= 0)[:, :, None])
        return jnp.einsum('bgrqn,bgqnd->bqgrd', prob, vg.astype(jnp.float32))

    o_sel = _unblock(lax.map(sel_chunk, jnp.arange(s // SEL_QCHUNK)), s)

    o_win, _, _ = _banded_attention(q, kw, vw, rel_bias, WIN, WIN - 1, 1)

    gts = jax.nn.sigmoid(bgate.reshape(bn, s, G, R, 3).astype(jnp.float32))
    o = gts[..., 0:1] * o_cmp + gts[..., 1:2] * o_sel + gts[..., 2:3] * o_win
    y = o.reshape(bn, s, NSA_WIDTH).astype(u.dtype) * jax.nn.silu(gpath)
    return y @ w_out

def first_inputs(seed: int = 0) -> dict:
    key = jax.random.key(seed)
    ks = iter(jax.random.split(key, 40))
    n_a = len(range(0, DEPTH, N_MIXERS))
    n_b = len(range(1, DEPTH, N_MIXERS))
    n_c = len(range(2, DEPTH, N_MIXERS))

    def nrm(shape, scale):
        return scale * jax.random.normal(next(ks), shape, jnp.float32)

    a_dec = jax.random.uniform(next(ks), (n_a, LRU_WIDTH), jnp.float32, minval=0.9, maxval=0.999)
    return {
        "x": nrm((BATCH, SEQ, D_MODEL), 1.0),
        "p": nrm((DEPTH, BATCH, SEQ, PLE_DIM), 1.0),
        "rel_bias": nrm((N_BUCKETS, N_BIAS_HEADS), 0.5),
        "norm_pre": 1.0 + nrm((DEPTH, D_MODEL), 0.05),
        "norm_post": 1.0 + nrm((DEPTH, D_MODEL), 0.05),
        "ple_w_proj": nrm((DEPTH, PLE_DIM, D_MODEL), PLE_DIM ** -0.5),
        "ple_w_gate": nrm((DEPTH, D_MODEL, D_MODEL), D_MODEL ** -0.5),
        "a_w_in": nrm((n_a, D_MODEL, 2 * LRU_WIDTH), D_MODEL ** -0.5),
        "a_conv_w": nrm((n_a, CONV_W, LRU_WIDTH), CONV_W ** -0.5),
        "a_conv_b": nrm((n_a, LRU_WIDTH), 0.01),
        "a_w_r": nrm((n_a, LRU_BLOCKS, LRU_BLOCK_W, LRU_BLOCK_W), LRU_BLOCK_W ** -0.5),
        "a_b_r": nrm((n_a, LRU_BLOCKS, LRU_BLOCK_W), 0.01),
        "a_w_i": nrm((n_a, LRU_BLOCKS, LRU_BLOCK_W, LRU_BLOCK_W), LRU_BLOCK_W ** -0.5),
        "a_b_i": nrm((n_a, LRU_BLOCKS, LRU_BLOCK_W), 0.01),
        "a_lam": jnp.log(a_dec) - jnp.log1p(-a_dec),
        "a_w_out": nrm((n_a, LRU_WIDTH, D_MODEL), LRU_WIDTH ** -0.5),
        "b_w_in": nrm((n_b, D_MODEL, DIL_IN_COLS), D_MODEL ** -0.5),
        "b_w_out": nrm((n_b, DIL_WIDTH, D_MODEL), DIL_WIDTH ** -0.5),
        "c_w_in": nrm((n_c, D_MODEL, NSA_IN_COLS), D_MODEL ** -0.5),
        "c_cmp_pos_k": nrm((n_c, CMP_BLOCK, NSA_HEAD_DIM), 0.1),
        "c_cmp_w1_k": nrm((n_c, CMP_BLOCK * NSA_HEAD_DIM, CMP_HIDDEN), (CMP_BLOCK * NSA_HEAD_DIM) ** -0.5),
        "c_cmp_w2_k": nrm((n_c, CMP_HIDDEN, NSA_HEAD_DIM), CMP_HIDDEN ** -0.5),
        "c_cmp_pos_v": nrm((n_c, CMP_BLOCK, NSA_HEAD_DIM), 0.1),
        "c_cmp_w1_v": nrm((n_c, CMP_BLOCK * NSA_HEAD_DIM, CMP_HIDDEN), (CMP_BLOCK * NSA_HEAD_DIM) ** -0.5),
        "c_cmp_w2_v": nrm((n_c, CMP_HIDDEN, NSA_HEAD_DIM), CMP_HIDDEN ** -0.5),
        "c_w_out": nrm((n_c, NSA_WIDTH, D_MODEL), NSA_WIDTH ** -0.5),
    }

def first_block(x, p, rel_bias, norm_pre, norm_post, ple_w_proj, ple_w_gate,
              a_w_in, a_conv_w, a_conv_b, a_w_r, a_b_r, a_w_i, a_b_i, a_lam, a_w_out,
              b_w_in, b_w_out,
              c_w_in, c_cmp_pos_k, c_cmp_w1_k, c_cmp_w2_k, c_cmp_pos_v, c_cmp_w1_v, c_cmp_w2_v, c_w_out):
    h = x
    for i in range(DEPTH):
        kind = i % N_MIXERS
        j = i // N_MIXERS
        u = _rmsnorm(h, norm_pre[i])
        if kind == 0:
            y = _rglru_mixer(u, a_w_in[j], a_conv_w[j], a_conv_b[j], a_w_r[j], a_b_r[j],
                             a_w_i[j], a_b_i[j], a_lam[j], a_w_out[j])
        elif kind == 1:
            y = _dilated_mixer(u, b_w_in[j], b_w_out[j], rel_bias)
        else:
            y = _nsa_mixer(u, c_w_in[j], c_cmp_pos_k[j], c_cmp_w1_k[j], c_cmp_w2_k[j],
                           c_cmp_pos_v[j], c_cmp_w1_v[j], c_cmp_w2_v[j], c_w_out[j], rel_bias)
        h = h + _rmsnorm(y, norm_post[i])
        h = h + jax.nn.sigmoid(h @ ple_w_gate[i]) * (p[i] @ ple_w_proj[i])
    return h


N_BRANCHES = 3
POOL_WINDOWS = (2, 4, 8, 16)
N_POOL_GROUPS = 4
POOL_DIM = D_MODEL // 2
POOL_GROUP_DIM = POOL_DIM // N_POOL_GROUPS
CONV_DIM = D_MODEL // 2
CONV_WIDTH = 3
N_HEADS = 8
HEAD_DIM = 128
N_KV_HEADS = 2
GROUP = N_HEADS // N_KV_HEADS
ATTN_DIM = N_HEADS * HEAD_DIM
IDX_HEADS = 16
IDX_DIM = 64
TOPK_MAX = 256
NUM_BUCKETS = 32
MAX_EXACT = NUM_BUCKETS // 2
MAX_DISTANCE = 128
BRANCH_DIM = D_MODEL // 2
MLP_HIDDEN = 4 * D_MODEL
IN_SPLITS = (POOL_DIM, CONV_DIM, CONV_DIM, CONV_DIM, ATTN_DIM, N_KV_HEADS * HEAD_DIM,
             N_KV_HEADS * HEAD_DIM, IDX_HEADS * IDX_DIM, IDX_DIM, IDX_HEADS)
IN_WIDTH = sum(IN_SPLITS)


def _split_points():
    pts, acc = [], 0
    for w in IN_SPLITS[:-1]:
        acc += w
        pts.append(acc)
    return pts

def rmsnorm(x, g):
    xf = x.astype(jnp.float32)
    y = xf * lax.rsqrt(jnp.mean(jnp.square(xf), axis=-1, keepdims=True) + NORM_EPS)
    return (y * g.astype(jnp.float32)).astype(x.dtype)

def t5_bucket(dist):
    n = jnp.maximum(dist, 0)
    nf = jnp.maximum(n, 1).astype(jnp.float32)
    large = MAX_EXACT + (jnp.log(nf / MAX_EXACT) / math.log(MAX_DISTANCE / MAX_EXACT)
                         * (NUM_BUCKETS - MAX_EXACT)).astype(jnp.int32)
    large = jnp.minimum(large, NUM_BUCKETS - 1)
    return jnp.where(n < MAX_EXACT, n, large)

def pool_mixer(u, pool_w, pool_scale):
    B, S, _ = u.shape
    ug = u.astype(jnp.float32).reshape(B, S, N_POOL_GROUPS, POOL_GROUP_DIM)
    c0 = jnp.concatenate([jnp.zeros((B, 1, N_POOL_GROUPS, POOL_GROUP_DIM), jnp.float32),
                          jnp.cumsum(ug, axis=1)], axis=1)
    t = jnp.arange(S)
    win = jnp.array(POOL_WINDOWS, jnp.int32)
    lo = jnp.maximum(t[:, None] + 1 - win[None, :], 0)
    g_ar = jnp.arange(N_POOL_GROUPS)[None, :]
    window_sum = c0[:, 1:] - c0[:, lo, g_ar]
    cnt = (t[:, None] + 1 - lo).astype(jnp.float32)[None, :, :, None]
    d = window_sum / cnt - ug
    y = jnp.einsum('bsgc,gcd->bsgd', d, pool_w.astype(jnp.float32))
    return (y.reshape(B, S, POOL_DIM) * pool_scale.astype(jnp.float32)).astype(u.dtype)

def conv_mixer(u, gate_c, gate_b, conv_w):
    z = gate_c * u
    y = lax.conv_general_dilated(z, conv_w[:, None, :], window_strides=(1,),
                                 padding=[(CONV_WIDTH - 1, 0)],
                                 dimension_numbers=('NWC', 'WIO', 'NWC'),
                                 feature_group_count=CONV_DIM)
    return gate_b * y

def sparse_attention(q, k, v, q_idx, k_idx, w_idx, rel_bias):
    B, S = q.shape[0], q.shape[1]
    topk = min(TOPK_MAX, S // 4)
    nblk = S // Q_BLOCK
    key_pos = jnp.arange(S)
    k_idx32 = k_idx.astype(jnp.float32)
    table = rel_bias.astype(jnp.float32)

    def to_blocks(a):
        return jnp.moveaxis(a.reshape((B, nblk, Q_BLOCK) + a.shape[2:]), 1, 0)

    def block_fn(args):
        qb, qib, wb, blk = args
        q_pos = blk * Q_BLOCK + jnp.arange(Q_BLOCK)
        dots = jnp.einsum('bthd,bsd->bths', qib.astype(jnp.float32), k_idx32)
        score = jnp.einsum('bth,bths->bts', wb.astype(jnp.float32) * IDX_HEADS ** -0.5,
                           jax.nn.relu(dots))
        causal = key_pos[None, :] <= q_pos[:, None]
        score = jnp.where(causal[None], score, -jnp.inf)
        _, idx = lax.top_k(score, topk)
        k_sel = jax.vmap(lambda kb, ib: kb[ib])(k, idx)
        v_sel = jax.vmap(lambda vb, ib: vb[ib])(v, idx)
        qg = qb.reshape(B, Q_BLOCK, N_KV_HEADS, GROUP, HEAD_DIM).astype(jnp.float32)
        logits = jnp.einsum('btgrd,btkgd->btgrk', qg, k_sel.astype(jnp.float32)) * HEAD_DIM ** -0.5
        dist = q_pos[None, :, None] - idx
        bias = table[t5_bucket(dist)]
        bias = bias.reshape(B, Q_BLOCK, topk, N_KV_HEADS, GROUP).transpose(0, 1, 3, 4, 2)
        logits = jnp.where((dist >= 0)[:, :, None, None, :], logits + bias, -jnp.inf)
        p = jax.nn.softmax(logits, axis=-1)
        o = jnp.einsum('btgrk,btkgd->btgrd', p, v_sel.astype(jnp.float32))
        return o.reshape(B, Q_BLOCK, ATTN_DIM).astype(q.dtype)

    out = lax.map(block_fn, (to_blocks(q), to_blocks(q_idx), to_blocks(w_idx),
                             jnp.arange(nblk, dtype=jnp.int32)))
    return jnp.moveaxis(out, 0, 1).reshape(B, S, ATTN_DIM)

def second_inputs(seed: int = 0) -> dict:
    key = jax.random.key(seed)
    ks = jax.random.split(key, 13)

    def nrm(k, shape, scale):
        return jax.random.normal(k, shape, jnp.float32) * scale

    return {
        'x': nrm(ks[0], (BATCH, SEQ, D_MODEL), 1.0),
        'norm_gains': 1.0 + nrm(ks[1], (DEPTH, 4, D_MODEL), 0.05),
        'w_in': nrm(ks[2], (DEPTH, D_MODEL, IN_WIDTH), D_MODEL ** -0.5),
        'pool_w': nrm(ks[3], (DEPTH, N_POOL_GROUPS, POOL_GROUP_DIM, POOL_GROUP_DIM), POOL_GROUP_DIM ** -0.5),
        'pool_scale': 1.0 + nrm(ks[4], (DEPTH, POOL_DIM), 0.05),
        'conv_w': nrm(ks[5], (DEPTH, CONV_WIDTH, CONV_DIM), CONV_WIDTH ** -0.5),
        'rel_bias': nrm(ks[6], (NUM_BUCKETS, N_HEADS), 0.5),
        'w_branch': nrm(ks[7], (DEPTH, N_BRANCHES, BRANCH_DIM, D_MODEL), BRANCH_DIM ** -0.5),
        'w_gate': nrm(ks[8], (DEPTH, D_MODEL, N_BRANCHES * D_MODEL), D_MODEL ** -0.5),
        'b_gate': nrm(ks[9], (DEPTH, N_BRANCHES, D_MODEL), 0.1),
        'w_out': nrm(ks[10], (DEPTH, D_MODEL, D_MODEL), D_MODEL ** -0.5),
        'w_up': nrm(ks[11], (DEPTH, D_MODEL, MLP_HIDDEN), D_MODEL ** -0.5),
        'w_down': nrm(ks[12], (DEPTH, MLP_HIDDEN, D_MODEL), MLP_HIDDEN ** -0.5),
    }

def second_block(x, norm_gains, w_in, pool_w, pool_scale, conv_w, rel_bias, w_branch,
              w_gate, b_gate, w_out, w_up, w_down):
    B, S, D = x.shape
    pts = _split_points()
    for l in range(DEPTH):
        g = norm_gains[l]
        h = rmsnorm(x, g[0])
        proj = h @ w_in[l]
        (u_pool, u_conv, c_gate, b_gate_conv, q, k, v, qi, ki, wi) = jnp.split(proj, pts, axis=-1)
        y_pool = pool_mixer(u_pool, pool_w[l], pool_scale[l])
        y_conv = conv_mixer(u_conv, c_gate, b_gate_conv, conv_w[l])
        y_attn = sparse_attention(q.reshape(B, S, N_HEADS, HEAD_DIM),
                                  k.reshape(B, S, N_KV_HEADS, HEAD_DIM),
                                  v.reshape(B, S, N_KV_HEADS, HEAD_DIM),
                                  qi.reshape(B, S, IDX_HEADS, IDX_DIM), ki, wi, rel_bias)
        branches = jnp.stack([y_pool, y_conv, y_attn], axis=2)
        up = jnp.einsum('bsnc,ncd->bsnd', branches, w_branch[l])
        gates = jax.nn.sigmoid((h @ w_gate[l]).reshape(B, S, N_BRANCHES, D) + b_gate[l])
        mixed = jnp.sum(gates * up, axis=2) @ w_out[l]
        x = x + rmsnorm(mixed, g[1])
        h = rmsnorm(x, g[2])
        m = jnp.square(jax.nn.relu(h @ w_up[l])) @ w_down[l]
        x = x + rmsnorm(m, g[3])
    return x


def setup_inputs(seed=0):
    out = dict(first_inputs(seed))
    for name, value in second_inputs(seed + 1).items():
        if name != "x":
            out[name + "_2"] = value
    return out


def reference(
    x, p, rel_bias, norm_pre, norm_post, ple_w_proj, ple_w_gate, a_w_in, a_conv_w, a_conv_b,
    a_w_r, a_b_r, a_w_i, a_b_i, a_lam, a_w_out, b_w_in, b_w_out, c_w_in, c_cmp_pos_k,
    c_cmp_w1_k, c_cmp_w2_k, c_cmp_pos_v, c_cmp_w1_v, c_cmp_w2_v, c_w_out, norm_gains_2, w_in_2,
    pool_w_2, pool_scale_2, conv_w_2, rel_bias_2, w_branch_2, w_gate_2, b_gate_2, w_out_2,
    w_up_2, w_down_2,
):
    x = first_block(
        x, p, rel_bias, norm_pre, norm_post, ple_w_proj, ple_w_gate, a_w_in, a_conv_w, a_conv_b,
        a_w_r, a_b_r, a_w_i, a_b_i, a_lam, a_w_out, b_w_in, b_w_out, c_w_in, c_cmp_pos_k,
        c_cmp_w1_k, c_cmp_w2_k, c_cmp_pos_v, c_cmp_w1_v, c_cmp_w2_v, c_w_out,
    )
    return second_block(
        x, norm_gains_2, w_in_2, pool_w_2, pool_scale_2, conv_w_2, rel_bias_2, w_branch_2,
        w_gate_2, b_gate_2, w_out_2, w_up_2, w_down_2,
    )


_drawn_inputs = setup_inputs


def setup_inputs(seed=0):
    import zlib

    import numpy as np

    out = dict(_drawn_inputs(seed))
    spreads = {}
    factors = {'a_b_r': 32.078, 'a_b_i': 8.0, 'pool_scale_2': 3.157, 'rel_bias_2': 2.752}
    for name, (base, spread) in spreads.items():
        noise = np.random.default_rng([zlib.crc32(name.encode()), seed]).standard_normal(out[name].shape)
        drawn = base * np.exp(spread * noise) if base else spread * noise
        out[name] = jnp.asarray(drawn.astype(out[name].dtype))
    for name, factor in factors.items():
        out[name] = (out[name] * factor).astype(out[name].dtype)
    return out
```

```python
from contextlib import ExitStack

import numpy as np

import concourse.bass as bass
from concourse import mybir

F32 = mybir.dt.float32
F32R = mybir.dt.float32r
BF16 = mybir.dt.bfloat16
ALU = mybir.AluOpType
ACT = mybir.ActivationFunctionType
AX_X = mybir.AxisListType.X

P = 128
T = 256
D = 2048
KT = D // P
EPS = 1e-6
CONV_W = 4
LRU_C = 8.0
PLE = 256
POOL_WINDOWS = (2, 4, 8, 16)
PAD_POOL = 16
HALF = D // 2
CONV2_W = 3
HEADS = 8
HD = 128
KV_HEADS = 2
GROUP = HEADS // KV_HEADS
IDX_HEADS = 16
IDX_DIM = 64
TOPK = T // 4
BUCKETS = 32
MAX_EXACT = BUCKETS // 2
MAX_DIST = 128
MLP = 4 * D
TOK_TILES = T // P
REV = P - 1 + T
MASKED = -1e38
TAKEN = -3e38
UNSELECTED = -1e30

WCOLS = 1024
CHUNK = 512
N_STAGE = 4
N_SPLIT = 3
AHEAD = N_SPLIT - 1

C_POOL, C_UCONV, C_CGATE, C_BGATE, C_Q, C_KV, C_QI, C_KI, C_WI = (
    0, 1024, 2048, 3072, 4096, 5120, 5632, 6656, 6720)
TAIL = 2 * IDX_DIM + IDX_HEADS

VEC_SIZES = [("norm_pre", KT), ("norm_post", KT), ("gain0", KT), ("gain1", KT), ("gain2", KT), ("gain3", KT),
             ("a_conv_w", KT * CONV_W), ("a_conv_b", KT), ("b_r", KT), ("b_i", KT), ("lam", KT),
             ("pool_scale", HALF // P), ("conv_w", HALF // P * CONV2_W), ("b_gate", 3 * KT)]
VEC = {}
VEC_COLS = 0
for _name, _n in VEC_SIZES:
    VEC[_name] = (VEC_COLS, _n)
    VEC_COLS += _n

CST = {"ident": (0, P), "flip": (P, P), "inv_count": (2 * P, 4 * PAD_POOL), "eps": (2 * P + 4 * PAD_POOL, 1)}
CST_COLS = 2 * P + 4 * PAD_POOL + 1


def shape_constants():
    cst = np.zeros((P, CST_COLS), np.float32)
    cst[:, 0:P] = np.eye(P)
    cst[:, P:2 * P] = np.eye(P)[::-1]
    for g, w in enumerate(POOL_WINDOWS):
        at = CST["inv_count"][0] + g * PAD_POOL
        cst[:, at:at + PAD_POOL] = 1.0 / np.minimum(np.arange(PAD_POOL) + 1, w)
    cst[:, CST["eps"][0]] = EPS
    query = np.arange(T).reshape(TOK_TILES, P)
    ahead = np.where(np.arange(T)[None, None, :] > query[:, :, None], MASKED, 0.0)
    ahead = np.ascontiguousarray(ahead.transpose(1, 0, 2)).astype(np.float32)
    dist = np.maximum(T - 1 - np.arange(REV), 0)
    far = MAX_EXACT + (np.log(np.maximum(dist, 1).astype(np.float32) / np.float32(MAX_EXACT))
                       / np.float32(np.log(MAX_DIST / MAX_EXACT)) * (BUCKETS - MAX_EXACT)).astype(np.int32)
    bucket = np.where(dist < MAX_EXACT, dist, np.minimum(far, BUCKETS - 1))
    onehot = (np.arange(BUCKETS)[:, None] == bucket[None, :]).astype(np.float32)
    return cst, ahead, onehot


class Queue:

    def __init__(self, done):
        self.items = []
        self.done = done
        self.count = 0

    def put(self, make, after=(), signal=True):
        if signal:
            self.count += 1
        self.items.append((make, [t for t in after if t is not None], (self.done, 1) if signal else None))
        return (self.done, self.count) if signal else None

    def put_dma(self, make, sem, after=()):
        sem[1] += 16
        self.items.append((make, [t for t in after if t is not None], (sem[0], 16)))
        return (sem[0], sem[1])

    def play(self, engine):
        seen = {}
        for make, after, inc in self.items:
            for sem, value in after:
                if seen.get(sem.name, 0) < value:
                    engine.wait_ge(sem, value)
                    seen[sem.name] = value
            if make is None:
                continue
            ins = make(engine)
            if inc:
                ins.then_inc(inc[0], inc[1])


class Tile:

    def __init__(self, loads, cols, products, needs):
        self.loads = loads
        self.cols = cols
        self.products = products
        self.needs = needs


def build(nc, x_in, p_in, vec_in, cst_in, ahead_in, onehot_in, table_in, rev_dram,
          ple_proj, ple_gate, a_in, a_r, a_i, a_out, w_in, w_tail, pool_w, w_branch, w_gate, w_out, w_up, w_down,
          out):
    with ExitStack() as ctx:
        def sem(name):
            return ctx.enter_context(nc.semaphore(name))

        cursor = [(nc.sbuf_base + 63) // 64 * 64]

        def at(name, shape, dt, offset):
            return nc.alloc_sbuf_tensor_at(name, shape, dt, offset=offset)

        def fixed(name, shape, dt=F32):
            size = int(np.prod(shape[1:])) * (2 if dt == BF16 else 4)
            t = at(name, shape, dt, cursor[0])
            cursor[0] += (size + 63) // 64 * 64
            return t

        x = fixed("x", [P, KT, T])
        y_base = cursor[0]
        y = fixed("y", [P, KT, T])
        u_hi = fixed("u_hi", [P, KT, T], F32R)
        u_lo = fixed("u_lo", [P, KT, T], F32R)
        stage = fixed("stage", [P, N_STAGE, WCOLS])
        w_hi = fixed("w_hi", [P, N_SPLIT, WCOLS], F32R)
        w_lo = fixed("w_lo", [P, N_SPLIT, WCOLS], F32R)
        vec = fixed("vec", [P, VEC_COLS])
        cst = fixed("cst", [P, CST_COLS])
        ones = fixed("ones", [P, P])
        ident_b = fixed("ident_b", [P, P], BF16)
        tmp = [fixed(f"tmp{i}", [P, 2 * T]) for i in range(4)]
        rstd = fixed("rstd", [P, T])
        squares = fixed("squares", [P, 2 * T])
        gates = fixed("gates", [P, 4, T])
        sp = fixed("sp", [P, 4, KT])
        wi = fixed("wi", [P, TOK_TILES, IDX_HEADS])
        top8 = fixed("top8", [P, 8])
        row_max = fixed("row_max", [P, 2, GROUP])
        row_sum = fixed("row_sum", [P, 2, GROUP])
        arena = cursor[0]

        hs = at("hs", [P, KT, T], F32, arena)
        g_hi = at("g_hi", [P, KT, T], F32R, arena + 16384)
        g_lo = at("g_lo", [P, KT, T], F32R, arena + 32768)
        o = arena + 49152
        xb = at("xb", [P, 4, T + CONV_W - 1], F32, o)
        o += 4160
        xc = at("xc", [P, 4, T], F32, o)
        xc_hi = at("xc_hi", [P, 4, T], F32R, o + 4096)
        xc_lo = at("xc_lo", [P, 4, T], F32R, o + 8192)
        r_buf = at("r_buf", [P, 4, T], F32, o + 12288)
        i_buf = at("i_buf", [P, 4, T], F32, o + 16384)
        a_buf = at("a_buf", [P, 4, T], F32, o + 20480)
        t_buf = at("t_buf", [P, 4, T], F32, o + 24576)
        p_hi = at("p_hi", [P, 2, T], F32R, o + 28672)
        p_lo = at("p_lo", [P, 2, T], F32R, o + 30720)
        pp = at("pp", [P, KT, T], F32, arena)

        b_hi = at("b_hi", [P, 2 * HALF // P, T], F32R, arena)
        b_lo = at("b_lo", [P, 2 * HALF // P, T], F32R, arena + 16384)
        o_hi = at("o_hi", [P, HEADS, T], F32R, arena + 32768)
        o_lo = at("o_lo", [P, HEADS, T], F32R, arena + 40960)
        bias = at("bias", [P, HEADS, T], F32, arena + 32768)
        qi = at("qi", [P, IDX_HEADS // 2, T], F32, arena + 40960)
        q = at("q", [P, HEADS, T], F32, arena + 49152)
        o = arena + 57344
        k = at("k", [P, KV_HEADS, T], F32, o)
        v = at("v", [P, TOK_TILES, KV_HEADS * HD], F32, o + 2048)
        ki = at("ki", [P, T], F32, o + 4096)
        o += 5120
        score = at("score", [P, TOK_TILES, T], F32, o)
        left = at("left", [P, T], F32, o + 2048)
        mask = at("mask", [P, TOK_TILES, T], BF16, o + 3072)
        prob = [at(f"prob{i}", [P, 2 * T], F32, o + 4096 + 2048 * i) for i in range(2)]
        prob_t = [at(f"prob_t{i}", [P, 4, P], F32, o + 8192 + 2048 * i) for i in range(2)]
        ahead = at("ahead", [P, TOK_TILES, T], F32, o + 12288)
        relu = [at(f"relu{i}", [P, 2 * T], F32, o + 14336 + 2048 * i) for i in range(2)]
        onehot = at("onehot", [BUCKETS, REV], F32, o + 18432)
        rev = at("rev", [HEADS, REV], F32, o + 19968)
        table = at("table", [BUCKETS, HEADS], F32, o + 21504)
        mix_hi = at("mix_hi", [P, KT, T], F32R, arena)
        mix_lo = at("mix_lo", [P, KT, T], F32R, arena + 16384)
        pool_u = at("pool_u", [P, 4, T], F32, y_base)
        conv_z = at("conv_z", [P, 4, T], F32, y_base)
        d_lo = at("d_lo", [P, 4, T], F32R, y_base + 4096)
        conv_y = at("conv_y", [P, 4, T], F32, y_base + 4096)
        conv_u = at("conv_u", [P, 4, T], F32, y_base + 8192)
        d_hi = at("d_hi", [P, 4, T], F32R, y_base + 12288)
        hid_hi = at("hid_hi", [P, MLP // 2 // P, T], F32R, arena)
        hid_lo = at("hid_lo", [P, MLP // 2 // P, T], F32R, arena + 32768)

        acc = [[ctx.enter_context(nc.psum_tensor(f"acc{s}{b}", [P, 2, T], F32)) for b in range(2)] for s in range(2)]
        misc = [ctx.enter_context(nc.psum_tensor(f"misc{i}", [P, 2 * T], F32)) for i in range(4)]

        sp_q = Queue(None)
        scalar = Queue(sem("scalar_done"))
        vector = Queue(sem("vector_done"))
        tensor = Queue(sem("tensor_done"))
        stage_in = [[sem(f"stage_in{i}"), 0] for i in range(N_STAGE)]
        const_in = [sem("const_in"), 0]
        x_in_sem = [[sem(f"x_in{i}"), 0] for i in range(4)]
        late_in = [sem("late_in"), 0]
        rev_out = [sem("rev_out"), 0]
        bias_in = [sem("bias_in"), 0]
        out_done = [sem("out_done"), 0]

        def act(out, in_, func, after=(), bias=None, scale=None, accum=None):
            kw = {}
            if bias is not None:
                kw["bias"] = bias
            if scale is not None:
                kw["scale"] = scale
            if accum is not None:
                kw["accum_out"] = accum
            return scalar.put(lambda e: e.activation(out, in_, func, **kw), after)

        def tt(out, a, b, op, after=()):
            return vector.put(lambda e: e.tensor_tensor(out, a, b, op), after)

        def ts(out, a, s1, s2, op0, op1, after=()):
            if s2 is None:
                return vector.put(lambda e: e.tensor_scalar(out, a, s1, None, op0), after)
            return vector.put(lambda e: e.tensor_scalar(out, a, s1, s2, op0, op1), after)

        def stt(out, a, s, b, op0, op1, after=()):
            return vector.put(lambda e: e.scalar_tensor_tensor(out=out, in0=a, scalar=s, in1=b, op0=op0, op1=op1), after)

        def vec_do(make, after=()):
            return vector.put(make, after)

        def mm(out, lhs, rhs, start, stop, after=(), signal=False):
            return tensor.put(lambda e: e.matmul(out, lhs, rhs, start=start, stop=stop, skip_group_check=True),
                              after, signal)

        def v_of(name, i):
            return vec[:, VEC[name][0] + i:VEC[name][0] + i + 1]

        def c_of(name):
            return cst[:, CST[name][0]:CST[name][0] + CST[name][1]]

        def as32(ap):
            return ap.bitcast(F32)

        def split(hi, lo, src, after=()):
            t_hi = act(hi, src, ACT.Copy, after)
            return tt(lo, src, as32(hi), ALU.subtract, [t_hi])

        tiles = []
        jobs = {}
        tile_done = []
        split_done = {}

        def job(step, fn):
            jobs.setdefault(step, []).append(fn)

        def load_tile(n):
            slot = n % N_STAGE
            before = [split_done[n - N_STAGE]] if n >= N_STAGE else []
            for (a, b), shape_k, src in tiles[n].loads:
                dst = stage[:, slot, a:b].rearrange("p (k n) -> p k n", k=shape_k)
                sp_q.put_dma(lambda e, dst=dst, src=src: e.dma_start(dst, src), stage_in[slot], before)
            tiles[n].landed = (stage_in[slot][0], stage_in[slot][1])

        def split_tile(n):
            slot, buf, cols = n % N_STAGE, n % N_SPLIT, tiles[n].cols
            free = [tile_done[n - N_SPLIT]] if n >= N_SPLIT else []
            src = stage[:, slot, 0:cols]
            hi = w_hi[:, buf, 0:cols]
            t_hi = act(hi, src, ACT.Copy, [tiles[n].landed] + free)
            split_done[n] = tt(w_lo[:, buf, 0:cols], src, as32(hi), ALU.subtract, [t_hi])
            if n + N_STAGE < len(tiles):
                load_tile(n + N_STAGE)

        def multiply_tile(n):
            buf = n % N_SPLIT
            tile = tiles[n]
            after = [split_done[n]] + tile.needs()
            products = tile.products(w_hi[:, buf, :], w_lo[:, buf, :])
            for i, (out_, lhs, rhs, start, stop) in enumerate(products):
                token = mm(out_, lhs, rhs, start, stop, after, signal=i == len(products) - 1)
                after = ()
            tile_done.append(token)

        bank_free = [[], []]
        chunk_no = [0]

        def chunk(w, c0, act_hi, act_lo, ready, epilogue, kts, k0=0, delay=0, cols=CHUNK):
            s = chunk_no[0] % 2
            chunk_no[0] += 1
            per = WCOLS // cols
            first = len(tiles)
            for i in range(0, kts, per):
                src = w[i * P:(i + per) * P, c0:c0 + cols].rearrange("(k p) n -> p k n", p=P)

                def products(hi, lo, i=i):
                    got = []
                    for dk in range(per):
                        kt = i + dk
                        for j in range(cols // P):
                            c = dk * cols + j * P
                            o_ = acc[s][j // 2][:, j % 2, :]
                            wh, wl = hi[:, c:c + P], lo[:, c:c + P]
                            xh, xl = act_hi[:, k0 + kt, :], act_lo[:, k0 + kt, :]
                            got += [(o_, wh, xh, kt == 0 and j % 2 == 0, False), (o_, wh, xl, False, False),
                                    (o_, wl, xh, False, kt == kts - 1)]
                    return got

                def needs(i=i):
                    return (list(bank_free[s]) if i == 0 else []) + \
                        [t for dk in range(per) for t in ready(k0 + i + dk)]

                tiles.append(Tile([((0, WCOLS), per, src)], WCOLS, products, needs))
            job(len(tiles) - 1, lambda: epilogue(s))
            return first

        def block_chunk(w, n0, act_hi, act_lo, ready, epilogue):
            s = chunk_no[0] % 2
            chunk_no[0] += 1
            src = w[n0:n0 + 2].rearrange("b (k p) d -> p (b k) d", p=P)

            def products(hi, lo):
                got = []
                for b in range(2):
                    for e in range(2):
                        for kk in range(2):
                            kt = 2 * b + kk
                            c = kt * 256 + e * P
                            o_ = acc[s][b][:, e, :]
                            wh, wl = hi[:, c:c + P], lo[:, c:c + P]
                            got += [(o_, wh, act_hi[:, kt, :], kk == 0 and e == 0, False),
                                    (o_, wh, act_lo[:, kt, :], False, False),
                                    (o_, wl, act_hi[:, kt, :], False, kk == 1)]
                return got

            tiles.append(Tile([((0, WCOLS), 4, src)], WCOLS, products, lambda: list(bank_free[s]) + ready(0)))
            job(len(tiles) - 1, lambda: epilogue(s))

        def evacuated(s, tokens):
            bank_free[s] = list(tokens)

        norm = {}
        misc_free = [None] * 4
        tmp_free = [[] for _ in range(4)]

        def rms(after):
            std = tmp[3][:, 0:T]
            t = act(std, misc[0][:, 0:T], ACT.Sqrt, after + tmp_free[3], bias=c_of("eps"), scale=1.0 / D)
            misc_free[0] = t
            t = vec_do(lambda e: e.reciprocal(rstd[:, :], std), [t])
            tmp_free[3] = [t]
            return t

        def sum_squares(after):
            mm(misc[0][:, 0:T], ones[:, :], squares[:, 0:T], True, False, after + [misc_free[0]])
            return mm(misc[0][:, 0:T], ones[:, :], squares[:, T:2 * T], False, True, signal=True)

        def norm_pair(j, src, gain, t_rstd, dst_hi, dst_lo, after=()):
            b = tmp[j % 2]
            t = None
            for d in range(2):
                kt = 2 * j + d
                t = stt(b[:, d * T:(d + 1) * T], src[:, kt, :], v_of(gain, kt), rstd[:, :], ALU.mult, ALU.mult,
                        [t_rstd] + list(after) + tmp_free[j % 2])
            tmp_free[j % 2] = [split(dst_hi[:, 2 * j:2 * j + 2, :].rearrange("p k t -> p (k t)"),
                                     dst_lo[:, 2 * j:2 * j + 2, :].rearrange("p k t -> p (k t)"), b[:, :], [t])]
            return tmp_free[j % 2][0]

        def flat(ap):
            return ap.rearrange("p k t -> p (k t)")

        def spread(step, fn, n=KT // 2):
            fn(0)
            fn(1)
            for j in range(2, n):
                job(step + j - 1, lambda j=j: fn(j))

        for qd in range(4):
            sp_q.put_dma(lambda e, qd=qd: e.dma_start(x[:, 4 * qd:4 * qd + 4, :], x_in[:, 4 * qd:4 * qd + 4, :]),
                         x_in_sem[qd])
        pool_q = Queue(sem("gpsimd_done"))
        act_dma = [(vec[:, :], vec_in), (cst[:, :], cst_in)]
        for d_, s_ in act_dma:
            t_const = scalar.put_dma(lambda e, d_=d_, s_=s_: e.dma_start(d_, s_), const_in)
        t_ones = vec_do(lambda e: e.memset(ones[:, :], 1.0))
        t_xb_pad = vec_do(lambda e: e.memset(xb[:, :, 0:CONV_W - 1], 0.0))
        p_in_sem = [sem("p_in"), 0]
        t_p_in = scalar.put_dma(lambda e: e.dma_start(tmp[2][:, :], p_in), p_in_sem)

        lam = vec[:, VEC["lam"][0]:VEC["lam"][0] + KT]
        e_, z_, z2_, s_ = (sp[:, i, :] for i in range(4))
        t = act(e_, lam, ACT.Abs, [t_const])
        t = act(e_, e_, ACT.Exp, [t], scale=-1.0)
        t = ts(z_, e_, 2.0, None, ALU.add, None, [t])
        t = vec_do(lambda e: e.reciprocal(z2_, z_), [t])
        t = tt(z_, z2_, e_, ALU.mult, [t])
        t = tt(z2_, z_, z_, ALU.mult, [t])
        t = vec_do(lambda e: e.memset(s_, 1.0 / 17), [])
        for odd in (15, 13, 11, 9, 7, 5, 3, 1):
            t = tt(s_, s_, z2_, ALU.mult, [t])
            t = ts(s_, s_, 1.0 / odd, None, ALU.add, None, [t])
        t = tt(s_, s_, z_, ALU.mult, [t])
        t = ts(e_, lam, -1.0, 0.0, ALU.mult, ALU.max, [t])
        t = stt(z_, s_, 2.0, e_, ALU.mult, ALU.add, [t])
        decay, neg_decay = sp[:, 2, :], sp[:, 3, :]
        t = ts(decay, z_, LRU_C, None, ALU.mult, None, [t])
        t_decay = ts(neg_decay, z_, -LRU_C, None, ALU.mult, None, [t])

        for qd in range(4):
            t = act(y[:, 4 * qd:4 * qd + 4, :], x[:, 4 * qd:4 * qd + 4, :], ACT.Square,
                    [(x_in_sem[qd][0], 16)])
            for d in range(4):
                kt = 4 * qd + d
                t_sum = mm(misc[0][:, 0:T], ones[:, :], y[:, kt, :], kt == 0, kt == KT - 1, [t, t_ones],
                           signal=kt == KT - 1)
        t_rstd0 = rms([t_sum])
        u_ready = {}

        def ready_u(kt):
            return [u_ready[kt // 2]]

        def first_norm(j):
            u_ready[j] = norm_pair(j, x, "norm_pre", t_rstd0, u_hi, u_lo)

        xc_ready, r_ready, i_ready, h_ready, xb_free = {}, {}, {}, {}, {}
        state = {"xc_free": None, "i_free": None, "a_free": None}

        def xb_epilogue(c):
            def go(s):
                got = []
                for b in range(2):
                    got.append(act(xb[:, 2 * b:2 * b + 2, CONV_W - 1:], acc[s][b][:, :, :], ACT.Copy,
                                   [tile_done[-1], t_xb_pad] + xb_free.get(c - 1, [])))
                evacuated(s, got)
                state["xb", c] = got
                if c == 0:
                    conv(0)
            return go

        def conv(c):
                got = state["xb", c]
                toks = [None] * 4
                for i in range(CONV_W):
                    for j in range(4):
                        kt = 4 * c + j
                        w_ = v_of("a_conv_w", kt * CONV_W + i)
                        if i == 0:
                            toks[j] = ts(xc[:, j, :], xb[:, j, 0:T], w_, v_of("a_conv_b", kt), ALU.mult, ALU.add,
                                         [got[j // 2], state["xc_free"]])
                        else:
                            toks[j] = stt(xc[:, j, :], xb[:, j, i:i + T], w_, xc[:, j, :], ALU.mult, ALU.add,
                                          [toks[j]])
                xb_free[c] = [toks[3]]
                xc_ready[c] = split(flat(xc_hi[:, :, :]), flat(xc_lo[:, :, :]), flat(xc[:, :, :]),
                                    [toks[3], state.get("xc_read")])

        def r_epilogue(c):
            def go(s):
                got = [act(r_buf[:, j, :], acc[s][j // 2][:, j % 2, :], ACT.Sigmoid,
                           [tile_done[-1]] + h_ready.get(c - 1, []), bias=v_of("b_r", 4 * c + j)) for j in range(4)]
                evacuated(s, [got[3]])
                r_ready[c] = got[3]
            return go

        def i_epilogue(c):
            def go(s):
                got = [act(i_buf[:, j, :], acc[s][j // 2][:, j % 2, :], ACT.Sigmoid,
                           [tile_done[-1]] + h_ready.get(c - 1, []), bias=v_of("b_i", 4 * c + j)) for j in range(4)]
                evacuated(s, [got[3]])
                for j in range(4):
                    t_a = act(a_buf[:, j, :], r_buf[:, j, :], ACT.Exp, [r_ready[c], t_decay],
                              scale=neg_decay[:, 4 * c + j:4 * c + j + 1])
                for j in range(4):
                    t_t = act(t_buf[:, j, :], r_buf[:, j, :], ACT.Tanh, [],
                              scale=decay[:, 4 * c + j:4 * c + j + 1])
                t_m = tt(flat(r_buf[:, :, :]), flat(a_buf[:, :, :]), flat(a_buf[:, :, :]), ALU.mult, [t_a, t_t])
                t_m = stt(flat(r_buf[:, :, :]), flat(r_buf[:, :, :]), 1.0, flat(t_buf[:, :, :]), ALU.add, ALU.mult,
                          [t_m])
                t_i = tt(flat(i_buf[:, :, :]), flat(i_buf[:, :, :]), flat(xc[:, :, :]), ALU.mult, [got[3]])
                state["xc_free"] = t_i
                state["xc_read"] = tile_done[-1]
                t_s = act(flat(t_buf[:, :, :]), flat(r_buf[:, :, :]), ACT.Sqrt, [t_m])
                t_b = tt(flat(i_buf[:, :, :]), flat(i_buf[:, :, :]), flat(t_buf[:, :, :]), ALU.mult, [t_s, t_i])
                for j in range(4):
                    t_h = vec_do(lambda e, j=j: e.tensor_tensor_scan(hs[:, 4 * c + j, :], a_buf[:, j, :],
                                                                     i_buf[:, j, :], 0.0, ALU.mult, ALU.add), [t_b])
                h_ready[c] = [t_h]
                if c < 3:
                    conv(c + 1)
            return go

        y_ready = {}

        def gate_epilogue(c):
            def go(s):
                got = []
                for b in range(2):
                    sg, yy = tmp[2 * b], tmp[2 * b + 1]
                    got.append(act(sg[:, :], flat(acc[s][b][:, :, :]), ACT.Silu, [tile_done[-1]] + tmp_free[2 * b]))
                    j = 4 * c + 2 * b
                    t = tt(yy[:, :], flat(hs[:, j:j + 2, :]), sg[:, :], ALU.mult, [got[b]] + h_ready[c]
                           + tmp_free[2 * b + 1])
                    tmp_free[2 * b] = [t]
                    t = split(flat(g_hi[:, j:j + 2, :]), flat(g_lo[:, j:j + 2, :]), yy[:, :], [t])
                    tmp_free[2 * b + 1] = [t]
                    y_ready[2 * c + b] = t
                evacuated(s, got)
            return go

        first_norm(0)
        first_norm(1)
        for j in range(2, KT // 2):
            job(j - 2, lambda j=j: first_norm(j))

        def xb_chunk(c):
            chunk(a_in, c * CHUNK, u_hi, u_lo, ready_u, xb_epilogue(c), KT)

        def ri_chunk(c):
            block_chunk(a_r, 2 * c, xc_hi, xc_lo, lambda kt: [xc_ready[c]], r_epilogue(c))
            block_chunk(a_i, 2 * c, xc_hi, xc_lo, lambda kt: [xc_ready[c]], i_epilogue(c))

        def g_chunk(c):
            chunk(a_in, D + c * CHUNK, u_hi, u_lo, ready_u, gate_epilogue(c), KT)

        def split_p():
            state["p"] = split(flat(p_hi[:, :, :]), flat(p_lo[:, :, :]), tmp[2][:, :], [t_p_in])
            tmp_free[2] = [state["p"]]
        job(1, split_p)

        xb_chunk(0)
        xb_chunk(1)
        ri_chunk(0)
        xb_chunk(2)
        ri_chunk(1)
        xb_chunk(3)
        ri_chunk(2)
        g_chunk(0)
        ri_chunk(3)
        g_chunk(1)
        g_chunk(2)
        g_chunk(3)

        sq = {"t": None}

        def add_squares(src, after, first):
            t = act(tmp[2][:, :], src, ACT.Square, list(after) + tmp_free[2])
            if first:
                sq["t"] = vec_do(lambda e: e.tensor_copy(squares[:, :], tmp[2][:, :]), [t, sq["t"]])
            else:
                sq["t"] = tt(squares[:, :], squares[:, :], tmp[2][:, :], ALU.add, [t, sq["t"]])
            tmp_free[2] = [sq["t"]]
            return t

        def y_epilogue(c, then=None):
            def go(s):
                got = []
                for b in range(2):
                    j = 4 * c + 2 * b
                    act(flat(y[:, j:j + 2, :]), flat(acc[s][b][:, :, :]), ACT.Copy, [tile_done[-1]])
                    got.append(add_squares(flat(acc[s][b][:, :, :]), [], c == 0 and b == 0))
                evacuated(s, got)
                if then:
                    then()
            return go

        def residual_pair(j, gain, t_rstd, after=()):
            b = tmp[j % 2]
            for d in range(2):
                kt = 2 * j + d
                t = stt(b[:, d * T:(d + 1) * T], y[:, kt, :], v_of(gain, kt), rstd[:, :], ALU.mult, ALU.mult,
                        [t_rstd] + list(after) + tmp_free[j % 2])
            t = tt(flat(x[:, 2 * j:2 * j + 2, :]), flat(x[:, 2 * j:2 * j + 2, :]), b[:, :], ALU.add, [t])
            tmp_free[j % 2] = [t]
            return t

        def ready_g(kt):
            return [y_ready[kt // 2]]

        for c in range(3):
            chunk(a_out, c * CHUNK, g_hi, g_lo, ready_g, y_epilogue(c), KT)

        def after_a_out():
            t = sum_squares([sq["t"]])
            state["rstd1"] = rms([t])
        chunk(a_out, 3 * CHUNK, g_hi, g_lo, ready_g, y_epilogue(3, after_a_out), KT)

        pp_ready = {}

        def pp_epilogue(c):
            def go(s):
                got = [act(flat(pp[:, 4 * c + 2 * b:4 * c + 2 * b + 2, :]), flat(acc[s][b][:, :, :]), ACT.Copy,
                           [tile_done[-1]]) for b in range(2)]
                evacuated(s, got)
                pp_ready[c] = got[1]
            return go

        h_split = {}

        def residual1(j):
            t = residual_pair(j, "norm_post", state["rstd1"])
            h_split[j] = split(flat(u_hi[:, 2 * j:2 * j + 2, :]), flat(u_lo[:, 2 * j:2 * j + 2, :]),
                               flat(x[:, 2 * j:2 * j + 2, :]), [t])
        for c in range(4):
            chunk(ple_proj, c * CHUNK, p_hi, p_lo, lambda kt: [state["p"]], pp_epilogue(c), PLE // P)
            job(len(tiles) - 1, lambda c=c: (residual1(2 * c), residual1(2 * c + 1)))

        def ready_h(kt):
            return [h_split[kt // 2]]

        def ple_epilogue(c, then=None):
            def go(s):
                got = []
                for b in range(2):
                    j = 4 * c + 2 * b
                    g = tmp[b]
                    xs = flat(x[:, j:j + 2, :])
                    got.append(act(g[:, :], flat(acc[s][b][:, :, :]), ACT.Sigmoid, [tile_done[-1]] + tmp_free[b]))
                    t = tt(g[:, :], g[:, :], flat(pp[:, j:j + 2, :]), ALU.mult, [got[b], pp_ready[c]])
                    t = tt(xs, xs, g[:, :], ALU.add, [t])
                    tmp_free[b] = [t]
                    add_squares(xs, [t], c == 0 and b == 0)
                evacuated(s, got)
                if then:
                    then()
            return go

        for c in range(3):
            chunk(ple_gate, c * CHUNK, u_hi, u_lo, ready_h, ple_epilogue(c), KT)

        u2_ready = {}

        def norm2(j):
            u2_ready[j] = norm_pair(j, x, "gain0", state["rstd2"], u_hi, u_lo)

        def after_ple():
            state["rstd2"] = rms([sum_squares([sq["t"]])])
            spread(state["ple_end"], norm2)
        chunk(ple_gate, 3 * CHUNK, u_hi, u_lo, ready_h, ple_epilogue(3, after_ple), KT)
        state["ple_end"] = len(tiles) - 1

        def ready_u2(kt):
            return [u2_ready[kt // 2]]

        def bias_table():
            t1 = scalar.put_dma(lambda e: e.dma_start(onehot[:, :], onehot_in), late_in, [tile_done[-1]])
            t1 = scalar.put_dma(lambda e: e.dma_start(table[:, :], table_in), late_in)
            state["late"] = scalar.put_dma(lambda e: e.dma_start(ahead[:, :, :], ahead_in), late_in)

        def bias_rev():
            t = mm(misc[1][0:HEADS, 0:REV], table[:, :], onehot[:, :], True, True, [state["late"], misc_free[1]],
                   signal=True)
            t = act(rev[:, :], misc[1][0:HEADS, 0:REV], ACT.Copy, [t])
            misc_free[1] = t
            t = scalar.put_dma(lambda e: e.dma_start(rev_dram, rev[:, :]), rev_out, [t])
            src = rev_dram[:, 0:T].unsqueeze(0).broadcast_to([P, HEADS, T]) if False else None
            state["bias"] = scalar.put_dma(lambda e: e.dma_start(bias[:, :, :], hankel), bias_in, [t])
        hankel = bass.AP(rev_dram.tensor, 0, [[1, P], [REV, HEADS], [1, T]])

        t_identb = {}

        def tail_chunk(epilogue):
            s = chunk_no[0] % 2
            chunk_no[0] += 1
            per = 6
            for k0 in range(0, KT, per):
                n = min(per, KT - k0)
                src = w_tail[:, k0:k0 + n, :]

                def products(hi, lo, k0=k0, n=n):
                    got = []
                    for dk in range(n):
                        kt = k0 + dk
                        c = dk * TAIL
                        kw = slice(c, c + 2 * IDX_DIM)
                        ww = slice(c + 2 * IDX_DIM, c + TAIL)
                        o_ = acc[s][0][:, 0, :]
                        xh, xl = u_hi[:, kt, :], u_lo[:, kt, :]
                        got += [(o_, hi[:, kw], xh, kt == 0, False), (o_, hi[:, kw], xl, False, False),
                                (o_, lo[:, kw], xh, False, kt == KT - 1)]
                        for t_ in range(TOK_TILES):
                            o_ = acc[s][1][:, t_, 0:IDX_HEADS]
                            tok = slice(t_ * P, (t_ + 1) * P)
                            got += [(o_, u_hi[:, kt, tok], hi[:, ww], kt == 0 and t_ == 0, False),
                                    (o_, u_lo[:, kt, tok], hi[:, ww], False, False),
                                    (o_, u_hi[:, kt, tok], lo[:, ww], False, kt == KT - 1)]
                    return got

                def needs(k0=k0, n=n):
                    return (list(bank_free[s]) if k0 == 0 else []) + [t for d in range(n) for t in ready_u2(k0 + d)]
                tiles.append(Tile([((0, n * TAIL), n, src)], n * TAIL, products, needs))
            job(len(tiles) - 1, lambda: epilogue(s))

        def tail_epilogue(s):
            t1 = act(ki[:, :], acc[s][0][:, 0, :], ACT.Copy, [tile_done[-1]])
            t2 = act(wi[:, :, :], acc[s][1][:, :, 0:IDX_HEADS], ACT.Copy, [], scale=IDX_HEADS ** -0.5)
            evacuated(s, [t2])
            state["ki"] = t2

        def copy_epilogue(dst, j0, key, scale=1.0):
            def go(s):
                got = [act(flat(dst[:, j0 + 2 * b:j0 + 2 * b + 2, :]), flat(acc[s][b][:, :, :]), ACT.Copy,
                           [tile_done[-1]], scale=scale) for b in range(2)]
                evacuated(s, got)
                state[key] = got[1]
            return go

        def kv_chunk():
            s = chunk_no[0] % 2
            chunk_no[0] += 1
            for i in range(0, KT, 2):
                src = w_in[i * P:(i + 2) * P, C_KV:C_KV + CHUNK].rearrange("(k p) n -> p k n", p=P)

                def products(hi, lo, i=i):
                    got = []
                    for dk in range(2):
                        kt = i + dk
                        xh, xl = u_hi[:, kt, :], u_lo[:, kt, :]
                        for j in range(KV_HEADS):
                            c = dk * CHUNK + j * HD
                            o_ = acc[s][0][:, j, :]
                            wh, wl = hi[:, c:c + HD], lo[:, c:c + HD]
                            got += [(o_, wh, xh, kt == 0 and j == 0, False), (o_, wh, xl, False, False),
                                    (o_, wl, xh, False, kt == KT - 1)]
                        for t_ in range(TOK_TILES):
                            c = dk * CHUNK + KV_HEADS * HD
                            o_ = acc[s][1][:, t_, :]
                            tok = slice(t_ * P, (t_ + 1) * P)
                            wh, wl = hi[:, c:c + KV_HEADS * HD], lo[:, c:c + KV_HEADS * HD]
                            got += [(o_, xh[:, tok], wh, kt == 0 and t_ == 0, False), (o_, xl[:, tok], wh, False, False),
                                    (o_, xh[:, tok], wl, False, kt == KT - 1)]
                    return got

                tiles.append(Tile([((0, WCOLS), 2, src)], WCOLS, products,
                                  lambda i=i: (list(bank_free[s]) if i == 0 else []) + ready_u2(i)))

            def epilogue(s=s):
                t1 = act(flat(k[:, :, :]), flat(acc[s][0][:, :, :]), ACT.Copy, [tile_done[-1]])
                t2 = act(flat(v[:, :, :]), flat(acc[s][1][:, :, :]), ACT.Copy)
                evacuated(s, [t2])
                state["kv"] = t2
            job(len(tiles) - 1, epilogue)

        relu_free = [None, None]
        dots = {}

        def score_banks(n):
            return (1, 2) if n % 2 == 0 else (3, 0)

        def score_dots(n, t_, heads, nk):
            for i, h in enumerate(heads):
                bank = score_banks(n)[h % 2]
                lo_p = (h % 2) * IDX_DIM
                tok = mm(misc[bank][:, i // 2 * nk:(i // 2 + 1) * nk],
                         qi[lo_p:lo_p + IDX_DIM, h // 2, t_ * P:(t_ + 1) * P],
                         ki[lo_p:lo_p + IDX_DIM, 0:nk], True, True, [state["qi"], state["ki"], misc_free[bank]],
                         signal=i == len(heads) - 1)
            dots[n] = tok

        def score_relu(n, t_, heads, nk):
            for odd in range(2):
                bank = score_banks(n)[odd]
                misc_free[bank] = act(relu[n % 2][:, odd * T:(odd + 1) * T], misc[bank][:, 0:T], ACT.Relu,
                                      [dots[n], relu_free[n % 2]])
            dots[n] = misc_free[bank]

        def score_add(n, t_, heads, nk):
            for i, h in enumerate(heads):
                base = ahead if h == 0 else score
                at_ = (h % 2) * T + i // 2 * nk
                tok = stt(score[:, t_, 0:nk], relu[n % 2][:, at_:at_ + nk], wi[:, t_, h:h + 1],
                          base[:, t_, 0:nk], ALU.mult, ALU.add, [dots[n], state["late"], state.get("score")])
                state["score"] = tok
            relu_free[n % 2] = tok

        def topk_round(t_, r, nk):
            src = score[:, t_, 0:nk] if r == 0 else left[:, 0:nk]
            tok = vec_do(lambda e: e.max(top8[:, :], src), [state["score"], state.get("mask")])
            state["score"] = vec_do(lambda e: e.match_replace(left[:, 0:nk], top8[:, :], src, TAKEN), [tok])

        def topk_mask(t_, nk):
            tok = ts(left[:, 0:nk], left[:, 0:nk], 2 * MASKED, UNSELECTED, ALU.is_ge, ALU.mult, [state["score"]])
            state["mask"] = tt(mask[:, t_, 0:nk], left[:, 0:nk], ahead[:, t_, 0:nk], ALU.add, [tok])

        unit = {}

        def a_logits(n, t_, heads, nk):
            for i, h in enumerate(heads):
                o_ = misc[1][:, i * nk:(i + 1) * nk]
                off = (TOK_TILES - 1 - t_) * P
                mm(o_, q[:, h, t_ * P:(t_ + 1) * P], k[:, h // GROUP, 0:nk], True, False,
                   [state["q"], state["kv"], misc_free[1]])
                mm(o_, c_of("flip"), bias[:, h, off:off + nk], False, False, [state["bias"]])
                tok = mm(o_, ident_b[:, :], mask[:, t_, 0:nk], False, True, [state["mask"], state["identb"]],
                         signal=i == len(heads) - 1)
            unit[n] = tok

        def a_max(n, t_, heads, nk):
            g = len(heads)
            src = misc[1][:, 0:g * nk].rearrange("p (g k) -> p g k", g=g)
            m_ = row_max[:, n % 2, 0:g]
            tok = vec_do(lambda e: e.reduce_max(m_, src, AX_X), [unit[n]])
            unit[n] = ts(m_, m_, -1.0, None, ALU.mult, None, [tok])

        def a_exp(n, t_, heads, nk):
            for i, h in enumerate(heads):
                tok = act(prob[n % 2][:, i * nk:(i + 1) * nk], misc[1][:, i * nk:(i + 1) * nk], ACT.Exp,
                          [unit[n], unit.get(("prob_free", n % 2))], bias=row_max[:, n % 2, i:i + 1],
                          accum=row_sum[:, n % 2, i:i + 1])
            misc_free[1] = tok
            unit[n] = tok

        def a_norm(n, t_, heads, nk):
            g = len(heads)
            rs = row_sum[:, n % 2, 0:g]
            tok = vec_do(lambda e: e.reciprocal(rs, rs), [unit[n]])
            for i in range(g):
                pr = prob[n % 2][:, i * nk:(i + 1) * nk]
                last = ts(pr, pr, row_sum[:, n % 2, i:i + 1], None, ALU.mult, None, [tok])
            unit[n] = last

        def a_turn(n, t_, heads, nk):
            for b in range(4):
                dst, src = misc[2][:, b * P:(b + 1) * P], prob[n % 2][:, b * P:(b + 1) * P]
                tok = tensor.put(lambda e, dst=dst, src=src: e.transpose(dst, src, c_of("ident")),
                                 [unit[n], misc_free[2]], b == 3)
            unit["prob_free", n % 2] = tok
            unit[n] = tok

        def a_turned(n, t_, heads, nk):
            tok = act(flat(prob_t[n % 2][:, :, :]), misc[2][:, :], ACT.Copy,
                      [unit[n], unit.get(("prob_t_free", n % 2))])
            misc_free[2] = tok
            unit[n] = tok

        def a_values(n, t_, heads, nk):
            kb = nk // P
            for i, h in enumerate(heads):
                g = h // GROUP
                for b in range(kb):
                    tok = mm(misc[3][:, i * P:(i + 1) * P], v[:, b, g * HD:(g + 1) * HD],
                             prob_t[n % 2][:, i * kb + b, :], b == 0, b == kb - 1, [unit[n], misc_free[3]],
                             signal=i == len(heads) - 1 and b == kb - 1)
            unit["prob_t_free", n % 2] = tok
            unit[n] = tok

        def a_out_split(n, t_, heads, nk):
            g, h0 = len(heads), heads[0]
            src = misc[3][:, 0:g * P].rearrange("p (g q) -> p g q", g=g)
            hi, lo = (b_[:, h0:h0 + g, t_ * P:(t_ + 1) * P] for b_ in (o_hi, o_lo))
            t1 = act(hi, src, ACT.Copy, [unit[n], state["scores_done"], state["logits_done"]])
            misc_free[3] = tt(lo, src, as32(hi), ALU.subtract, [t1])
            state["attn"] = misc_free[3]

        def plan_attention(step):
            n = 0
            for t_, per, nk in ((0, 4, P), (1, 2, T)):
                for h in range(0, IDX_HEADS, per):
                    hh = list(range(h, h + per))
                    for d, fn in enumerate((score_dots, score_relu, score_add)):
                        job(step + n + d, lambda fn=fn, n=n, t_=t_, hh=hh, nk=nk: fn(n, t_, hh, nk))
                    n += 1
            step += n + 2

            def scored():
                state["scores_done"] = state["score"]
            job(step, scored)
            for t_, nk in ((0, P), (1, T)):
                for r in range(0, TOPK // 8, 2):
                    job(step, lambda t_=t_, r=r, nk=nk: (topk_round(t_, r, nk), topk_round(t_, r + 1, nk)))
                    step += 1
                job(step - 1, lambda t_=t_, nk=nk: topk_mask(t_, nk))
            units = [(0, list(range(h, h + 4)), P) for h in range(0, HEADS, 4)] + \
                    [(1, list(range(h, h + 2)), T) for h in range(0, HEADS, 2)]
            stages = (a_logits, a_max, a_exp, a_norm, a_turn, a_turned, a_values, a_out_split)
            return units, stages, step

        for c in range(2):
            chunk(w_in, C_QI + c * CHUNK, u_hi, u_lo, ready_u2, copy_epilogue(qi, 4 * c, "qi"), KT)
            if c == 0:
                job(len(tiles) - 7, bias_table)
                job(len(tiles) - 3, bias_rev)

                def make_identb():
                    state["identb"] = vec_do(lambda e: e.tensor_copy(ident_b[:, :], c_of("ident")), [t_const])
                job(len(tiles) - 5, make_identb)
        tail_chunk(tail_epilogue)
        score_step = len(tiles)
        for c in range(2):
            chunk(w_in, C_Q + c * CHUNK, u_hi, u_lo, ready_u2, copy_epilogue(q, 4 * c, "q", HD ** -0.5), KT)
        kv_chunk()
        kv_end = len(tiles) - 1
        units, stages, attn_step = plan_attention(score_step)
        attn_step = max(attn_step, kv_end) + 1

        def plan_units():
            pass

        order = [units[2], units[3], units[0], units[4], units[5], units[1]]

        def mark_logits():
            state["logits_done"] = unit["last_logits"]

        n_units = len(order)
        GAP = 3
        for n, (t_, hh, nk) in enumerate(order):
            for d, fn in enumerate(stages):
                def run(fn=fn, n=n, t_=t_, hh=hh, nk=nk):
                    fn(n, t_, hh, nk)
                if fn is not a_out_split:
                    job(attn_step + GAP * n + d, run)
        for n, (t_, hh, nk) in enumerate(order):
            def run_out(n=n, t_=t_, hh=hh, nk=nk):
                state["logits_done"] = unit["logits", n // 3 * 3 + 2]
                a_out_split(n, t_, hh, nk)
            job(attn_step + GAP * n + 7, run_out)
        for n in (2, 5):
            def keep(n=n):
                unit["logits", n] = unit[n]
            jobs[attn_step + GAP * n].append(keep)

        b_ready = {}

        def pool_epilogue(c):
            def go(s):
                got = [act(pool_u[:, 2 * b:2 * b + 2, :], acc[s][b][:, :, :], ACT.Copy,
                           [tile_done[-1], state.get("pool_u_free")]) for b in range(2)]
                evacuated(s, got)
                job(state["pool_end"][c] + 1, lambda: pool_group(c, 0, got[0]))
                job(state["pool_end"][c] + 2, lambda: pool_group(c, 1, got[1]))
            return go

        def pool_group(c, g, after):
            gg = 2 * c + g
            w_ = POOL_WINDOWS[gg]
            uu = pool_u[:, 2 * g:2 * g + 2, :]
            t = after
            have = 1
            n = 0
            src = uu
            while have < w_:
                dst = tmp[n % 2][:, :].rearrange("p (k t) -> p k t", k=2)
                vec_do(lambda e, dst=dst, src=src, have=have:
                       e.tensor_copy(dst[:, :, 0:have], src[:, :, 0:have]), [t] + tmp_free[n % 2])
                t = tt(dst[:, :, have:], src[:, :, have:], src[:, :, 0:T - have], ALU.add, [t])
                src = dst
                have *= 2
                n += 1
            ic = cst[:, CST["inv_count"][0] + gg * PAD_POOL:CST["inv_count"][0] + (gg + 1) * PAD_POOL]
            mean = tmp[n % 2][:, :].rearrange("p (k t) -> p k t", k=2)
            for d in range(2):
                t1 = tt(mean[:, d, 0:PAD_POOL], src[:, d, 0:PAD_POOL], ic, ALU.mult, [t] + tmp_free[n % 2])
            t2 = ts(mean[:, :, PAD_POOL:], src[:, :, PAD_POOL:], 1.0 / w_, None, ALU.mult, None, [])
            t3 = tt(mean, mean, uu, ALU.subtract, [t2])
            state["pool_u_free"] = t3
            tmp_free[(n + 1) % 2] = [t3]
            hi, lo = flat(d_hi[:, 2 * g:2 * g + 2, :]), flat(d_lo[:, 2 * g:2 * g + 2, :])
            t4 = split(hi, lo, tmp[n % 2][:, :], [t3, state.get("d_free")])
            tmp_free[n % 2] = [t4]
            state["d", c, g] = t4

        def pool_out_epilogue(c):
            def go(s):
                state["d_free"] = tile_done[-1]
                got = []
                for b in range(2):
                    bb = tmp[b]
                    for d in range(2):
                        kt = 4 * c + 2 * b + d
                        t = act(bb[:, d * T:(d + 1) * T], acc[s][b][:, d, :], ACT.Copy, [tile_done[-1]] + tmp_free[b],
                                scale=v_of("pool_scale", kt))
                    got.append(t)
                    kt = 4 * c + 2 * b
                    t = split(flat(b_hi[:, kt:kt + 2, :]), flat(b_lo[:, kt:kt + 2, :]), bb[:, :], [t])
                    tmp_free[b] = [t]
                    b_ready[kt // 2] = t
                evacuated(s, got)
            return go

        state["pool_end"] = {}
        for c in range(2):
            chunk(w_in, C_POOL + c * CHUNK, u_hi, u_lo, ready_u2, pool_epilogue(c), KT)
            state["pool_end"][c] = len(tiles) - 1
            if c == 0:
                uconv_first = True

            def uconv_epilogue(s, c=c):
                got = [act(flat(conv_u[:, 2 * b:2 * b + 2, :]), flat(acc[s][b][:, :, :]), ACT.Copy,
                           [tile_done[-1], state.get("conv_u_free")]) for b in range(2)]
                evacuated(s, got)
                state["conv_u"] = got[1]
            if c == 0:
                chunk(w_in, C_UCONV, u_hi, u_lo, ready_u2, uconv_epilogue, KT)
                block_chunk(pool_w, 0, d_hi, d_lo, lambda kt: [state["d", 0, 0], state["d", 0, 1]],
                            pool_out_epilogue(0))

        def cgate_epilogue(c):
            def go(s):
                got = [tt(conv_z[:, 2 * b:2 * b + 2, :], acc[s][b][:, :, :], conv_u[:, 2 * b:2 * b + 2, :],
                          ALU.mult, [tile_done[-1], state["conv_u"], state["pool_u_free"]]) for b in range(2)]
                evacuated(s, got)
                state["conv_u_free"] = got[1]
                toks = [None] * 4
                for back in range(CONV2_W):
                    for j in range(4):
                        w_ = v_of("conv_w", (4 * c + j) * CONV2_W + CONV2_W - 1 - back)
                        if back == 0:
                            toks[j] = ts(conv_y[:, j, :], conv_z[:, j, :], w_, None, ALU.mult, None,
                                         [got[1], state["d_free"]])
                        else:
                            toks[j] = stt(conv_y[:, j, back:], conv_z[:, j, 0:T - back], w_, conv_y[:, j, back:],
                                          ALU.mult, ALU.add, [toks[j]])
                state["conv_y"] = toks[3]
            return go

        def bgate_epilogue(c):
            def go(s):
                got = []
                for b in range(2):
                    bb = tmp[b]
                    got.append(tt(bb[:, :], flat(acc[s][b][:, :, :]), flat(conv_y[:, 2 * b:2 * b + 2, :]), ALU.mult,
                                  [tile_done[-1], state["conv_y"]] + tmp_free[b]))
                    kt = HALF // P + 4 * c + 2 * b
                    t = split(flat(b_hi[:, kt:kt + 2, :]), flat(b_lo[:, kt:kt + 2, :]), bb[:, :], [got[b]])
                    tmp_free[b] = [t]
                    b_ready[kt // 2] = t
                evacuated(s, got)
            return go

        def uconv1(s):
            got = [act(flat(conv_u[:, 2 * b:2 * b + 2, :]), flat(acc[s][b][:, :, :]), ACT.Copy,
                       [tile_done[-1], state["conv_u_free"]]) for b in range(2)]
            evacuated(s, got)
            state["conv_u"] = got[1]

        mix = {}

        def gate_chunk(n, c):
            def go(s):
                for j in range(4):
                    t = act(gates[:, j, :], acc[s][j // 2][:, j % 2, :], ACT.Sigmoid,
                            [tile_done[-1], mix.get("gates_free")], bias=v_of("b_gate", n * KT + 4 * c + j))
                evacuated(s, [t])
                mix["gates"] = t
            chunk(w_gate, n * D + c * CHUNK, u_hi, u_lo, ready_u2, go, KT)

        def up_chunk(n, c, hi, lo, k0, ready):
            def go(s):
                got = []
                for b in range(2):
                    j = 4 * c + 2 * b
                    g = flat(gates[:, 2 * b:2 * b + 2, :])
                    ys = flat(y[:, j:j + 2, :])
                    if n == 0:
                        got.append(tt(ys, flat(acc[s][b][:, :, :]), g, ALU.mult,
                                      [tile_done[-1], mix["gates"], mix["y_free"]]))
                        continue
                    bb = tmp[b]
                    got.append(tt(bb[:, :], flat(acc[s][b][:, :, :]), g, ALU.mult,
                                  [tile_done[-1], mix["gates"]] + tmp_free[b]))
                    t = tt(ys, ys, bb[:, :], ALU.add, [got[b]])
                    tmp_free[b] = [t]
                    if n == 2:
                        mix["mixed", 2 * c + b] = split(flat(mix_hi[:, j:j + 2, :]), flat(mix_lo[:, j:j + 2, :]),
                                                        ys, [t])
                evacuated(s, got)
                mix["gates_free"] = got[1]
            chunk(w_branch[n], c * CHUNK, hi, lo, ready, go, HALF // P, k0=k0)

        gate_chunk(0, 0)
        block_chunk(pool_w, 2, d_hi, d_lo, lambda kt: [state["d", 1, 0], state["d", 1, 1]], pool_out_epilogue(1))
        for c in range(2):
            if c == 1:
                chunk(w_in, C_UCONV + CHUNK, u_hi, u_lo, ready_u2, uconv1, KT)
            chunk(w_in, C_CGATE + c * CHUNK, u_hi, u_lo, ready_u2, cgate_epilogue(c), KT)
            chunk(w_in, C_BGATE + c * CHUNK, u_hi, u_lo, ready_u2, bgate_epilogue(c), KT)

        def ready_b(kt):
            return [b_ready[kt // 2]]

        def y_free():
            mix["y_free"] = b_ready[2 * HALF // P // 2 - 1]
        job(len(tiles) - 1, y_free)
        sources = [(b_hi, b_lo, 0, ready_b), (b_hi, b_lo, HALF // P, ready_b),
                   (o_hi, o_lo, 0, lambda kt: [state["attn"]])]
        for n in range(3):
            for c in range(4):
                if (n, c) != (0, 0):
                    gate_chunk(n, c)
                up_chunk(n, c, *sources[n][:2], sources[n][2], sources[n][3])
        attn_needed = len(tiles) - 4 * 4 - 3 * 8
        assert attn_step + GAP * n_units + 8 < attn_needed

        def ready_mix(kt):
            return [mix["mixed", kt // 2]]

        for c in range(3):
            chunk(w_out, c * CHUNK, mix_hi, mix_lo, ready_mix, y_epilogue(c), KT)
        u3_ready = {}

        def after_out():
            t_rstd = rms([sum_squares([sq["t"]])])
            for j in range(KT // 2):
                t = residual_pair(j, "gain1", t_rstd)
                add_squares(flat(x[:, 2 * j:2 * j + 2, :]), [t], j == 0)
            state["rstd3"] = rms([sum_squares([sq["t"]])])
            spread(state["out_end"], norm3)

        def norm3(j):
            u3_ready[j] = norm_pair(j, x, "gain2", state["rstd3"], u_hi, u_lo)
        chunk(w_out, 3 * CHUNK, mix_hi, mix_lo, ready_mix, y_epilogue(3, after_out), KT)
        state["out_end"] = len(tiles) - 1

        hid_ready = {}

        def up_epilogue(c):
            def go(s):
                got = []
                for b in range(2):
                    r_, h_ = tmp[b], tmp[2 + b]
                    j = 4 * c + 2 * b
                    got.append(act(r_[:, :], flat(acc[s][b][:, :, :]), ACT.Relu, [tile_done[-1]] + tmp_free[b]))
                    t = tt(h_[:, :], r_[:, :], r_[:, :], ALU.mult, [got[b]] + tmp_free[2 + b])
                    tmp_free[b] = [t]
                    t = split(flat(hid_hi[:, j:j + 2, :]), flat(hid_lo[:, j:j + 2, :]), h_[:, :], [t])
                    tmp_free[2 + b] = [t]
                    hid_ready[j // 2] = t
                evacuated(s, got)
            return go

        def down_epilogue(half, c, then=None):
            def go(s):
                if half == 0:
                    got = [act(flat(y[:, 4 * c + 2 * b:4 * c + 2 * b + 2, :]), flat(acc[s][b][:, :, :]), ACT.Copy,
                               [tile_done[-1]]) for b in range(2)]
                    evacuated(s, got)
                    mix["half0", c] = got[1]
                    return
                got = []
                for b in range(2):
                    j = 4 * c + 2 * b
                    ys = flat(y[:, j:j + 2, :])
                    got.append(tt(ys, flat(acc[s][b][:, :, :]), ys, ALU.add, [tile_done[-1], mix["half0", c]]))
                    add_squares(ys, [got[b]], c == 0 and b == 0)
                evacuated(s, got)
                if then:
                    then()
            return go

        def finish():
            t_rstd = rms([sum_squares([sq["t"]])])
            for j in range(KT // 2):
                t = residual_pair(j, "gain3", t_rstd)
                sp_q.put_dma(lambda e, j=j: e.dma_start(out[:, 2 * j:2 * j + 2, :], x[:, 2 * j:2 * j + 2, :]),
                             out_done, [t])
            sp_q.items.append((None, [(out_done[0], out_done[1])], None))

        hidden_kt = MLP // 2 // P
        for half in range(2):
            for c in range(MLP // 2 // CHUNK):
                chunk(w_up, half * (MLP // 2) + c * CHUNK, u_hi, u_lo, lambda kt: [u3_ready[kt // 2]],
                      up_epilogue(c), KT)
            rows = w_down[half * (MLP // 2):(half + 1) * (MLP // 2), :]
            for c in range(4):
                chunk(rows, c * CHUNK, hid_hi, hid_lo, lambda kt: [hid_ready[kt // 2]],
                      down_epilogue(half, c, finish if (half, c) == (1, 3) else None), hidden_kt)

        for n in range(min(N_STAGE, len(tiles))):
            load_tile(n)
        for n in range(AHEAD):
            split_tile(n)
        step = 0
        while step < len(tiles) or any(s_ >= step for s_ in jobs):
            if step + AHEAD < len(tiles):
                split_tile(step + AHEAD)
            if step < len(tiles):
                multiply_tile(step)
            for fn in jobs.pop(step, []):
                fn()
            step += 1

        block = ctx.enter_context(nc.Block())

        @block.sync
        def _(e):
            sp_q.play(e)

        @block.scalar
        def _(e):
            scalar.play(e)

        @block.vector
        def _(e):
            vector.play(e)

        @block.tensor
        def _(e):
            tensor.play(e)


def kernel(**inputs):
    import numpy as _np
    import concourse.bacc as _bacc
    from concourse import mybir as _mybir
    from concourse.bass_utils import run_bass_kernel_spmd as _run

    get = {k_: _np.asarray(v_) for k_, v_ in inputs.items()}

    def features(a, extra=()):
        a = a.reshape(-1, a.shape[-1] // P, P)
        return _np.ascontiguousarray(a.transpose(2, 1, 0))

    def columns(a):
        return features(a).reshape(P, -1)

    gains = get["norm_gains_2"][0]
    parts = {
        "norm_pre": get["norm_pre"][0], "norm_post": get["norm_post"][0],
        "gain0": gains[0], "gain1": gains[1], "gain2": gains[2], "gain3": gains[3],
        "a_conv_w": get["a_conv_w"][0], "a_conv_b": get["a_conv_b"][0],
        "b_r": get["a_b_r"][0].reshape(-1), "b_i": get["a_b_i"][0].reshape(-1), "lam": get["a_lam"][0],
        "pool_scale": get["pool_scale_2"][0], "conv_w": get["conv_w_2"][0],
    }
    packed = [columns(parts[name]) for name, _ in VEC_SIZES[:-1]]
    packed.append(get["b_gate_2"][0].reshape(3, KT, P).transpose(2, 0, 1).reshape(P, -1))
    cst, ahead, onehot = shape_constants()
    w_in = get["w_in_2"][0]
    tail = _np.concatenate([w_in[:, C_KI:C_WI], w_in[:, C_KI:C_WI], w_in[:, C_WI:]], axis=1)
    arrays = {
        "x": features(get["x"][0]), "p": features(get["p"][0, 0]).reshape(P, -1),
        "vec": _np.concatenate(packed, axis=1), "cst": cst, "ahead": ahead, "onehot": onehot,
        "table": get["rel_bias_2"],
        "ple_proj": get["ple_w_proj"][0], "ple_gate": get["ple_w_gate"][0], "a_in": get["a_w_in"][0],
        "a_r": get["a_w_r"][0], "a_i": get["a_w_i"][0], "a_out": get["a_w_out"][0], "w_in": w_in,
        "w_tail": tail.reshape(KT, P, TAIL).transpose(1, 0, 2), "pool_w": get["pool_w_2"][0],
        "w_branch": get["w_branch_2"][0], "w_gate": get["w_gate_2"][0], "w_out": get["w_out_2"][0],
        "w_up": get["w_up_2"][0], "w_down": get["w_down_2"][0],
    }
    arrays = {f"in_{k_}": _np.ascontiguousarray(v_) for k_, v_ in arrays.items()}
    nc = _bacc.Bacc("TRN2", target_bir_lowering=False, num_devices=1)
    ap = {k_[3:]: nc.dram_tensor(k_, v_.shape, _mybir.dt.from_np(v_.dtype), kind="ExternalInput").ap()
          for k_, v_ in arrays.items()}
    out = nc.dram_tensor("out_dram", (P, KT, T), _mybir.dt.float32, kind="ExternalOutput").ap()
    rev_dram = nc.dram_tensor("rev_dram", (HEADS, REV), _mybir.dt.float32).ap()
    build(nc, ap["x"], ap["p"], ap["vec"], ap["cst"], ap["ahead"], ap["onehot"], ap["table"], rev_dram,
          ap["ple_proj"], ap["ple_gate"], ap["a_in"], ap["a_r"], ap["a_i"], ap["a_out"], ap["w_in"], ap["w_tail"],
          ap["pool_w"], ap["w_branch"], ap["w_gate"], ap["w_out"], ap["w_up"], ap["w_down"], out)
    got = _run(nc, [arrays], core_ids=[0]).results[0]["out_dram"]
    return _np.ascontiguousarray(got.transpose(2, 1, 0)).reshape(1, T, D)
```

```python
from contextlib import ExitStack

import numpy as np

import concourse.bass as bass
from concourse import mybir

F32 = mybir.dt.float32
F32R = mybir.dt.float32r
BF16 = mybir.dt.bfloat16
ALU = mybir.AluOpType
ACT = mybir.ActivationFunctionType
AX_X = mybir.AxisListType.X

P = 128
T = 256
D = 2048
KT = D // P
EPS = 1e-6
CONV_W = 4
LRU_C = 8.0
PLE = 256
POOL_WINDOWS = (2, 4, 8, 16)
PAD_POOL = 16
HALF = D // 2
CONV2_W = 3
HEADS = 8
HD = 128
KV_HEADS = 2
GROUP = HEADS // KV_HEADS
IDX_HEADS = 16
IDX_DIM = 64
TOPK = T // 4
BUCKETS = 32
MAX_EXACT = BUCKETS // 2
MAX_DIST = 128
MLP = 4 * D
TOK_TILES = T // P
REV = P - 1 + T
MASKED = -1e38
TAKEN = -3e38
UNSELECTED = -1e30

WCOLS = 1024
CHUNK = 512
N_STAGE = 4
N_SPLIT = 4
AHEAD = N_SPLIT - 1

C_POOL, C_UCONV, C_CGATE, C_BGATE, C_Q, C_KV, C_QI, C_KI, C_WI = (
    0, 1024, 2048, 3072, 4096, 5120, 5632, 6656, 6720)
TAIL = 2 * IDX_DIM + IDX_HEADS

VEC_SIZES = [("norm_pre", KT), ("norm_post", KT), ("gain0", KT), ("gain1", KT), ("gain2", KT), ("gain3", KT),
             ("a_conv_w", KT * CONV_W), ("a_conv_b", KT), ("b_r", KT), ("b_i", KT), ("lam", KT),
             ("pool_scale", HALF // P), ("conv_w", HALF // P * CONV2_W), ("b_gate", 3 * KT)]
VEC = {}
VEC_COLS = 0
for _name, _n in VEC_SIZES:
    VEC[_name] = (VEC_COLS, _n)
    VEC_COLS += _n

CST = {"ident": (0, P), "flip": (P, P), "inv_count": (2 * P, 4 * PAD_POOL), "eps": (2 * P + 4 * PAD_POOL, 1)}
CST_COLS = 2 * P + 4 * PAD_POOL + 1


def shape_constants():
    cst = np.zeros((P, CST_COLS), np.float32)
    cst[:, 0:P] = np.eye(P)
    cst[:, P:2 * P] = np.eye(P)[::-1]
    for g, w in enumerate(POOL_WINDOWS):
        at = CST["inv_count"][0] + g * PAD_POOL
        cst[:, at:at + PAD_POOL] = 1.0 / np.minimum(np.arange(PAD_POOL) + 1, w)
    cst[:, CST["eps"][0]] = EPS
    query = np.arange(T).reshape(TOK_TILES, P)
    ahead = np.where(np.arange(T)[None, None, :] > query[:, :, None], MASKED, 0.0)
    ahead = np.ascontiguousarray(ahead.transpose(1, 0, 2)).astype(np.float32)
    dist = np.maximum(T - 1 - np.arange(REV), 0)
    far = MAX_EXACT + (np.log(np.maximum(dist, 1).astype(np.float32) / np.float32(MAX_EXACT))
                       / np.float32(np.log(MAX_DIST / MAX_EXACT)) * (BUCKETS - MAX_EXACT)).astype(np.int32)
    bucket = np.where(dist < MAX_EXACT, dist, np.minimum(far, BUCKETS - 1))
    onehot = (np.arange(BUCKETS)[:, None] == bucket[None, :]).astype(np.float32)
    return cst, ahead, onehot


class Queue:

    def __init__(self, done):
        self.items = []
        self.done = done
        self.count = 0

    def put(self, make, after=(), signal=True):
        if signal:
            self.count += 1
        self.items.append((make, [t for t in after if t is not None], (self.done, 1) if signal else None))
        return (self.done, self.count) if signal else None

    def put_dma(self, make, sem, after=()):
        sem[1] += 16
        self.items.append((make, [t for t in after if t is not None], (sem[0], 16)))
        return (sem[0], sem[1])

    def play(self, engine):
        seen = {}
        for make, after, inc in self.items:
            for sem, value in after:
                if seen.get(sem.name, 0) < value:
                    engine.wait_ge(sem, value)
                    seen[sem.name] = value
            if make is None:
                continue
            ins = make(engine)
            if inc:
                ins.then_inc(inc[0], inc[1])


class Tile:

    def __init__(self, loads, cols, products, needs):
        self.loads = loads
        self.cols = cols
        self.products = products
        self.needs = needs


def build(nc, x_in, p_in, vec_in, cst_in, ahead_in, onehot_in, table_in, rev_dram,
          ple_proj, ple_gate, a_in, a_r, a_i, a_out, w_in, w_tail, pool_w, w_branch, w_gate, w_out, w_up, w_down,
          out):
    with ExitStack() as ctx:
        def sem(name):
            return ctx.enter_context(nc.semaphore(name))

        cursor = [(nc.sbuf_base + 63) // 64 * 64]

        def at(name, shape, dt, offset):
            return nc.alloc_sbuf_tensor_at(name, shape, dt, offset=offset)

        def fixed(name, shape, dt=F32):
            size = int(np.prod(shape[1:])) * (2 if dt == BF16 else 4)
            t = at(name, shape, dt, cursor[0])
            cursor[0] += (size + 63) // 64 * 64
            return t

        x = fixed("x", [P, KT, T])
        y_base = cursor[0]
        y = fixed("y", [P, KT, T])
        stage = fixed("stage", [P, N_STAGE, WCOLS])
        w_hi = fixed("w_hi", [P, N_SPLIT, WCOLS], F32R)
        w_lo = fixed("w_lo", [P, N_SPLIT, WCOLS], F32R)
        vec = fixed("vec", [P, VEC_COLS])
        cst = fixed("cst", [P, CST_COLS])
        ones = fixed("ones", [P, P])
        ident_b = fixed("ident_b", [P, P], BF16)
        tmp = [fixed(f"tmp{i}", [P, 2 * T]) for i in range(4)]
        rstd_u = fixed("rstd_u", [P, T])
        rstd_y = fixed("rstd_y", [P, T])
        rstd_col = fixed("rstd_col", [P, TOK_TILES])
        squares = fixed("squares", [P, 2 * T])
        sp = fixed("sp", [P, 4, KT])
        wi = fixed("wi", [P, TOK_TILES, IDX_HEADS])
        top8 = fixed("top8", [P, 8])
        row_max = fixed("row_max", [P, 2, GROUP])
        row_sum = fixed("row_sum", [P, 2, GROUP])
        dummy = fixed("dummy", [P, 1])
        SPLIT_ACT = 2 * KT * T * 4
        region_a = cursor[0]
        region_b = region_a + SPLIT_ACT
        region_c = region_b + SPLIT_ACT

        def pair(name, kts, offset, offset_lo=None):
            lo_at = offset + kts * T * 4 if offset_lo is None else offset_lo
            return at(name + "_hi", [P, kts, T], F32R, offset), at(name + "_lo", [P, kts, T], F32R, lo_at)

        u1_hi, u1_lo = pair("u1", KT, region_a)
        g_hi, g_lo = pair("g", KT, region_b)
        h_hi, h_lo = pair("h", KT, region_a)
        u2_hi, u2_lo = pair("u2", KT, region_b)
        b_hi, b_lo = pair("b", 2 * HALF // P, region_a)
        mix_hi, mix_lo = pair("mix", KT, region_a)
        u3_hi, u3_lo = pair("u3", KT, region_b)
        hid_hi, hid_lo = pair("hid", MLP // 2 // P, region_a, region_c)

        hs = at("hs", [P, KT, T], F32, region_c)
        pp = at("pp", [P, KT, T], F32, region_c)
        o = region_c + 16384
        xb = at("xb", [P, 4, T + CONV_W - 1], F32, o)
        p32 = at("p32", [P, 2 * T], F32, o)
        p_hi, p_lo = pair("p", 2, o + 2048)
        o += 4160
        xc = at("xc", [P, 4, T], F32, o + 2048)
        xc_hi, xc_lo = pair("xc", 4, o + 6144)
        t_buf = at("t_buf", [P, 4, T], F32, o + 6144)
        r_buf = at("r_buf", [P, 4, T], F32, o + 14336)
        i_buf = at("i_buf", [P, 4, T], F32, o + 18432)
        a_buf = at("a_buf", [P, 4, T], F32, o + 22528)
        o_hi, o_lo = pair("o", HEADS, region_c)
        bias = at("bias", [P, HEADS, T], F32, region_c)
        qi = at("qi", [P, IDX_HEADS // 2, T], F32, region_c + 8192)
        q = at("q", [P, HEADS, T], F32, region_c + 16384)
        o = region_c + 24576
        k = at("k", [P, KV_HEADS, T], F32, o)
        v = at("v", [P, TOK_TILES, KV_HEADS * HD], F32, o + 2048)
        ki = at("ki", [P, T], F32, o + 4096)
        o += 5120
        score = at("score", [P, TOK_TILES, T], F32, o)
        left = at("left", [P, T], F32, o + 2048)
        mask = at("mask", [P, TOK_TILES, T], BF16, o + 3072)
        ahead = at("ahead", [P, TOK_TILES, T], F32, o + 4096)
        prob_t = [at(f"prob_t{i}", [P, 4, P], F32, o + 6144 + 2048 * i) for i in range(2)]
        prob = [at(f"prob{i}", [P, 2 * T], F32, o + 10240 + 2048 * i) for i in range(2)]
        relu = [at(f"relu{i}", [P, 2 * T], F32, o + 10240 + 2048 * i) for i in range(2)]
        onehot = at("onehot", [BUCKETS, REV], F32, o + 6144)
        rev = at("rev", [HEADS, REV], F32, o + 7680)
        table = at("table", [BUCKETS, HEADS], F32, o + 9216)
        gates = at("gates", [P, 4, T], F32, o + 14336)
        pool_u = at("pool_u", [P, 4, T], F32, y_base)
        conv_z = at("conv_z", [P, 4, T], F32, y_base)
        d_lo = at("d_lo", [P, 4, T], F32R, y_base + 4096)
        conv_y = at("conv_y", [P, 4, T], F32, y_base + 4096)
        conv_u = at("conv_u", [P, 4, T], F32, y_base + 8192)
        d_hi = at("d_hi", [P, 4, T], F32R, y_base + 12288)

        acc = [[ctx.enter_context(nc.psum_tensor(f"acc{s}{b}", [P, 2, T], F32)) for b in range(2)] for s in range(2)]
        misc = [ctx.enter_context(nc.psum_tensor(f"misc{i}", [P, 2 * T], F32)) for i in range(4)]

        sp_q = Queue(None)
        scalar = Queue(sem("scalar_done"))
        vector = Queue(sem("vector_done"))
        tensor = Queue(sem("tensor_done"))
        stage_in = [[sem(f"stage_in{i}"), 0] for i in range(N_STAGE)]
        const_in = [sem("const_in"), 0]
        x_in_sem = [[sem(f"x_in{i}"), 0] for i in range(4)]
        late_in = [sem("late_in"), 0]
        rev_out = [sem("rev_out"), 0]
        bias_in = [sem("bias_in"), 0]
        out_done = [sem("out_done"), 0]

        def act(out, in_, func, after=(), bias=None, scale=None, accum=None):
            kw = {}
            if bias is not None:
                kw["bias"] = bias
            if scale is not None:
                kw["scale"] = scale
            if accum is not None:
                kw["accum_out"] = accum
            return scalar.put(lambda e: e.activation(out, in_, func, **kw), after)

        def tt(out, a, b, op, after=()):
            return vector.put(lambda e: e.tensor_tensor(out, a, b, op), after)

        def ts(out, a, s1, s2, op0, op1, after=()):
            if s2 is None:
                return vector.put(lambda e: e.tensor_scalar(out, a, s1, None, op0), after)
            return vector.put(lambda e: e.tensor_scalar(out, a, s1, s2, op0, op1), after)

        def stt(out, a, s, b, op0, op1, after=()):
            return vector.put(lambda e: e.scalar_tensor_tensor(out=out, in0=a, scalar=s, in1=b, op0=op0, op1=op1), after)

        def vec_do(make, after=()):
            return vector.put(make, after)

        def mm(out, lhs, rhs, start, stop, after=(), signal=False):
            return tensor.put(lambda e: e.matmul(out, lhs, rhs, start=start, stop=stop, skip_group_check=True),
                              after, signal)

        def v_of(name, i):
            return vec[:, VEC[name][0] + i:VEC[name][0] + i + 1]

        def c_of(name):
            return cst[:, CST[name][0]:CST[name][0] + CST[name][1]]

        def as32(ap):
            return ap.bitcast(F32)

        def split(hi, lo, src, after=()):
            t_hi = act(hi, src, ACT.Copy, after)
            return tt(lo, src, as32(hi), ALU.subtract, [t_hi])

        tiles = []
        jobs = {}
        tile_done = []
        split_done = {}

        now = [0]

        def soon(delay, fn):
            job(now[0] + delay, fn)

        def job(step, fn):
            jobs.setdefault(step, []).append(fn)

        def load_tile(n):
            slot = n % N_STAGE
            before = [split_done[n - N_STAGE]] if n >= N_STAGE else []
            for (a, b), shape_k, src in tiles[n].loads:
                dst = stage[:, slot, a:b].rearrange("p (k n) -> p k n", k=shape_k)
                sp_q.put_dma(lambda e, dst=dst, src=src: e.dma_start(dst, src), stage_in[slot], before)
            tiles[n].landed = (stage_in[slot][0], stage_in[slot][1])

        def split_tile(n):
            slot, buf, cols = n % N_STAGE, n % N_SPLIT, tiles[n].cols
            free = [tile_done[n - N_SPLIT]] if n >= N_SPLIT else []
            src = stage[:, slot, 0:cols]
            hi = w_hi[:, buf, 0:cols]
            t_hi = act(hi, src, ACT.Copy, [tiles[n].landed] + free)
            split_done[n] = tt(w_lo[:, buf, 0:cols], src, as32(hi), ALU.subtract, [t_hi])
            if n + N_STAGE < len(tiles):
                load_tile(n + N_STAGE)

        def multiply_tile(n):
            buf = n % N_SPLIT
            tile = tiles[n]
            after = [split_done[n]] + tile.needs()
            products = tile.products(w_hi[:, buf, :], w_lo[:, buf, :])
            for i, (out_, lhs, rhs, start, stop) in enumerate(products):
                token = mm(out_, lhs, rhs, start, stop, after, signal=i == len(products) - 1)
                after = ()
            tile_done.append(token)

        bank_free = [[], []]
        chunk_no = [0]

        def chunk(w, c0, act_hi, act_lo, ready, epilogue, kts, k0=0, delay=0, cols=CHUNK):
            s = chunk_no[0] % 2
            chunk_no[0] += 1
            per = WCOLS // cols
            first = len(tiles)
            for i in range(0, kts, per):
                src = w[i * P:(i + per) * P, c0:c0 + cols].rearrange("(k p) n -> p k n", p=P)

                def products(hi, lo, i=i):
                    got = []
                    for dk in range(per):
                        kt = i + dk
                        for j in range(cols // P):
                            c = dk * cols + j * P
                            o_ = acc[s][j // 2][:, j % 2, :]
                            wh, wl = hi[:, c:c + P], lo[:, c:c + P]
                            xh, xl = act_hi[:, k0 + kt, :], act_lo[:, k0 + kt, :]
                            got += [(o_, wh, xh, kt == 0 and j % 2 == 0, False), (o_, wh, xl, False, False),
                                    (o_, wl, xh, False, kt == kts - 1)]
                    return got

                def needs(i=i):
                    return (list(bank_free[s]) if i == 0 else []) + \
                        [t for dk in range(per) for t in ready(k0 + i + dk)]

                tiles.append(Tile([((0, WCOLS), per, src)], WCOLS, products, needs))
            job(len(tiles) - 1, lambda: epilogue(s))
            return first

        def block_chunk(w, n0, act_hi, act_lo, ready, epilogue):
            s = chunk_no[0] % 2
            chunk_no[0] += 1
            src = w[n0:n0 + 2].rearrange("b (k p) d -> p (b k) d", p=P)

            def products(hi, lo):
                got = []
                for b in range(2):
                    for e in range(2):
                        for kk in range(2):
                            kt = 2 * b + kk
                            c = kt * 256 + e * P
                            o_ = acc[s][b][:, e, :]
                            wh, wl = hi[:, c:c + P], lo[:, c:c + P]
                            got += [(o_, wh, act_hi[:, kt, :], kk == 0 and e == 0, False),
                                    (o_, wh, act_lo[:, kt, :], False, False),
                                    (o_, wl, act_hi[:, kt, :], False, kk == 1)]
                return got

            tiles.append(Tile([((0, WCOLS), 4, src)], WCOLS, products, lambda: list(bank_free[s]) + ready(0)))
            job(len(tiles) - 1, lambda: epilogue(s))

        def evacuated(s, tokens):
            bank_free[s] = list(tokens)

        norm = {}
        misc_free = [None] * 4
        tmp_free = [[] for _ in range(4)]

        def flat(ap):
            return ap.rearrange("p k t -> p (k t)")

        def both(rstd):
            return rstd[:, :].unsqueeze(1).broadcast_to([P, 2, T])

        def square_sums(parts, after, first=True, last=True):
            for i, part in enumerate(parts):
                t = mm(misc[0][:, 0:T], ones[:, :], part, first and i == 0, last and i == len(parts) - 1,
                       list(after) + [misc_free[0]], signal=i == len(parts) - 1)
            return t

        def rms(rstd, after):
            t = act(rstd[:, :], misc[0][:, 0:T], ACT.Sqrt, after, bias=c_of("eps"), scale=1.0 / D)
            misc_free[0] = t
            return vec_do(lambda e: e.reciprocal(rstd[:, :], rstd[:, :]), [t])

        def load_sqrt():
            act(dummy[:, :], c_of("eps"), ACT.Sqrt, [t_const])

        def gained_split(kt, src, gain, hi, lo, after):
            n = kt // 2 % 2
            b = tmp[n]
            for d in range(2):
                t = ts(b[:, d * T:(d + 1) * T], src[:, kt + d, :], v_of(gain, kt + d), None, ALU.mult, None,
                       list(after) + tmp_free[n])
            t = split(flat(hi[:, kt:kt + 2, :]), flat(lo[:, kt:kt + 2, :]), b[:, :], [t])
            tmp_free[n] = [t]
            return t

        def flat(ap):
            return ap.rearrange("p k t -> p (k t)")

        def load_x(qd):
            sp_q.put_dma(lambda e: e.dma_start(x[:, 4 * qd:4 * qd + 4, :], x_in[:, 4 * qd:4 * qd + 4, :]),
                         x_in_sem[qd])
        for d_, s_ in [(vec[:, :], vec_in), (cst[:, :], cst_in)]:
            t_const = scalar.put_dma(lambda e, d_=d_, s_=s_: e.dma_start(d_, s_), const_in)
        t_ones = vec_do(lambda e: e.memset(ones[:, :], 1.0))
        t_xb_pad = vec_do(lambda e: e.memset(xb[:, :, 0:CONV_W - 1], 0.0))

        def softplus():
            lam = vec[:, VEC["lam"][0]:VEC["lam"][0] + KT]
            e_, z_, z2_, s_ = (sp[:, i, :] for i in range(4))
            t = act(e_, lam, ACT.Abs, [t_const])
            t = act(e_, e_, ACT.Exp, [t], scale=-1.0)
            t = ts(z_, e_, 2.0, None, ALU.add, None, [t])
            t = vec_do(lambda e: e.reciprocal(z2_, z_), [t])
            t = tt(z_, z2_, e_, ALU.mult, [t])
            t = tt(z2_, z_, z_, ALU.mult, [t])
            t = vec_do(lambda e: e.memset(s_, 1.0 / 17), [])
            for odd in (15, 13, 11, 9, 7, 5, 3, 1):
                t = tt(s_, s_, z2_, ALU.mult, [t])
                t = ts(s_, s_, 1.0 / odd, None, ALU.add, None, [t])
            t = tt(s_, s_, z_, ALU.mult, [t])
            t = ts(e_, lam, -1.0, 0.0, ALU.mult, ALU.max, [t])
            t = stt(z_, s_, 2.0, e_, ALU.mult, ALU.add, [t])
            t = ts(decay, z_, LRU_C, None, ALU.mult, None, [t])
            state["decay"] = ts(neg_decay, z_, -LRU_C, None, ALU.mult, None, [t])

        decay, neg_decay = sp[:, 2, :], sp[:, 3, :]

        u1_ready = {}
        state = {}
        sq = {"t": None}

        def ready_u(kt):
            return [u1_ready[kt // 2]]

        def first_gain(j):
            u1_ready[j] = gained_split(2 * j, x, "norm_pre", u1_hi, u1_lo, [(x_in_sem[j // 2][0], 16), t_const])

        def first_squares(qd):
            t = act(y[:, 4 * qd:4 * qd + 4, :], x[:, 4 * qd:4 * qd + 4, :], ACT.Square, [(x_in_sem[qd][0], 16)])
            state["x_squared", qd] = t

        def first_sums(qd):
            state["sums0"] = square_sums([y[:, 4 * qd + d, :] for d in range(4)], [state["x_squared", qd], t_ones],
                                         qd == 0, qd == 3)
        for j in range(AHEAD, KT // 2):
            job(j - AHEAD, lambda j=j: first_gain(j))
        for qd in range(4):
            job(qd + 1, lambda qd=qd: first_squares(qd))
            job(qd + 2, lambda qd=qd: first_sums(qd))

        def first_rms():
            state["rstd0"] = rms(rstd_u, [state["sums0"]])
        job(6, first_rms)
        job(9, softplus)

        xc_ready, h_ready, xb_free = {}, {}, {}

        def xb_epilogue(c):
            def go(s):
                got = [tt(xb[:, 2 * b:2 * b + 2, CONV_W - 1:], acc[s][b][:, :, :], both(rstd_u), ALU.mult,
                          [tile_done[-1], state["rstd0"], t_xb_pad] + xb_free.get(c - 1, [])) for b in range(2)]
                evacuated(s, got)
                state["xb", c] = got
                if c == 0:
                    plan_conv(0, 1)
            return go

        def plan_conv(c, delay):
            soon(delay, lambda: conv(c, (0, 1)))
            soon(delay + 1, lambda: conv(c, (2, 3)))

            def conv_split():
                xc_ready[c] = split(flat(xc_hi[:, :, :]), flat(xc_lo[:, :, :]), flat(xc[:, :, :]),
                                    xb_free[c] + [state.get("xc_read"), state.get("t_buf_free")])
            soon(delay + 2, conv_split)

        def conv(c, js):
            got = state["xb", c]
            toks = {}
            for i in range(CONV_W):
                for j in js:
                    kt = 4 * c + j
                    w_ = v_of("a_conv_w", kt * CONV_W + i)
                    if i == 0:
                        toks[j] = ts(xc[:, j, :], xb[:, j, 0:T], w_, v_of("a_conv_b", kt), ALU.mult, ALU.add,
                                     [got[j // 2], state.get("xc_free")])
                    else:
                        toks[j] = stt(xc[:, j, :], xb[:, j, i:i + T], w_, xc[:, j, :], ALU.mult, ALU.add,
                                      [toks[j]])
            xb_free[c] = [toks[js[-1]]]

        def recurrence_gate(buf, name, key, c):
            def go(s):
                got = [act(buf[:, j, :], acc[s][j // 2][:, j % 2, :], ACT.Sigmoid,
                           [tile_done[-1]] + h_ready.get(c - 1, []), bias=v_of(name, 4 * c + j)) for j in range(4)]
                evacuated(s, [got[3]])
                state[key] = got[3]
                if key == "i":
                    state["xc_read"] = tile_done[-1]
                    plan_scan(c)
            return go

        def plan_scan(c):
            def decays():
                for j in range(4):
                    act(a_buf[:, j, :], r_buf[:, j, :], ACT.Exp, [state["r"], state["decay"]],
                        scale=neg_decay[:, 4 * c + j:4 * c + j + 1])

            def tanhs():
                for j in range(4):
                    state["a"] = act(t_buf[:, j, :], r_buf[:, j, :], ACT.Tanh, [state["xc_read"]],
                                     scale=decay[:, 4 * c + j:4 * c + j + 1])

            def ones_less_squares():
                r_, a_, t_ = (flat(b_[:, :, :]) for b_ in (r_buf, a_buf, t_buf))
                t = tt(r_, a_, a_, ALU.mult, [state["a"]])
                state["m"] = stt(r_, r_, 1.0, t_, ALU.add, ALU.mult, [t])

            def inputs():
                state["xc_free"] = tt(flat(i_buf[:, :, :]), flat(i_buf[:, :, :]), flat(xc[:, :, :]), ALU.mult,
                                      [state["i"]])
                state["root"] = act(flat(t_buf[:, :, :]), flat(r_buf[:, :, :]), ACT.Sqrt, [state["m"]])

            def scans():
                t = tt(flat(i_buf[:, :, :]), flat(i_buf[:, :, :]), flat(t_buf[:, :, :]), ALU.mult,
                       [state["root"], state["xc_free"]])
                state["t_buf_free"] = t
                for j in range(4):
                    t_h = vec_do(lambda e, j=j: e.tensor_tensor_scan(hs[:, 4 * c + j, :], a_buf[:, j, :],
                                                                     i_buf[:, j, :], 0.0, ALU.mult, ALU.add), [t])
                h_ready[c] = [t_h]

            for n, fn in enumerate((decays, tanhs, ones_less_squares, inputs, scans)):
                soon(n + 1, fn)
            if c < 3:
                plan_conv(c + 1, 6)

        y_ready = {}

        def gate_epilogue(c):
            def go(s):
                got = [tt(tmp[b][:, :].rearrange("p (k t) -> p k t", k=2), acc[s][b][:, :, :], both(rstd_u), ALU.mult,
                          [tile_done[-1]] + tmp_free[b]) for b in range(2)]
                evacuated(s, got)

                def silus():
                    for b in range(2):
                        state["silu", b] = act(tmp[b][:, :], tmp[b][:, :], ACT.Silu, [got[b]])

                def gated():
                    for b in range(2):
                        j = 4 * c + 2 * b
                        t = tt(tmp[2 + b][:, :], flat(hs[:, j:j + 2, :]), tmp[b][:, :], ALU.mult,
                               [state["silu", b]] + h_ready[c] + tmp_free[2 + b])
                        tmp_free[b] = [t]
                        t = split(flat(g_hi[:, j:j + 2, :]), flat(g_lo[:, j:j + 2, :]), tmp[2 + b][:, :], [t])
                        tmp_free[2 + b] = [t]
                        y_ready[2 * c + b] = t
                soon(1, silus)
                soon(2, gated)
            return go

        def xb_chunk(c):
            chunk(a_in, c * CHUNK, u1_hi, u1_lo, ready_u, xb_epilogue(c), KT)

        def ri_chunk(c):
            block_chunk(a_r, 2 * c, xc_hi, xc_lo, lambda kt: [xc_ready[c]], recurrence_gate(r_buf, "b_r", "r", c))
            block_chunk(a_i, 2 * c, xc_hi, xc_lo, lambda kt: [xc_ready[c]], recurrence_gate(i_buf, "b_i", "i", c))

        def g_chunk(c):
            chunk(a_in, D + c * CHUNK, u1_hi, u1_lo, ready_u, gate_epilogue(c), KT)

        xb_chunk(0)
        for c in range(1, 4):
            xb_chunk(c)
            ri_chunk(c - 1)
        g_chunk(0)
        ri_chunk(3)
        for c in range(1, 4):
            g_chunk(c)

        def add_squares(src, after, first):
            t = act(tmp[2][:, :], src, ACT.Square, list(after) + tmp_free[2])
            if first:
                sq["t"] = vec_do(lambda e: e.tensor_copy(squares[:, :], tmp[2][:, :]), [t, sq["t"]])
            else:
                sq["t"] = tt(squares[:, :], squares[:, :], tmp[2][:, :], ALU.add, [t, sq["t"]])
            tmp_free[2] = [sq["t"]]
            return t

        def all_squares():
            return [squares[:, 0:T], squares[:, T:2 * T]]

        def y_copy(s, b, c, after):
            j = 4 * c + 2 * b
            return act(flat(y[:, j:j + 2, :]), flat(acc[s][b][:, :, :]), ACT.Copy, after)

        def y_epilogue(c):
            def go(s):
                got = []
                for b in range(2):
                    y_copy(s, b, c, [tile_done[-1]])
                    got.append(add_squares(flat(acc[s][b][:, :, :]), [], c == 0 and b == 0))
                evacuated(s, got)
            return go

        def y_last(then):
            def go(s):
                t_sum = square_sums(all_squares(), [sq["t"]], True, False)
                for b in range(2):
                    n = 2 + b
                    t = act(tmp[n][:, :], flat(acc[s][b][:, :, :]), ACT.Square, [tile_done[-1]] + tmp_free[n])
                    t_sum = square_sums([tmp[n][:, 0:T], tmp[n][:, T:2 * T]], [t], False, b == 1)
                    tmp_free[n] = [t_sum]
                sq["t"] = t_sum
                t_rstd = rms(rstd_y, [t_sum])
                got = [y_copy(s, b, 3, []) for b in range(2)]
                state["y"] = got[1]
                evacuated(s, got)
                then(t_rstd)
            return go

        def residual_pair(j, gain, t_rstd, after=()):
            b = tmp[j % 2]
            for d in range(2):
                kt = 2 * j + d
                t = stt(b[:, d * T:(d + 1) * T], y[:, kt, :], v_of(gain, kt), rstd_y[:, :], ALU.mult, ALU.mult,
                        [t_rstd] + list(after) + tmp_free[j % 2])
            t = tt(flat(x[:, 2 * j:2 * j + 2, :]), flat(x[:, 2 * j:2 * j + 2, :]), b[:, :], ALU.add, [t])
            tmp_free[j % 2] = [t]
            return t

        def ready_g(kt):
            return [y_ready[kt // 2]]

        for c in range(3):
            chunk(a_out, c * CHUNK, g_hi, g_lo, ready_g, y_epilogue(c), KT)
            if c == 0:
                def load_p():
                    state["p32"] = scalar.put_dma(lambda e: e.dma_start(p32[:, :], p_in), p_in_sem, [tile_done[-1]])

                def split_p():
                    state["p"] = split(flat(p_hi[:, :, :]), flat(p_lo[:, :, :]), p32[:, :], [state["p32"]])
                job(len(tiles) - 1, load_p)
                job(len(tiles) + 3, split_p)
                job(len(tiles) + 4, load_sqrt)
        p_in_sem = [sem("p_in"), 0]

        pp_ready = {}
        h_split = {}

        def after_a_out(t_rstd):
            state["rstd1"] = t_rstd
            residual1(0)
        chunk(a_out, 3 * CHUNK, g_hi, g_lo, ready_g, y_last(after_a_out), KT)

        def pp_epilogue(c):
            def go(s):
                got = [act(flat(pp[:, 4 * c + 2 * b:4 * c + 2 * b + 2, :]), flat(acc[s][b][:, :, :]), ACT.Copy,
                           [tile_done[-1]]) for b in range(2)]
                evacuated(s, got)
                pp_ready[c] = got[1]
            return go

        def residual1(j):
            t = residual_pair(j, "norm_post", state["rstd1"], [state["y"]] if j >= 6 else [])
            h_split[j] = split(flat(h_hi[:, 2 * j:2 * j + 2, :]), flat(h_lo[:, 2 * j:2 * j + 2, :]),
                               flat(x[:, 2 * j:2 * j + 2, :]), [t])
        for c in range(4):
            chunk(ple_proj, c * CHUNK, p_hi, p_lo, lambda kt: [state["p"]], pp_epilogue(c), PLE // P)
            job(len(tiles) - 1, lambda c=c: residual1(c + 1))
        for j in range(5, KT // 2):
            job(len(tiles) + j - 5, lambda j=j: residual1(j))

        def ready_h(kt):
            return [h_split[kt // 2]]

        u2_ready = {}

        def ple_epilogue(c):
            def go(s):
                got = [act(tmp[b][:, :], flat(acc[s][b][:, :, :]), ACT.Sigmoid, [tile_done[-1]] + tmp_free[b])
                       for b in range(2)]
                evacuated(s, got)

                def finish_x(b):
                    j = 4 * c + 2 * b
                    xs = flat(x[:, j:j + 2, :])
                    g = tmp[b]
                    t = tt(g[:, :], g[:, :], flat(pp[:, j:j + 2, :]), ALU.mult, [got[b], pp_ready[c]])
                    t = tt(xs, xs, g[:, :], ALU.add, [t])
                    tmp_free[b] = [t]
                    state["x", b] = t

                def split_x(b):
                    j = 4 * c + 2 * b
                    u2_ready[j // 2] = gained_split(j, x, "gain0", u2_hi, u2_lo, [state["x", b]])

                def square_x(b):
                    j = 4 * c + 2 * b
                    add_squares(flat(x[:, j:j + 2, :]), [state["x", b]], c == 0 and b == 0)
                for n, (fn, b) in enumerate(((finish_x, 0), (finish_x, 1), (split_x, 0), (split_x, 1), (square_x, 0),
                                             (square_x, 1))):
                    soon(n // 2 + 1, lambda fn=fn, b=b: fn(b))
                if c == 3:
                    soon(4, lambda: state.__setitem__("sums2", square_sums(all_squares(), [sq["t"]])))
                    soon(5, norm2)
            return go

        def norm2():
            t = rms(rstd_u, [state["sums2"]])
            state["rstd2"] = t
            for t_ in range(TOK_TILES):
                t1 = mm(misc[1][:, t_:t_ + 1], rstd_u[:, t_ * P:(t_ + 1) * P], cst[:, 0:1], True, True,
                        [t, misc_free[1]], signal=True)
            state["rstd_col"] = vec_do(lambda e: e.tensor_copy(rstd_col[:, :], misc[1][:, 0:TOK_TILES]), [t1])
            misc_free[1] = state["rstd_col"]

        for c in range(4):
            chunk(ple_gate, c * CHUNK, h_hi, h_lo, ready_h, ple_epilogue(c), KT)

        def ready_u2(kt):
            return [u2_ready[kt // 2]]

        def bias_table():
            t1 = scalar.put_dma(lambda e: e.dma_start(onehot[:, :], onehot_in), late_in, [tile_done[-1]])
            t1 = scalar.put_dma(lambda e: e.dma_start(table[:, :], table_in), late_in)
            state["late"] = scalar.put_dma(lambda e: e.dma_start(ahead[:, :, :], ahead_in), late_in)

        def bias_rev():
            t = mm(misc[1][0:HEADS, 0:REV], table[:, :], onehot[:, :], True, True, [state["late"], misc_free[1]],
                   signal=True)
            t = act(rev[:, :], misc[1][0:HEADS, 0:REV], ACT.Copy, [t])
            misc_free[1] = t
            t = scalar.put_dma(lambda e: e.dma_start(rev_dram, rev[:, :]), rev_out, [t])
            state["bias"] = scalar.put_dma(lambda e: e.dma_start(bias[:, :, :], hankel), bias_in, [t])
        hankel = bass.AP(rev_dram.tensor, 0, [[1, P], [REV, HEADS], [1, T]])

        t_identb = {}

        def tail_chunk(epilogue):
            s = chunk_no[0] % 2
            chunk_no[0] += 1
            per = 6
            for k0 in range(0, KT, per):
                n = min(per, KT - k0)
                src = w_tail[:, k0:k0 + n, :]

                def products(hi, lo, k0=k0, n=n):
                    got = []
                    for dk in range(n):
                        kt = k0 + dk
                        c = dk * TAIL
                        kw = slice(c, c + 2 * IDX_DIM)
                        ww = slice(c + 2 * IDX_DIM, c + TAIL)
                        o_ = acc[s][0][:, 0, :]
                        xh, xl = u2_hi[:, kt, :], u2_lo[:, kt, :]
                        got += [(o_, hi[:, kw], xh, kt == 0, False), (o_, hi[:, kw], xl, False, False),
                                (o_, lo[:, kw], xh, False, kt == KT - 1)]
                        for t_ in range(TOK_TILES):
                            o_ = acc[s][1][:, t_, 0:IDX_HEADS]
                            tok = slice(t_ * P, (t_ + 1) * P)
                            got += [(o_, u2_hi[:, kt, tok], hi[:, ww], kt == 0 and t_ == 0, False),
                                    (o_, u2_lo[:, kt, tok], hi[:, ww], False, False),
                                    (o_, u2_hi[:, kt, tok], lo[:, ww], False, kt == KT - 1)]
                    return got

                def needs(k0=k0, n=n):
                    return (list(bank_free[s]) if k0 == 0 else []) + [t for d in range(n) for t in ready_u2(k0 + d)]
                tiles.append(Tile([((0, n * TAIL), n, src)], n * TAIL, products, needs))
            job(len(tiles) - 1, lambda: epilogue(s))

        def tail_epilogue(s):
            t2 = tt(ki[:, :], acc[s][0][:, 0, :], rstd_u[:, :], ALU.mult, [tile_done[-1], state["rstd2"]])
            for t_ in range(TOK_TILES):
                t2 = ts(wi[:, t_, :], acc[s][1][:, t_, 0:IDX_HEADS], rstd_col[:, t_:t_ + 1], IDX_HEADS ** -0.5,
                        ALU.mult, ALU.mult, [state["rstd_col"]])
            evacuated(s, [t2])
            state["ki"] = t2

        def copy_epilogue(dst, j0, key, scale=1.0):
            def go(s):
                got = [stt(dst[:, j0 + 2 * b:j0 + 2 * b + 2, :], acc[s][b][:, :, :], scale, both(rstd_u), ALU.mult,
                           ALU.mult, [tile_done[-1], state["rstd2"]]) for b in range(2)]
                evacuated(s, got)
                state[key] = got[1]
            return go

        def kv_chunk():
            s = chunk_no[0] % 2
            chunk_no[0] += 1
            for i in range(0, KT, 2):
                src = w_in[i * P:(i + 2) * P, C_KV:C_KV + CHUNK].rearrange("(k p) n -> p k n", p=P)

                def products(hi, lo, i=i):
                    got = []
                    for dk in range(2):
                        kt = i + dk
                        xh, xl = u2_hi[:, kt, :], u2_lo[:, kt, :]
                        for j in range(KV_HEADS):
                            c = dk * CHUNK + j * HD
                            o_ = acc[s][0][:, j, :]
                            wh, wl = hi[:, c:c + HD], lo[:, c:c + HD]
                            got += [(o_, wh, xh, kt == 0 and j == 0, False), (o_, wh, xl, False, False),
                                    (o_, wl, xh, False, kt == KT - 1)]
                        for t_ in range(TOK_TILES):
                            c = dk * CHUNK + KV_HEADS * HD
                            o_ = acc[s][1][:, t_, :]
                            tok = slice(t_ * P, (t_ + 1) * P)
                            wh, wl = hi[:, c:c + KV_HEADS * HD], lo[:, c:c + KV_HEADS * HD]
                            got += [(o_, xh[:, tok], wh, kt == 0 and t_ == 0, False), (o_, xl[:, tok], wh, False, False),
                                    (o_, xh[:, tok], wl, False, kt == KT - 1)]
                    return got

                tiles.append(Tile([((0, WCOLS), 2, src)], WCOLS, products,
                                  lambda i=i: (list(bank_free[s]) if i == 0 else []) + ready_u2(i)))

            def epilogue(s=s):
                t1 = tt(k[:, :, :], acc[s][0][:, :, :], both(rstd_u), ALU.mult, [tile_done[-1]])
                for t_ in range(TOK_TILES):
                    t2 = act(v[:, t_, :], acc[s][1][:, t_, :], ACT.Copy, [tile_done[-1], state["rstd_col"]],
                             scale=rstd_col[:, t_:t_ + 1])
                evacuated(s, [t1, t2])
                state["k"], state["v"] = t1, t2
            job(len(tiles) - 1, epilogue)

        relu_free = [None, None]
        dots = {}

        def score_banks(n):
            return (1, 2) if n % 2 == 0 else (3, 0)

        def score_dots(n, t_, heads, nk):
            for i, h in enumerate(heads):
                bank = score_banks(n)[h % 2]
                lo_p = (h % 2) * IDX_DIM
                tok = mm(misc[bank][:, i // 2 * nk:(i // 2 + 1) * nk],
                         qi[lo_p:lo_p + IDX_DIM, h // 2, t_ * P:(t_ + 1) * P],
                         ki[lo_p:lo_p + IDX_DIM, 0:nk], True, True, [state["qi"], state["ki"], misc_free[bank]],
                         signal=i == len(heads) - 1)
            dots[n] = tok

        def score_relu(n, t_, heads, nk):
            for odd in range(2):
                bank = score_banks(n)[odd]
                misc_free[bank] = act(relu[n % 2][:, odd * T:(odd + 1) * T], misc[bank][:, 0:T], ACT.Relu,
                                      [dots[n], relu_free[n % 2]])
            dots[n] = misc_free[bank]

        def score_add(n, t_, heads, nk):
            for i, h in enumerate(heads):
                base = ahead if h == 0 else score
                at_ = (h % 2) * T + i // 2 * nk
                tok = stt(score[:, t_, 0:nk], relu[n % 2][:, at_:at_ + nk], wi[:, t_, h:h + 1],
                          base[:, t_, 0:nk], ALU.mult, ALU.add, [dots[n], state["late"], state.get("score")])
                state["score"] = tok
            relu_free[n % 2] = tok

        def topk_round(t_, r, nk):
            src = score[:, t_, 0:nk] if r == 0 else left[:, 0:nk]
            tok = vec_do(lambda e: e.max(top8[:, :], src), [state["score"], state.get("mask")])
            state["score"] = vec_do(lambda e: e.match_replace(left[:, 0:nk], top8[:, :], src, TAKEN), [tok])

        def topk_mask(t_, nk):
            tok = ts(left[:, 0:nk], left[:, 0:nk], 2 * MASKED, UNSELECTED, ALU.is_ge, ALU.mult, [state["score"]])
            state["mask"] = tt(mask[:, t_, 0:nk], left[:, 0:nk], ahead[:, t_, 0:nk], ALU.add, [tok])

        unit = {}

        def a_logits(n, t_, heads, nk):
            for i, h in enumerate(heads):
                o_ = misc[1][:, i * nk:(i + 1) * nk]
                off = (TOK_TILES - 1 - t_) * P
                mm(o_, q[:, h, t_ * P:(t_ + 1) * P], k[:, h // GROUP, 0:nk], True, False,
                   [state["q"], state["k"], misc_free[1]])
                mm(o_, c_of("flip"), bias[:, h, off:off + nk], False, False, [state["bias"]])
                tok = mm(o_, ident_b[:, :], mask[:, t_, 0:nk], False, True, [state["mask"], state["identb"]],
                         signal=i == len(heads) - 1)
            unit[n] = tok

        def a_max(n, t_, heads, nk):
            g = len(heads)
            src = misc[1][:, 0:g * nk].rearrange("p (g k) -> p g k", g=g)
            m_ = row_max[:, n % 2, 0:g]
            tok = vec_do(lambda e: e.reduce_max(m_, src, AX_X), [unit[n]])
            unit[n] = ts(m_, m_, -1.0, None, ALU.mult, None, [tok])

        def a_exp(n, t_, heads, nk):
            for i, h in enumerate(heads):
                tok = act(prob[n % 2][:, i * nk:(i + 1) * nk], misc[1][:, i * nk:(i + 1) * nk], ACT.Exp,
                          [unit[n], unit.get(("prob_free", n % 2))], bias=row_max[:, n % 2, i:i + 1],
                          accum=row_sum[:, n % 2, i:i + 1])
            misc_free[1] = tok
            unit[n] = tok

        def a_norm(n, t_, heads, nk):
            g = len(heads)
            rs = row_sum[:, n % 2, 0:g]
            tok = vec_do(lambda e: e.reciprocal(rs, rs), [unit[n]])
            for i in range(g):
                pr = prob[n % 2][:, i * nk:(i + 1) * nk]
                last = ts(pr, pr, row_sum[:, n % 2, i:i + 1], None, ALU.mult, None, [tok])
            unit[n] = last

        def a_turn(n, t_, heads, nk):
            for b in range(4):
                dst, src = misc[2][:, b * P:(b + 1) * P], prob[n % 2][:, b * P:(b + 1) * P]
                tok = tensor.put(lambda e, dst=dst, src=src: e.transpose(dst, src, c_of("ident")),
                                 [unit[n], misc_free[2]], b == 3)
            unit["prob_free", n % 2] = tok
            unit[n] = tok

        def a_turned(n, t_, heads, nk):
            tok = act(flat(prob_t[n % 2][:, :, :]), misc[2][:, :], ACT.Copy,
                      [unit[n], unit.get(("prob_t_free", n % 2))])
            misc_free[2] = tok
            unit[n] = tok

        def a_values(n, t_, heads, nk):
            kb = nk // P
            for i, h in enumerate(heads):
                g = h // GROUP
                for b in range(kb):
                    tok = mm(misc[3][:, i * P:(i + 1) * P], v[:, b, g * HD:(g + 1) * HD],
                             prob_t[n % 2][:, i * kb + b, :], b == 0, b == kb - 1, [unit[n], state["v"], misc_free[3]],
                             signal=i == len(heads) - 1 and b == kb - 1)
            unit["prob_t_free", n % 2] = tok
            unit[n] = tok

        def a_out_split(n, t_, heads, nk):
            g, h0 = len(heads), heads[0]
            src = misc[3][:, 0:g * P].rearrange("p (g q) -> p g q", g=g)
            hi, lo = (b_[:, h0:h0 + g, t_ * P:(t_ + 1) * P] for b_ in (o_hi, o_lo))
            t1 = act(hi, src, ACT.Copy, [unit[n], state["scores_done"], state["logits_done"]])
            misc_free[3] = tt(lo, src, as32(hi), ALU.subtract, [t1])
            state["attn"] = misc_free[3]

        def plan_attention(step):
            n = 0
            for t_, per, nk in ((0, 4, P), (1, 2, T)):
                for h in range(0, IDX_HEADS, per):
                    hh = list(range(h, h + per))
                    for d, fn in enumerate((score_dots, score_relu, score_add)):
                        job(step + n + d, lambda fn=fn, n=n, t_=t_, hh=hh, nk=nk: fn(n, t_, hh, nk))
                    n += 1
            step += n + 2

            def scored():
                state["scores_done"] = state["score"]
            job(step, scored)
            for t_, nk in ((0, P), (1, T)):
                for r in range(0, TOPK // 8, 2):
                    job(step, lambda t_=t_, r=r, nk=nk: (topk_round(t_, r, nk), topk_round(t_, r + 1, nk)))
                    step += 1
                job(step - 1, lambda t_=t_, nk=nk: topk_mask(t_, nk))
            units = [(0, list(range(h, h + 4)), P) for h in range(0, HEADS, 4)] + \
                    [(1, list(range(h, h + 2)), T) for h in range(0, HEADS, 2)]
            stages = (a_logits, a_max, a_exp, a_norm, a_turn, a_turned, a_values, a_out_split)
            return units, stages, step

        for c in range(2):
            chunk(w_in, C_QI + c * CHUNK, u2_hi, u2_lo, ready_u2, copy_epilogue(qi, 4 * c, "qi"), KT)
            if c == 0:
                job(len(tiles) - 7, bias_table)
                job(len(tiles) - 3, bias_rev)

                def make_identb():
                    state["identb"] = vec_do(lambda e: e.tensor_copy(ident_b[:, :], c_of("ident")), [t_const])
                job(len(tiles) - 5, make_identb)
        tail_chunk(tail_epilogue)
        score_step = len(tiles)
        for c in range(2):
            chunk(w_in, C_Q + c * CHUNK, u2_hi, u2_lo, ready_u2, copy_epilogue(q, 4 * c, "q", HD ** -0.5), KT)
        kv_chunk()
        kv_end = len(tiles) - 1
        units, stages, attn_step = plan_attention(score_step)
        attn_step = max(attn_step, kv_end) + 1

        order = [units[2], units[3], units[0], units[4], units[5], units[1]]

        n_units = len(order)
        GAP = 3
        for n, (t_, hh, nk) in enumerate(order):
            for d, fn in enumerate(stages):
                def run(fn=fn, n=n, t_=t_, hh=hh, nk=nk):
                    fn(n, t_, hh, nk)
                if fn is not a_out_split:
                    job(attn_step + GAP * n + d, run)
        for n, (t_, hh, nk) in enumerate(order):
            def run_out(n=n, t_=t_, hh=hh, nk=nk):
                state["logits_done"] = unit["logits", n // 3 * 3 + 2]
                a_out_split(n, t_, hh, nk)
            job(attn_step + GAP * n + 7, run_out)
        for n in (2, 5):
            def keep(n=n):
                unit["logits", n] = unit[n]
            jobs[attn_step + GAP * n].append(keep)

        b_ready = {}

        def pool_epilogue(c):
            def go(s):
                got = [tt(pool_u[:, 2 * b:2 * b + 2, :], acc[s][b][:, :, :], both(rstd_u), ALU.mult,
                          [tile_done[-1], state.get("pool_u_free")]) for b in range(2)]
                evacuated(s, got)
                job(state["pool_end"][c] + 1, lambda: pool_group(c, 0, got[0]))
                job(state["pool_end"][c] + 2, lambda: pool_group(c, 1, got[1]))
            return go

        def pool_group(c, g, after):
            gg = 2 * c + g
            w_ = POOL_WINDOWS[gg]
            uu = pool_u[:, 2 * g:2 * g + 2, :]
            t = after
            have = 1
            n = 0
            src = uu
            while have < w_:
                dst = tmp[n % 2][:, :].rearrange("p (k t) -> p k t", k=2)
                vec_do(lambda e, dst=dst, src=src, have=have:
                       e.tensor_copy(dst[:, :, 0:have], src[:, :, 0:have]), [t] + tmp_free[n % 2])
                t = tt(dst[:, :, have:], src[:, :, have:], src[:, :, 0:T - have], ALU.add, [t])
                src = dst
                have *= 2
                n += 1
            ic = cst[:, CST["inv_count"][0] + gg * PAD_POOL:CST["inv_count"][0] + (gg + 1) * PAD_POOL]
            mean = tmp[n % 2][:, :].rearrange("p (k t) -> p k t", k=2)
            for d in range(2):
                t1 = tt(mean[:, d, 0:PAD_POOL], src[:, d, 0:PAD_POOL], ic, ALU.mult, [t] + tmp_free[n % 2])
            t2 = ts(mean[:, :, PAD_POOL:], src[:, :, PAD_POOL:], 1.0 / w_, None, ALU.mult, None, [])
            t3 = tt(mean, mean, uu, ALU.subtract, [t2])
            state["pool_u_free"] = t3
            tmp_free[(n + 1) % 2] = [t3]
            hi, lo = flat(d_hi[:, 2 * g:2 * g + 2, :]), flat(d_lo[:, 2 * g:2 * g + 2, :])
            t4 = split(hi, lo, tmp[n % 2][:, :], [t3, state.get("d_free")])
            tmp_free[n % 2] = [t4]
            state["d", c, g] = t4

        def pool_out_epilogue(c):
            def go(s):
                state["d_free"] = tile_done[-1]
                got = []
                for b in range(2):
                    bb = tmp[b]
                    for d in range(2):
                        kt = 4 * c + 2 * b + d
                        t = act(bb[:, d * T:(d + 1) * T], acc[s][b][:, d, :], ACT.Copy, [tile_done[-1]] + tmp_free[b],
                                scale=v_of("pool_scale", kt))
                    got.append(t)
                    kt = 4 * c + 2 * b
                    t = split(flat(b_hi[:, kt:kt + 2, :]), flat(b_lo[:, kt:kt + 2, :]), bb[:, :], [t])
                    tmp_free[b] = [t]
                    b_ready[kt // 2] = t
                evacuated(s, got)
            return go

        state["pool_end"] = {}
        for c in range(2):
            chunk(w_in, C_POOL + c * CHUNK, u2_hi, u2_lo, ready_u2, pool_epilogue(c), KT)
            state["pool_end"][c] = len(tiles) - 1

            def uconv_epilogue(s, c=c):
                got = [tt(conv_u[:, 2 * b:2 * b + 2, :], acc[s][b][:, :, :], both(rstd_u), ALU.mult,
                          [tile_done[-1], state.get("conv_u_free")]) for b in range(2)]
                evacuated(s, got)
                state["conv_u"] = got[1]
            if c == 0:
                chunk(w_in, C_UCONV, u2_hi, u2_lo, ready_u2, uconv_epilogue, KT)
                block_chunk(pool_w, 0, d_hi, d_lo, lambda kt: [state["d", 0, 0], state["d", 0, 1]],
                            pool_out_epilogue(0))

        def cgate_epilogue(c):
            def go(s):
                got = []
                for b in range(2):
                    z_ = conv_z[:, 2 * b:2 * b + 2, :]
                    got.append(tt(z_, acc[s][b][:, :, :], both(rstd_u), ALU.mult,
                                  [tile_done[-1], state["pool_u_free"]]))
                    t = tt(z_, z_, conv_u[:, 2 * b:2 * b + 2, :], ALU.mult, [got[b], state["conv_u"]])
                evacuated(s, got)
                state["conv_u_free"] = t
                soon(1, lambda: conv2(c, (0, 1), t))
                soon(2, lambda: conv2(c, (2, 3), t))
            return go

        def conv2(c, js, t_z):
            toks = {}
            for back in range(CONV2_W):
                for j in js:
                    w_ = v_of("conv_w", (4 * c + j) * CONV2_W + CONV2_W - 1 - back)
                    if back == 0:
                        toks[j] = ts(conv_y[:, j, :], conv_z[:, j, :], w_, None, ALU.mult, None,
                                     [t_z, state["d_free"]])
                    else:
                        toks[j] = stt(conv_y[:, j, back:], conv_z[:, j, 0:T - back], w_, conv_y[:, j, back:],
                                      ALU.mult, ALU.add, [toks[j]])
            state["conv_y"] = toks[js[-1]]

        def bgate_epilogue(c):
            def go(s):
                got = []
                for b in range(2):
                    bb = tmp[b]
                    got.append(tt(bb[:, :].rearrange("p (k t) -> p k t", k=2), acc[s][b][:, :, :], both(rstd_u),
                                  ALU.mult, [tile_done[-1]] + tmp_free[b]))

                def gated(b):
                    bb = tmp[b]
                    kt = HALF // P + 4 * c + 2 * b
                    t = tt(bb[:, :], bb[:, :], flat(conv_y[:, 2 * b:2 * b + 2, :]), ALU.mult,
                           [got[b], state["conv_y"]])
                    t = split(flat(b_hi[:, kt:kt + 2, :]), flat(b_lo[:, kt:kt + 2, :]), bb[:, :], [t])
                    tmp_free[b] = [t]
                    b_ready[kt // 2] = t
                    mix["y_free"] = t
                soon(1, lambda: gated(0))
                soon(2, lambda: gated(1))
                evacuated(s, got)
            return go

        def uconv1(s):
            got = [tt(conv_u[:, 2 * b:2 * b + 2, :], acc[s][b][:, :, :], both(rstd_u), ALU.mult,
                      [tile_done[-1], state["conv_u_free"]]) for b in range(2)]
            evacuated(s, got)
            state["conv_u"] = got[1]

        mix = {}

        def gate_chunk(n, c):
            def go(s):
                got = [tt(gates[:, 2 * b:2 * b + 2, :], acc[s][b][:, :, :], both(rstd_u), ALU.mult,
                          [tile_done[-1], mix.get("gates_free")]) for b in range(2)]
                evacuated(s, got)

                def sigmoids():
                    for j in range(4):
                        t = act(gates[:, j, :], gates[:, j, :], ACT.Sigmoid, [got[j // 2]],
                                bias=v_of("b_gate", n * KT + 4 * c + j))
                    mix["gates"] = t
                soon(1, sigmoids)
            chunk(w_gate, n * D + c * CHUNK, u2_hi, u2_lo, ready_u2, go, KT)

        def up_chunk(n, c, hi, lo, k0, ready):
            def go(s):
                got = []
                for b in range(2):
                    j = 4 * c + 2 * b
                    g = flat(gates[:, 2 * b:2 * b + 2, :])
                    ys = flat(y[:, j:j + 2, :])
                    if n == 0:
                        got.append(tt(ys, flat(acc[s][b][:, :, :]), g, ALU.mult,
                                      [tile_done[-1], mix["gates"], mix["y_free"]]))
                        continue
                    bb = tmp[b]
                    got.append(tt(bb[:, :], flat(acc[s][b][:, :, :]), g, ALU.mult,
                                  [tile_done[-1], mix["gates"]] + tmp_free[b]))
                    t = tt(ys, ys, bb[:, :], ALU.add, [got[b]])
                    tmp_free[b] = [t]
                    if n == 2:
                        mix["mixed", 2 * c + b] = split(flat(mix_hi[:, j:j + 2, :]), flat(mix_lo[:, j:j + 2, :]),
                                                        ys, [t])
                evacuated(s, got)
                mix["gates_free"] = got[1]
            chunk(w_branch[n], c * CHUNK, hi, lo, ready, go, HALF // P, k0=k0)

        gate_chunk(0, 0)
        block_chunk(pool_w, 2, d_hi, d_lo, lambda kt: [state["d", 1, 0], state["d", 1, 1]], pool_out_epilogue(1))
        for c in range(2):
            if c == 1:
                chunk(w_in, C_UCONV + CHUNK, u2_hi, u2_lo, ready_u2, uconv1, KT)
            chunk(w_in, C_CGATE + c * CHUNK, u2_hi, u2_lo, ready_u2, cgate_epilogue(c), KT)
            chunk(w_in, C_BGATE + c * CHUNK, u2_hi, u2_lo, ready_u2, bgate_epilogue(c), KT)

        def ready_b(kt):
            return [b_ready[kt // 2]]

        sources = [(b_hi, b_lo, 0, ready_b), (b_hi, b_lo, HALF // P, ready_b),
                   (o_hi, o_lo, 0, lambda kt: [state["attn"]])]
        for n in range(3):
            for c in range(4):
                if (n, c) != (0, 0):
                    gate_chunk(n, c)
                up_chunk(n, c, *sources[n][:2], sources[n][2], sources[n][3])
        attn_needed = len(tiles) - 4 * 4 - 3 * 8
        assert attn_step + GAP * n_units + 8 < attn_needed

        def ready_mix(kt):
            return [mix["mixed", kt // 2]]

        for c in range(3):
            chunk(w_out, c * CHUNK, mix_hi, mix_lo, ready_mix, y_epilogue(c), KT)
            if c == 1:
                job(len(tiles) - 1, load_sqrt)
        u3_ready = {}

        def after_out(t_rstd):
            state["rstd_y3"] = t_rstd
            for j in range(2):
                residual3(j)
            for j in range(2, KT // 2):
                soon(j - 1, lambda j=j: residual3(j))
            for j in range(KT // 2):
                soon(8 + j // 2, lambda j=j: add_squares(flat(x[:, 2 * j:2 * j + 2, :]), [u3_ready[j]], j == 0))
            soon(12, lambda: state.__setitem__("sums3", square_sums(all_squares(), [sq["t"]])))
            soon(12, lambda: state.__setitem__("rstd3", rms(rstd_u, [state["sums3"], mix["gates"]])))

        def residual3(j):
            t = residual_pair(j, "gain1", state["rstd_y3"], [state["y"]] if j >= 6 else [])
            u3_ready[j] = gained_split(2 * j, x, "gain2", u3_hi, u3_lo, [t])
        chunk(w_out, 3 * CHUNK, mix_hi, mix_lo, ready_mix, y_last(after_out), KT)

        hid_ready = {}

        def up_epilogue(c, delay):
            def go(s):
                t_tile = tile_done[-1]
                got = []

                def relus():
                    for b in range(2):
                        got.append(stt(tmp[b][:, :].rearrange("p (k t) -> p k t", k=2), acc[s][b][:, :, :], 0.0,
                                       both(rstd_u), ALU.max, ALU.mult, [t_tile, state["rstd3"]] + tmp_free[b]))
                    evacuated(s, got)

                def hidden():
                    for b in range(2):
                        j = 4 * c + 2 * b
                        t = act(tmp[b][:, :], tmp[b][:, :], ACT.Square, [got[b]])
                        state["hid", b] = act(flat(hid_hi[:, j:j + 2, :]), tmp[b][:, :], ACT.Copy, [t])

                def lows():
                    for b in range(2):
                        j = 4 * c + 2 * b
                        t = tt(flat(hid_lo[:, j:j + 2, :]), tmp[b][:, :], as32(flat(hid_hi[:, j:j + 2, :])),
                               ALU.subtract, [state["hid", b]])
                        tmp_free[b] = [t]
                        hid_ready[j // 2] = t
                if delay:
                    soon(delay, relus)
                else:
                    relus()
                soon(delay + 1, hidden)
                soon(delay + 2, lows)
            return go

        def down_epilogue(half, c):
            def go(s):
                if half == 0:
                    got = [y_copy(s, b, c, [tile_done[-1]]) for b in range(2)]
                    evacuated(s, got)
                    mix["half0", c] = got[1]
                    return
                got = []
                for b in range(2):
                    j = 4 * c + 2 * b
                    ys = flat(y[:, j:j + 2, :])
                    got.append(tt(ys, flat(acc[s][b][:, :, :]), ys, ALU.add, [tile_done[-1], mix["half0", c]]))
                    if c < 3:
                        soon(1, lambda b=b, ys=ys: add_squares(ys, [got[b]], c == 0 and b == 0))
                evacuated(s, got)
                if c == 3:
                    finish(got)
            return go

        def finish(got):
            t_sum = square_sums(all_squares(), [sq["t"]], True, False)
            for b in range(2):
                n = 2 + b
                t = act(tmp[n][:, :], flat(y[:, 12 + 2 * b:14 + 2 * b, :]), ACT.Square, [got[b]] + tmp_free[n])
                t_sum = square_sums([tmp[n][:, 0:T], tmp[n][:, T:2 * T]], [t], False, b == 1)
            t_rstd = rms(rstd_y, [t_sum])
            for j in range(KT // 2):
                t = residual_pair(j, "gain3", t_rstd)
                sp_q.put_dma(lambda e, j=j: e.dma_start(out[:, 2 * j:2 * j + 2, :], x[:, 2 * j:2 * j + 2, :]),
                             out_done, [t])
            sp_q.items.append((None, [(out_done[0], out_done[1])], None))

        hidden_kt = MLP // 2 // P
        for half in range(2):
            for c in range(MLP // 2 // CHUNK):
                chunk(w_up, half * (MLP // 2) + c * CHUNK, u3_hi, u3_lo, lambda kt: [u3_ready[kt // 2]],
                      up_epilogue(c, 5 if (half, c) == (0, 0) else 0), KT)
            rows = w_down[half * (MLP // 2):(half + 1) * (MLP // 2), :]
            for c in range(4):
                chunk(rows, c * CHUNK, hid_hi, hid_lo, lambda kt: [hid_ready[kt // 2]],
                      down_epilogue(half, c), hidden_kt)
                if (half, c) == (1, 1):
                    job(len(tiles), load_sqrt)

        for n in range(N_STAGE):
            load_x(n)
            load_tile(n)
        first_gain(0)
        split_tile(0)
        for n in range(1, AHEAD):
            first_gain(n)
            split_tile(n)
        step = 0
        while step < len(tiles) or any(s_ >= step for s_ in jobs):
            if step + AHEAD < len(tiles):
                split_tile(step + AHEAD)
            if step < len(tiles):
                multiply_tile(step)
            now[0] = step
            for fn in jobs.pop(step, []):
                fn()
            step += 1

        block = ctx.enter_context(nc.Block())

        @block.sync
        def _(e):
            sp_q.play(e)

        @block.scalar
        def _(e):
            scalar.play(e)

        @block.vector
        def _(e):
            vector.play(e)

        @block.tensor
        def _(e):
            tensor.play(e)


def kernel(**inputs):
    import numpy as _np
    import concourse.bacc as _bacc
    from concourse import mybir as _mybir
    from concourse.bass_utils import run_bass_kernel_spmd as _run

    get = {k_: _np.asarray(v_) for k_, v_ in inputs.items()}

    def features(a, extra=()):
        a = a.reshape(-1, a.shape[-1] // P, P)
        return _np.ascontiguousarray(a.transpose(2, 1, 0))

    def columns(a):
        return features(a).reshape(P, -1)

    gains = get["norm_gains_2"][0]
    parts = {
        "norm_pre": get["norm_pre"][0], "norm_post": get["norm_post"][0],
        "gain0": gains[0], "gain1": gains[1], "gain2": gains[2], "gain3": gains[3],
        "a_conv_w": get["a_conv_w"][0], "a_conv_b": get["a_conv_b"][0],
        "b_r": get["a_b_r"][0].reshape(-1), "b_i": get["a_b_i"][0].reshape(-1), "lam": get["a_lam"][0],
        "pool_scale": get["pool_scale_2"][0], "conv_w": get["conv_w_2"][0],
    }
    packed = [columns(parts[name]) for name, _ in VEC_SIZES[:-1]]
    packed.append(get["b_gate_2"][0].reshape(3, KT, P).transpose(2, 0, 1).reshape(P, -1))
    cst, ahead, onehot = shape_constants()
    w_in = get["w_in_2"][0]
    tail = _np.concatenate([w_in[:, C_KI:C_WI], w_in[:, C_KI:C_WI], w_in[:, C_WI:]], axis=1)
    arrays = {
        "x": features(get["x"][0]), "p": features(get["p"][0, 0]).reshape(P, -1),
        "vec": _np.concatenate(packed, axis=1), "cst": cst, "ahead": ahead, "onehot": onehot,
        "table": get["rel_bias_2"],
        "ple_proj": get["ple_w_proj"][0], "ple_gate": get["ple_w_gate"][0], "a_in": get["a_w_in"][0],
        "a_r": get["a_w_r"][0], "a_i": get["a_w_i"][0], "a_out": get["a_w_out"][0], "w_in": w_in,
        "w_tail": tail.reshape(KT, P, TAIL).transpose(1, 0, 2), "pool_w": get["pool_w_2"][0],
        "w_branch": get["w_branch_2"][0], "w_gate": get["w_gate_2"][0], "w_out": get["w_out_2"][0],
        "w_up": get["w_up_2"][0], "w_down": get["w_down_2"][0],
    }
    arrays = {f"in_{k_}": _np.ascontiguousarray(v_) for k_, v_ in arrays.items()}
    nc = _bacc.Bacc("TRN2", target_bir_lowering=False, num_devices=1)
    ap = {k_[3:]: nc.dram_tensor(k_, v_.shape, _mybir.dt.from_np(v_.dtype), kind="ExternalInput").ap()
          for k_, v_ in arrays.items()}
    out = nc.dram_tensor("out_dram", (P, KT, T), _mybir.dt.float32, kind="ExternalOutput").ap()
    rev_dram = nc.dram_tensor("rev_dram", (HEADS, REV), _mybir.dt.float32).ap()
    build(nc, ap["x"], ap["p"], ap["vec"], ap["cst"], ap["ahead"], ap["onehot"], ap["table"], rev_dram,
          ap["ple_proj"], ap["ple_gate"], ap["a_in"], ap["a_r"], ap["a_i"], ap["a_out"], ap["w_in"], ap["w_tail"],
          ap["pool_w"], ap["w_branch"], ap["w_gate"], ap["w_out"], ap["w_up"], ap["w_down"], out)
    got = _run(nc, [arrays], core_ids=[0]).results[0]["out_dram"]
    return _np.ascontiguousarray(got.transpose(2, 1, 0)).reshape(1, T, D)
```

```python
from contextlib import ExitStack

import numpy as np

import concourse.bass as bass
from concourse import mybir

F32 = mybir.dt.float32
F32R = mybir.dt.float32r
BF16 = mybir.dt.bfloat16
ALU = mybir.AluOpType
ACT = mybir.ActivationFunctionType
AX_X = mybir.AxisListType.X

P = 128
T = 256
D = 2048
KT = D // P
EPS = 1e-6
CONV_W = 4
LRU_C = 8.0
PLE = 256
POOL_WINDOWS = (2, 4, 8, 16)
PAD_POOL = 16
HALF = D // 2
CONV2_W = 3
HEADS = 8
HD = 128
KV_HEADS = 2
GROUP = HEADS // KV_HEADS
IDX_HEADS = 16
IDX_DIM = 64
TOPK = T // 4
BUCKETS = 32
MAX_EXACT = BUCKETS // 2
MAX_DIST = 128
MLP = 4 * D
TOK_TILES = T // P
REV = P - 1 + T
MASKED = -1e38
TAKEN = -3e38
UNSELECTED = -1e30

WCOLS = 1024
CHUNK = 512
N_STAGE = 4
N_SPLIT = 4
AHEAD = N_SPLIT - 1

C_POOL, C_UCONV, C_CGATE, C_BGATE, C_Q, C_KV, C_QI, C_KI, C_WI = (
    0, 1024, 2048, 3072, 4096, 5120, 5632, 6656, 6720)
TAIL = IDX_DIM + IDX_HEADS

VEC_SIZES = [("norm_pre", KT), ("norm_post", KT), ("gain0", KT), ("gain1", KT), ("gain2", KT),
             ("a_conv_w", KT * CONV_W), ("a_conv_b", KT), ("b_r", KT), ("b_i", KT), ("lam", KT),
             ("pool_scale", HALF // P), ("conv_w", HALF // P * CONV2_W), ("b_gate", 3 * KT)]
VEC = {}
VEC_COLS = 0
for _name, _n in VEC_SIZES:
    VEC[_name] = (VEC_COLS, _n)
    VEC_COLS += _n

CST = {"ident": (0, P), "flip": (P, P), "twice": (2 * P, P), "inv_count": (3 * P, 4 * PAD_POOL),
       "eps": (3 * P + 4 * PAD_POOL, 1)}
CST_COLS = 3 * P + 4 * PAD_POOL + 1


def shape_constants():
    cst = np.zeros((P, CST_COLS), np.float32)
    cst[:, 0:P] = np.eye(P)
    cst[:, P:2 * P] = np.eye(P)[::-1]
    cst[0:IDX_DIM, 2 * P:3 * P] = np.tile(np.eye(IDX_DIM), 2)
    for g, w in enumerate(POOL_WINDOWS):
        at = CST["inv_count"][0] + g * PAD_POOL
        cst[:, at:at + PAD_POOL] = 1.0 / np.minimum(np.arange(PAD_POOL) + 1, w)
    cst[:, CST["eps"][0]] = EPS
    query = np.arange(T).reshape(TOK_TILES, P)
    ahead = np.where(np.arange(T)[None, None, :] > query[:, :, None], MASKED, 0.0)
    ahead = np.ascontiguousarray(ahead.transpose(1, 0, 2)).astype(np.float32)
    dist = np.maximum(T - 1 - np.arange(REV), 0)
    far = MAX_EXACT + (np.log(np.maximum(dist, 1).astype(np.float32) / np.float32(MAX_EXACT))
                       / np.float32(np.log(MAX_DIST / MAX_EXACT)) * (BUCKETS - MAX_EXACT)).astype(np.int32)
    bucket = np.where(dist < MAX_EXACT, dist, np.minimum(far, BUCKETS - 1))
    onehot = (np.arange(BUCKETS)[:, None] == bucket[None, :]).astype(np.float32)
    return cst, ahead, onehot


class Queue:

    def __init__(self, done):
        self.items = []
        self.done = done
        self.count = 0

    def put(self, make, after=(), signal=True):
        if signal:
            self.count += 1
        self.items.append((make, [t for t in after if t is not None], (self.done, 1) if signal else None))
        return (self.done, self.count) if signal else None

    def put_dma(self, make, sem, after=()):
        sem[1] += 16
        self.items.append((make, [t for t in after if t is not None], (sem[0], 16)))
        return (sem[0], sem[1])

    def play(self, engine):
        seen = {}
        for make, after, inc in self.items:
            for sem, value in after:
                if seen.get(sem.name, 0) < value:
                    engine.wait_ge(sem, value)
                    seen[sem.name] = value
            if make is None:
                continue
            ins = make(engine)
            if inc:
                ins.then_inc(inc[0], inc[1])


class Tile:

    def __init__(self, src, ks, cols, products, needs):
        self.src = src
        self.ks = ks
        self.cols = cols
        self.products = products
        self.needs = needs


def build(nc, x_in, p_in, vec_in, cst_in, ahead_in, onehot_in, table_in, rev_dram,
          ple_proj, ple_gate, a_in, a_r, a_i, a_out, w_in, w_tail, pool_w, w_branch, w_gate, w_out, w_up, w_down,
          gain3_in, out):
    with ExitStack() as ctx:
        def sem(name):
            return ctx.enter_context(nc.semaphore(name))

        cursor = [(nc.sbuf_base + 63) // 64 * 64]

        def at(name, shape, dt, offset):
            return nc.alloc_sbuf_tensor_at(name, shape, dt, offset=offset)

        def fixed(name, shape, dt=F32):
            size = int(np.prod(shape[1:])) * (2 if dt == BF16 else 4)
            t = at(name, shape, dt, cursor[0])
            cursor[0] += (size + 63) // 64 * 64
            return t

        x = fixed("x", [P, KT, T])
        y_base = cursor[0]
        y = fixed("y", [P, KT, T])
        stage = fixed("stage", [P, N_STAGE, WCOLS])
        w_hi = fixed("w_hi", [P, N_SPLIT, WCOLS], F32R)
        w_lo = fixed("w_lo", [P, N_SPLIT, WCOLS], F32R)
        vec = fixed("vec", [P, VEC_COLS])
        cst = fixed("cst", [P, CST_COLS])
        ones = fixed("ones", [P, P])
        ident_b = fixed("ident_b", [P, P], BF16)
        tmp = [fixed(f"tmp{i}", [P, 2 * T]) for i in range(4)]
        rstd_u = fixed("rstd_u", [P, T])
        rstd_col = fixed("rstd_col", [P, TOK_TILES])
        chunk_sums = fixed("chunk_sums", [P, D // CHUNK, TOK_TILES])
        rstd_diag = fixed("rstd_diag", [P, TOK_TILES, P])
        squares = fixed("squares", [P, 2 * T])
        sp = fixed("sp", [P, 4, KT])
        wi = fixed("wi", [P, TOK_TILES, IDX_HEADS])
        top8 = fixed("top8", [P, 8])
        row_max = fixed("row_max", [P, 2, GROUP])
        row_sum = fixed("row_sum", [P, 2, GROUP])
        dummy = fixed("dummy", [P, 1])
        SPLIT_ACT = 2 * KT * T * 4
        region_a = cursor[0]
        region_b = region_a + SPLIT_ACT
        region_c = region_b + SPLIT_ACT

        def pair(name, kts, offset, offset_lo=None):
            lo_at = offset + kts * T * 4 if offset_lo is None else offset_lo
            return at(name + "_hi", [P, kts, T], F32R, offset), at(name + "_lo", [P, kts, T], F32R, lo_at)

        u1_hi, u1_lo = pair("u1", KT, region_a)
        g_hi, g_lo = pair("g", KT, region_b)
        h_hi, h_lo = pair("h", KT, region_a)
        u2_hi, u2_lo = pair("u2", KT, region_b)
        b_hi, b_lo = pair("b", 2 * HALF // P, region_a)
        mix_hi, mix_lo = pair("mix", KT, region_a)
        u3_hi, u3_lo = pair("u3", KT, region_b)
        hid_hi, hid_lo = pair("hid", MLP // 2 // P, region_a, region_c)

        hs = at("hs", [P, KT, T], F32, region_c)
        pp = at("pp", [P, KT, T], F32, region_c)
        o = region_c + 16384
        xb = at("xb", [P, 4, T + CONV_W - 1], F32, o)
        p32 = at("p32", [P, 2 * T], F32, o)
        p_hi, p_lo = pair("p", 2, o + 2048)
        o += 4160
        xc = at("xc", [P, 4, T], F32, o + 2048)
        xc_hi, xc_lo = pair("xc", 4, o + 6144)
        t_buf = at("t_buf", [P, 4, T], F32, o + 6144)
        r_buf = at("r_buf", [P, 4, T], F32, o + 14336)
        i_buf = at("i_buf", [P, 4, T], F32, o + 18432)
        a_buf = at("a_buf", [P, 4, T], F32, o + 22528)
        o_hi, o_lo = pair("o", HEADS, region_c)
        bias = at("bias", [P, HEADS, T], F32, region_c)
        qi = at("qi", [P, IDX_HEADS // 2, T], F32, region_c + 8192)
        q = at("q", [P, HEADS, T], F32, region_c + 16384)
        o = region_c + 24576
        k = at("k", [P, KV_HEADS, T], F32, o)
        v = at("v", [P, TOK_TILES, KV_HEADS * HD], F32, o + 2048)
        ki = at("ki", [P, T], F32, o + 4096)
        o += 5120
        score = at("score", [P, TOK_TILES, T], F32, o)
        left = at("left", [P, T], F32, o + 2048)
        mask = at("mask", [P, TOK_TILES, T], BF16, o + 3072)
        ahead = at("ahead", [P, TOK_TILES, T], F32, o + 4096)
        prob_t = [at(f"prob_t{i}", [P, 4, P], F32, o + 6144 + 2048 * i) for i in range(2)]
        prob = [at(f"prob{i}", [P, 2 * T], F32, o + 10240 + 2048 * i) for i in range(2)]
        relu = [at(f"relu{i}", [P, 2 * T], F32, o + 10240 + 2048 * i) for i in range(2)]
        onehot = at("onehot", [BUCKETS, REV], F32, o + 6144)
        rev = at("rev", [HEADS, REV], F32, o + 7680)
        table = at("table", [BUCKETS, HEADS], F32, o + 9216)
        gates = at("gates", [P, 4, T], F32, o + 14336)
        gain3_row = at("gain3_row", [P, D], F32, region_c + MLP // 2 // P * T * 4)
        pool_u = at("pool_u", [P, 4, T], F32, y_base)
        conv_z = at("conv_z", [P, 4, T], F32, y_base)
        d_lo = at("d_lo", [P, 4, T], F32R, y_base + 4096)
        conv_y = at("conv_y", [P, 4, T], F32, y_base + 4096)
        conv_u = at("conv_u", [P, 4, T], F32, y_base + 8192)
        d_hi = at("d_hi", [P, 4, T], F32R, y_base + 12288)

        acc = [[ctx.enter_context(nc.psum_tensor(f"acc{s}{b}", [P, 2, T], F32)) for b in range(2)] for s in range(2)]
        misc = [ctx.enter_context(nc.psum_tensor(f"misc{i}", [P, 2 * T], F32)) for i in range(4)]
        acc.append([misc[n][:, :].rearrange("p (k t) -> p k t", k=2) for n in (2, 3)])

        sp_q = Queue(None)
        scalar = Queue(sem("scalar_done"))
        vector = Queue(sem("vector_done"))
        tensor = Queue(sem("tensor_done"))
        stage_in = [[sem(f"stage_in{i}"), 0] for i in range(N_STAGE)]
        second_half_in = [sem("second_half_in"), 0]
        vec_loaded = [sem("vec_loaded"), 0]
        cst_loaded = [sem("cst_loaded"), 0]
        x_in_sem = [[sem(f"x_in{i}"), 0] for i in range(KT // 2)]
        late_in = [sem("late_in"), 0]
        rev_out = [sem("rev_out"), 0]
        bias_in = [sem("bias_in"), 0]
        out_done = [sem("out_done"), 0]

        def act(out, in_, func, after=(), bias=None, scale=None, accum=None):
            kw = {}
            if bias is not None:
                kw["bias"] = bias
            if scale is not None:
                kw["scale"] = scale
            if accum is not None:
                kw["accum_out"] = accum
            return scalar.put(lambda e: e.activation(out, in_, func, **kw), after)

        def tt(out, a, b, op, after=()):
            return vector.put(lambda e: e.tensor_tensor(out, a, b, op), after)

        def ts(out, a, s1, s2, op0, op1, after=()):
            if s2 is None:
                return vector.put(lambda e: e.tensor_scalar(out, a, s1, None, op0), after)
            return vector.put(lambda e: e.tensor_scalar(out, a, s1, s2, op0, op1), after)

        def stt(out, a, s, b, op0, op1, after=()):
            return vector.put(lambda e: e.scalar_tensor_tensor(out=out, in0=a, scalar=s, in1=b, op0=op0, op1=op1), after)

        def vec_do(make, after=()):
            return vector.put(make, after)

        def mm(out, lhs, rhs, start, stop, after=(), signal=False):
            return tensor.put(lambda e: e.matmul(out, lhs, rhs, start=start, stop=stop, skip_group_check=True),
                              after, signal)

        def v_of(name, i):
            return vec[:, VEC[name][0] + i:VEC[name][0] + i + 1]

        def c_of(name):
            return cst[:, CST[name][0]:CST[name][0] + CST[name][1]]

        def as32(ap):
            return ap.bitcast(F32)

        def split(hi, lo, src, after=()):
            t_hi = act(hi, src, ACT.Copy, after)
            return tt(lo, src, as32(hi), ALU.subtract, [t_hi])

        def split_later(hi, lo, src, after, then):
            t_hi = act(hi, src, ACT.Copy, after)
            soon(1, lambda: then(tt(lo, src, as32(hi), ALU.subtract, [t_hi])))

        tiles = []
        jobs = {}
        tile_done = []
        split_done = {}
        first_half_split = {}
        half_done = [None]

        now = [0]

        def soon(delay, fn):
            if delay == 0:
                fn()
            else:
                job(now[0] + delay, fn)

        def job(step, fn):
            jobs.setdefault(step, []).append(fn)

        def load_tile(n):
            slot = n % N_STAGE
            before = [split_done[n - N_STAGE]] if n >= N_STAGE else []
            ks, cols, src = tiles[n].ks, tiles[n].cols, tiles[n].src
            halves = [slice(0, ks // 2), slice(ks // 2, ks)] if n == 0 else [slice(0, ks)]
            dst = stage[:, slot, 0:cols].rearrange("p (k n) -> p k n", k=ks)
            tiles[n].landed = []
            for i, half in enumerate(halves):
                tiles[n].landed.append(sp_q.put_dma(lambda e, half=half: e.dma_start(dst[:, half, :], src[:, half, :]),
                                                    stage_in[slot] if i == 0 else second_half_in, before))

        def split_tile(n):
            slot, buf, cols = n % N_STAGE, n % N_SPLIT, tiles[n].cols
            free = [tile_done[n - N_SPLIT]] if n >= N_SPLIT else []
            halves = [(0, cols // 2), (cols // 2, cols)] if n == 0 else [(0, cols)]
            for landed, (a, b) in zip(tiles[n].landed, halves):
                src = stage[:, slot, a:b]
                hi = w_hi[:, buf, a:b]
                t_hi = act(hi, src, ACT.Copy, [landed] + free)
                split_done[n] = tt(w_lo[:, buf, a:b], src, as32(hi), ALU.subtract, [t_hi])
                first_half_split.setdefault(n, split_done[n])
            if n + N_STAGE < len(tiles):
                load_tile(n + N_STAGE)

        def multiply_tile(n):
            buf = n % N_SPLIT
            tile = tiles[n]
            products = tile.products(w_hi[:, buf, :], w_lo[:, buf, :])
            half = len(products) // 2
            for i, (out_, lhs, rhs, start, stop) in enumerate(products):
                after = []
                if i == 0:
                    after = [first_half_split[n]] + tile.needs(0)
                elif i == half:
                    after = [split_done[n]] + tile.needs(1)
                if i == half - 1:
                    half_done[0] = mm(out_, lhs, rhs, start, stop, after, signal=True)
                else:
                    token = mm(out_, lhs, rhs, start, stop, after, signal=i == len(products) - 1)
            tile_done.append(token)

        bank_free = [[], [], []]
        chunk_no = [0]

        def chunk_tiles(s, w, c0, act_hi, act_lo, ready, kts, k0=0):
            got_tiles = []
            per = WCOLS // CHUNK
            for i in range(0, kts, per):
                src = w[i * P:(i + per) * P, c0:c0 + CHUNK].rearrange("(k p) n -> p k n", p=P)

                def products(hi, lo, i=i):
                    got = []
                    order = [(dk, j) for dk in range(per) for j in range(CHUNK // P)]
                    if i + per == kts:
                        order.sort(key=lambda o: o[1])
                    for dk, j in order:
                        kt = i + dk
                        c = dk * CHUNK + j * P
                        o_ = acc[s][j // 2][:, j % 2, :]
                        wh, wl = hi[:, c:c + P], lo[:, c:c + P]
                        xh, xl = act_hi[:, k0 + kt, :], act_lo[:, k0 + kt, :]
                        got += [(o_, wh, xh, kt == 0 and j % 2 == 0, False), (o_, wh, xl, False, False),
                                (o_, wl, xh, False, kt == kts - 1)]
                    return got

                def needs(half, i=i):
                    free = bank_free[s] + (misc_free[2:4] if s == 2 else [])
                    return (free if i == half == 0 else []) + \
                        [t for dk in range(per) if i + per == kts or dk == half for t in ready(k0 + i + dk)]

                got_tiles.append(Tile(src, per, WCOLS, products, needs))
            return got_tiles

        def chunk(w, c0, act_hi, act_lo, ready, epilogue, kts, k0=0, s=None, delay=0):
            if s is None:
                s = chunk_no[0] % 2
                chunk_no[0] += 1
            tiles.extend(chunk_tiles(s, w, c0, act_hi, act_lo, ready, kts, k0))
            job(len(tiles) - 1 + delay, lambda: epilogue(s))

        def chunk_pair(first, second, between=None, delay=0):
            sets = (chunk_no[0] % 2, (chunk_no[0] + 1) % 2)
            chunk_no[0] += 2
            a, b = (chunk_tiles(s, *q_[:5], q_[6]) for s, q_ in zip(sets, (first, second)))
            for n, tile in enumerate(t_ for pair_ in zip(a, b) for t_ in pair_):
                if between and n == between[0]:
                    between[1]()
                tiles.append(tile)
            job(len(tiles) - 2 + delay, lambda: first[5](sets[0]))
            job(len(tiles) - 1 + delay, lambda: second[5](sets[1]))

        def block_tile(w, n0, banks, act_hi, act_lo, needs, epilogue):
            src = w[n0:n0 + 2].rearrange("b (k p) d -> p (b k) d", p=P)

            def products(hi, lo):
                got = []
                for b in range(2):
                    for e in range(2):
                        for kk in range(2):
                            kt = 2 * b + kk
                            c = kt * 256 + e * P
                            o_ = banks[b][:, e, :]
                            wh, wl = hi[:, c:c + P], lo[:, c:c + P]
                            got += [(o_, wh, act_hi[:, kt, :], kk == 0 and e == 0, False),
                                    (o_, wh, act_lo[:, kt, :], False, False),
                                    (o_, wl, act_hi[:, kt, :], False, kk == 1)]
                return got

            tiles.append(Tile(src, 4, WCOLS, products, needs))
            job(len(tiles) - 1, epilogue)

        def evacuated(s, tokens):
            bank_free[s] = list(tokens)
            if s == 2:
                misc_free[2] = misc_free[3] = tokens[-1]

        norm = {}
        misc_free = [None] * 4
        tmp_free = [[] for _ in range(4)]

        def flat(ap):
            return ap.rearrange("p k t -> p (k t)")

        def both(rstd):
            return rstd[:, :].unsqueeze(1).broadcast_to([P, 2, T])

        def square_sums(bank, parts, after, first=True, last=True):
            todo = [(part, t_) for part in parts for t_ in range(TOK_TILES)]
            for i, (part, t_) in enumerate(todo):
                t = mm(misc[bank][:, T + t_:T + t_ + 1], part[:, t_ * P:(t_ + 1) * P], ones[:, 0:1],
                       first and i == 0, last and i >= len(todo) - TOK_TILES, list(after) + [misc_free[bank]],
                       signal=i == len(todo) - 1)
            return t

        def rms_columns(bank, after):
            t = act(rstd_col[:, :], misc[bank][:, T:T + TOK_TILES], ACT.Sqrt, after, bias=c_of("eps"), scale=1.0 / D)
            t = vec_do(lambda e: e.reciprocal(rstd_col[:, :], rstd_col[:, :]), [t])
            return tt(rstd_diag[:, :, :], c_of("ident").unsqueeze(1).broadcast_to([P, TOK_TILES, P]),
                      rstd_col[:, :].unsqueeze(2).broadcast_to([P, TOK_TILES, P]), ALU.mult, [t])

        def rms_row(bank, after):
            return mm(misc[bank][:, 0:T], ones[:, :], flat(rstd_diag[:, :, :]), True, True, after, signal=True)

        def plan_rms_u(key, sums, readers):
            def columns():
                state["diag"] = rms_columns(0, [state["sums"]])

            def row():
                t = rms_row(0, [state["diag"]])
                state[key] = misc_free[0] = act(rstd_u[:, :], misc[0][:, 0:T], ACT.Copy, [t] + readers())

            def summed():
                state["sums"] = sums()
            summed()
            soon(1, columns)
            soon(2, row)

        def load_sqrt():
            act(dummy[:, :], c_of("eps"), ACT.Sqrt, [(cst_loaded[0], 16)])

        def gained_split(kt, gain, hi, lo, after, ready, delay):
            got = [act(hi[:, kt + d, :], x[:, kt + d, :], ACT.Copy, after, scale=v_of(gain, kt + d)) for d in range(2)]

            def lows():
                for d in range(2):
                    ready[kt + d] = stt(lo[:, kt + d, :], x[:, kt + d, :], v_of(gain, kt + d),
                                        as32(hi[:, kt + d, :]), ALU.mult, ALU.subtract, [got[d]])
            soon(delay, lows)

        def load_x(j):
            sp_q.put_dma(lambda e: e.dma_start(x[:, 2 * j:2 * j + 2, :], x_in[:, 2 * j:2 * j + 2, :]), x_in_sem[j])
        t_vec = scalar.put_dma(lambda e: e.dma_start(vec[:, :], vec_in), vec_loaded)
        t_ones = vec_do(lambda e: e.memset(ones[:, :], 1.0))
        act(dummy[:, :], ones[:, 0:1], ACT.Copy, [t_ones])
        t_xb_pad = vec_do(lambda e: e.memset(xb[:, :, 0:CONV_W - 1], 0.0))

        def softplus(step):
            lam = vec[:, VEC["lam"][0]:VEC["lam"][0] + KT]
            e_, z_, z2_, s_ = (sp[:, i, :] for i in range(4))

            def argument():
                t = act(e_, lam, ACT.Abs, [t_vec])
                t = act(e_, e_, ACT.Exp, [t], scale=-1.0)
                t = ts(z_, e_, 2.0, None, ALU.add, None, [t])
                t = vec_do(lambda e: e.reciprocal(z2_, z_), [t])
                t = tt(z_, z2_, e_, ALU.mult, [t])
                tt(z2_, z_, z_, ALU.mult, [t])
                state["series"] = vec_do(lambda e: e.memset(s_, 1.0 / 17), [])

            def term(odd):
                t = tt(s_, s_, z2_, ALU.mult, [state["series"]])
                state["series"] = ts(s_, s_, 1.0 / odd, None, ALU.add, None, [t])

            def result():
                t = tt(s_, s_, z_, ALU.mult, [state["series"]])
                t = ts(e_, lam, -1.0, 0.0, ALU.mult, ALU.max, [t])
                t = stt(z_, s_, 2.0, e_, ALU.mult, ALU.add, [t])
                t = ts(decay, z_, LRU_C, None, ALU.mult, None, [t])
                state["decay"] = ts(neg_decay, z_, -LRU_C, None, ALU.mult, None, [t])
            job(step, argument)
            odds = range(15, 0, -2)
            for n, odd in enumerate(odds):
                job(step + 1 + n, lambda odd=odd: term(odd))
            job(step + 1 + len(odds), result)

        decay, neg_decay = sp[:, 2, :], sp[:, 3, :]

        u1_ready = {}
        state = {}
        sq = {"t": None, "n": 2}

        def ready_u(kt):
            return [u1_ready[kt]]

        def first_gain(j):
            gained_split(2 * j, "norm_pre", u1_hi, u1_lo, [(x_in_sem[j][0], 16), t_vec], u1_ready, 0)

        def first_squares(j):
            b = tmp[j % 4]
            t = act(b[:, :], flat(x[:, 2 * j:2 * j + 2, :]), ACT.Square, [(x_in_sem[j][0], 16)] + tmp_free[j % 4])
            if j == 0:
                sq["t"] = vec_do(lambda e: e.tensor_copy(squares[:, :], b[:, :]), [t])
            else:
                sq["t"] = tt(squares[:, :], squares[:, :], b[:, :], ALU.add, [t, sq["t"]])
            tmp_free[j % 4] = [sq["t"]]

        def first_rms():
            plan_rms_u("rstd0", lambda: square_sums(0, all_squares(), [sq["t"], t_ones, (cst_loaded[0], 16)]), list)
        for j in range((AHEAD + 1) // 2, KT // 2):
            job(2 * j - AHEAD, lambda j=j: first_gain(j))
        for j in range(KT // 2):
            job(j + 3, lambda j=j: first_squares(j))
        job(11, first_rms)
        softplus(16)

        xc_ready, h_ready, xb_free = {}, {}, {}

        def xb_epilogue(c):
            def go(s):
                got = [tt(xb[:, 2 * b:2 * b + 2, CONV_W - 1:], acc[s][b][:, :, :], both(rstd_u), ALU.mult,
                          [tile_done[-1], state["rstd0"], t_xb_pad] + xb_free.get(c - 1, [])) for b in range(2)]
                evacuated(s, got)
                state["xb", c] = got
                if c == 0:
                    plan_conv(0, 1)
            return go

        def plan_conv(c, delay):
            for n in range(4):
                js, taps = ((0, 1), (2, 3))[n // 2], ((0, 1), (2, 3))[n % 2]
                soon(delay + n, lambda js=js, taps=taps: conv(c, js, taps))

            def conv_split():
                xc_ready[c] = split(flat(xc_hi[:, :, :]), flat(xc_lo[:, :, :]), flat(xc[:, :, :]),
                                    xb_free[c] + [state.get("xc_read"), state.get("t_buf_free")])
            soon(delay + 4, conv_split)

        def conv(c, js, taps):
            for i in taps:
                for j in js:
                    kt = 4 * c + j
                    w_ = v_of("a_conv_w", kt * CONV_W + i)
                    if i == 0:
                        state["conv", j] = act(xc[:, j, :], xb[:, j, 0:T], ACT.Identity,
                                               [state["xb", c][j // 2], state.get("xc_free")],
                                               bias=v_of("a_conv_b", kt), scale=w_)
                    else:
                        state["conv", j] = stt(xc[:, j, :], xb[:, j, i:i + T], w_, xc[:, j, :], ALU.mult, ALU.add,
                                               [state["conv", j]])
            xb_free[c] = [state["conv", js[-1]]]

        def recurrence_gate(buf, w, name, key, n, c):
            def go():
                got = [act(buf[:, j, :], banks[j // 2][:, j % 2, :], ACT.Sigmoid,
                           [tile_done[-1]] + h_ready.get(c - 1, []), bias=v_of(name, 4 * c + j)) for j in range(4)]
                misc_free[n] = misc_free[n + 1] = got[3]
                state[key] = got[3]
                if key == "i":
                    state["xc_read"] = tile_done[-1]
                    plan_scan(c)
            banks = [misc[n + b][:, :].rearrange("p (k t) -> p k t", k=2) for b in range(2)]
            block_tile(w, 2 * c, banks, xc_hi, xc_lo, lambda half: [xc_ready[c], misc_free[n], misc_free[n + 1]], go)

        def plan_scan(c):
            def decays():
                for j in range(4):
                    act(a_buf[:, j, :], r_buf[:, j, :], ACT.Exp, [state["r"], state["decay"]],
                        scale=neg_decay[:, 4 * c + j:4 * c + j + 1])

            def tanhs():
                for j in range(4):
                    state["a"] = act(t_buf[:, j, :], r_buf[:, j, :], ACT.Tanh, [state["xc_read"]],
                                     scale=decay[:, 4 * c + j:4 * c + j + 1])

            def ones_less_squares():
                r_, a_, t_ = (flat(b_[:, :, :]) for b_ in (r_buf, a_buf, t_buf))
                t = tt(r_, a_, a_, ALU.mult, [state["a"]])
                state["m"] = stt(r_, r_, 1.0, t_, ALU.add, ALU.mult, [t])

            def inputs():
                state["xc_free"] = tt(flat(i_buf[:, :, :]), flat(i_buf[:, :, :]), flat(xc[:, :, :]), ALU.mult,
                                      [state["i"]])
                state["root"] = act(flat(t_buf[:, :, :]), flat(r_buf[:, :, :]), ACT.Sqrt, [state["m"]])

            def scans():
                t = tt(flat(i_buf[:, :, :]), flat(i_buf[:, :, :]), flat(t_buf[:, :, :]), ALU.mult,
                       [state["root"], state["xc_free"]])
                state["t_buf_free"] = t
                for j in range(4):
                    t_h = vec_do(lambda e, j=j: e.tensor_tensor_scan(hs[:, 4 * c + j, :], a_buf[:, j, :],
                                                                     i_buf[:, j, :], 0.0, ALU.mult, ALU.add), [t])
                h_ready[c] = [t_h]

            for n, fn in enumerate((decays, tanhs, ones_less_squares, inputs, scans)):
                soon(n + 1, fn)
            if c < 3:
                plan_conv(c + 1, 6)
            for b in range(2):
                soon((11 if c < 3 else 6) + b, lambda b=b: gated(2 * c + b))

        y_ready = {}

        def gate_epilogue(c):
            def go(s):
                ys = [y[:, 4 * c + 2 * b:4 * c + 2 * b + 2, :] for b in range(2)]
                got = [tt(ys[b], acc[s][b][:, :, :], both(rstd_u), ALU.mult, [tile_done[-1], state["rstd0"]])
                       for b in range(2)]
                evacuated(s, got)
                state["rstd_u_read"] = got[1]

                def silus():
                    state["silu", c] = act(y[:, 4 * c:4 * c + 4, :], y[:, 4 * c:4 * c + 4, :], ACT.Silu, [got[1]])
                soon(1, silus)
            return go

        def gated(n):
            j, b = 2 * n, 2 + n % 2
            t = tt(tmp[b][:, :], flat(hs[:, j:j + 2, :]), flat(y[:, j:j + 2, :]), ALU.mult,
                   [state["silu", n // 2]] + h_ready[n // 2] + tmp_free[b])

            def done(t):
                tmp_free[b] = [t]
                y_ready[n] = t
            split_later(flat(g_hi[:, j:j + 2, :]), flat(g_lo[:, j:j + 2, :]), tmp[b][:, :], [t], done)

        def xb_chunk(c):
            chunk(a_in, c * CHUNK, u1_hi, u1_lo, ready_u, xb_epilogue(c), KT)

        def ri_chunk(c):
            recurrence_gate(r_buf, a_r, "b_r", "r", 0, c)
            recurrence_gate(i_buf, a_i, "b_i", "i", 2, c)

        def g_chunk(c):
            chunk(a_in, D + c * CHUNK, u1_hi, u1_lo, ready_u, gate_epilogue(c), KT)

        chunk_pair((a_in, 0, u1_hi, u1_lo, ready_u, xb_epilogue(0), KT),
                   (a_in, D, u1_hi, u1_lo, ready_u, gate_epilogue(0), KT))
        for c in range(1, 4):
            xb_chunk(c)
            ri_chunk(c - 1)
            g_chunk(c)

        def add_squares(src, after, first):
            n = sq["n"] = 5 - sq["n"]
            t = act(tmp[n][:, :], src, ACT.Square, list(after) + tmp_free[n])
            if first:
                sq["t"] = vec_do(lambda e: e.tensor_copy(squares[:, :], tmp[n][:, :]), [t, sq["t"]])
            else:
                sq["t"] = tt(squares[:, :], squares[:, :], tmp[n][:, :], ALU.add, [t, sq["t"]])
            tmp_free[n] = [sq["t"]]
            return t

        def all_squares():
            return [squares[:, 0:T], squares[:, T:2 * T]]

        def y_gained(s, b, c, gain, after):
            for d in range(2):
                kt = 4 * c + 2 * b + d
                t = act(y[:, kt, :], acc[s][b][:, d, :], ACT.Copy, after, scale=v_of(gain, kt))
            return t

        def y_epilogue(c, gain):
            def go(s):
                got = []
                for b in range(2):
                    y_gained(s, b, c, gain, [tile_done[-1], y_ready.get(KT // 2 - 1)])
                    got.append(add_squares(flat(acc[s][b][:, :, :]), [], c == 0 and b == 0))
                evacuated(s, got)
            return go

        def y_last(gain, then):
            def go(s):
                t_banks = [half_done[0], tile_done[-1]]
                t_sum = square_sums(1, all_squares(), [sq["t"]], True, False)
                for b in range(2):
                    n = 2 + b
                    t = act(tmp[n][:, :], flat(acc[s][b][:, :, :]), ACT.Square, [t_banks[b]] + tmp_free[n])
                    t_sum = square_sums(1, [tmp[n][:, 0:T], tmp[n][:, T:2 * T]], [t], False, b == 1)
                    tmp_free[n] = [t_sum]
                sq["t"] = t_sum
                t_rstd = rms_row(1, [rms_columns(1, [t_sum])])
                got = [y_gained(s, b, 3, gain, []) for b in range(2)]
                state["y"] = got[1]
                evacuated(s, got)
                then(t_rstd)
            return go

        def residual_pair(j, t_rstd, after=()):
            b = tmp[j % 2]
            row = misc[1][:, 0:T].unsqueeze(1).broadcast_to([P, 2, T])
            t = tt(b[:, :].rearrange("p (k t) -> p k t", k=2), y[:, 2 * j:2 * j + 2, :], row, ALU.mult,
                   [t_rstd] + list(after) + tmp_free[j % 2])
            misc_free[1] = t
            t = tt(flat(x[:, 2 * j:2 * j + 2, :]), flat(x[:, 2 * j:2 * j + 2, :]), b[:, :], ALU.add, [t])
            tmp_free[j % 2] = [t]
            return t

        def ready_g(kt):
            return [y_ready[kt // 2]]

        def load_p():
            state["p32"] = scalar.put_dma(lambda e: e.dma_start(p32[:, :], p_in), p_in_sem, [tile_done[-1], y_ready[7]])

        def split_p():
            state["p"] = split(flat(p_hi[:, :, :]), flat(p_lo[:, :, :]), p32[:, :], [state["p32"]])
        chunk_pair((a_out, 0, g_hi, g_lo, ready_g, y_epilogue(0, "norm_post"), KT),
                   (a_out, CHUNK, g_hi, g_lo, ready_g, y_epilogue(1, "norm_post"), KT),
                   (3, lambda: ri_chunk(3)))
        job(len(tiles), load_p)
        job(len(tiles) + 3, split_p)
        job(len(tiles) + 4, load_sqrt)
        chunk(a_out, 2 * CHUNK, g_hi, g_lo, ready_g, y_epilogue(2, "norm_post"), KT)
        p_in_sem = [sem("p_in"), 0]

        pp_ready = {}
        h_split = {}

        def after_a_out(t_rstd):
            state["rstd1"] = t_rstd
            for j in range(KT // 2):
                soon(2 * j, lambda j=j: residual1(j))
        chunk(a_out, 3 * CHUNK, g_hi, g_lo, ready_g, y_last("norm_post", after_a_out), KT)

        def pp_epilogue(c):
            def go(s):
                got = [act(flat(pp[:, 4 * c + 2 * b:4 * c + 2 * b + 2, :]), flat(acc[s][b][:, :, :]), ACT.Copy,
                           [tile_done[-1]]) for b in range(2)]
                evacuated(s, got)
                pp_ready[c] = got[1]
            return go

        def residual1(j):
            t = residual_pair(j, state["rstd1"], [state["y"]] if j >= 6 else [])
            h_split[j] = split(flat(h_hi[:, 2 * j:2 * j + 2, :]), flat(h_lo[:, 2 * j:2 * j + 2, :]),
                               flat(x[:, 2 * j:2 * j + 2, :]), [t])
        for c in range(4):
            chunk(ple_proj, c * CHUNK, p_hi, p_lo, lambda kt: [state["p"]], pp_epilogue(c), PLE // P)

        def ready_h(kt):
            return [h_split[kt // 2]]

        u2_ready = {}

        def ple_epilogue(c):
            def go(s):
                gs = [flat(y[:, 4 * c + 2 * b:4 * c + 2 * b + 2, :]) for b in range(2)]
                got = [act(gs[b], flat(acc[s][b][:, :, :]), ACT.Sigmoid, [tile_done[-1], h_split[KT // 2 - 1]])
                       for b in range(2)]
                evacuated(s, got)

                def finish_x(b):
                    j = 4 * c + 2 * b
                    xs = flat(x[:, j:j + 2, :])
                    t = tt(gs[b], gs[b], flat(pp[:, j:j + 2, :]), ALU.mult, [got[b], pp_ready[c]])
                    t = tt(xs, xs, gs[b], ALU.add, [t])
                    state["x", b] = t

                def split_x(b):
                    j = 4 * c + 2 * b
                    gained_split(j, "gain0", u2_hi, u2_lo, [state["x", b]], u2_ready, 1)

                def square_x(b):
                    j = 4 * c + 2 * b
                    add_squares(flat(x[:, j:j + 2, :]), [state["x", b]], c == 0 and b == 0)
                for n, (fn, b) in enumerate(((finish_x, 0), (finish_x, 1), (split_x, 0), (split_x, 1), (square_x, 0),
                                             (square_x, 1))):
                    soon(n + 1, lambda fn=fn, b=b: fn(b))
                if c == 3:
                    soon(7, norm2)
            return go

        def norm2():
            plan_rms_u("rstd2", lambda: square_sums(0, all_squares(), [sq["t"]]), lambda: [state["rstd_u_read"]])

        ple = [(ple_gate, c * CHUNK, h_hi, h_lo, ready_h, ple_epilogue(c), KT) for c in range(4)]
        chunk_pair(*ple[:2])
        for c in range(2, 4):
            chunk(*ple[c])

        def ready_u2(kt):
            return [u2_ready[kt]]

        def bias_table():
            t1 = scalar.put_dma(lambda e: e.dma_start(onehot[:, :], onehot_in), late_in, [tile_done[-1]])
            t1 = scalar.put_dma(lambda e: e.dma_start(table[:, :], table_in), late_in)
            state["late"] = scalar.put_dma(lambda e: e.dma_start(ahead[:, :, :], ahead_in), late_in)

        def bias_rev():
            t = mm(misc[1][0:HEADS, 0:REV], table[:, :], onehot[:, :], True, True, [state["late"], misc_free[1]],
                   signal=True)
            t = act(rev[:, :], misc[1][0:HEADS, 0:REV], ACT.Copy, [t])
            misc_free[1] = t
            t = scalar.put_dma(lambda e: e.dma_start(rev_dram, rev[:, :]), rev_out, [t])
            state["bias"] = scalar.put_dma(lambda e: e.dma_start(bias[:, :, :], hankel), bias_in, [t])
        hankel = bass.AP(rev_dram.tensor, 0, [[1, P], [REV, HEADS], [1, T]])

        t_identb = {}

        def tail_chunk(epilogue):
            s = chunk_no[0] % 2
            chunk_no[0] += 1
            per = KT // 2
            for k0 in range(0, KT, per):
                src = w_tail[:, k0:k0 + per, :]

                def products(hi, lo, k0=k0):
                    got = []
                    for dk in range(per):
                        kt = k0 + dk
                        c = slice(dk * TAIL, (dk + 1) * TAIL)
                        o_ = acc[s][0][0:TAIL, 0, :]
                        xh, xl = u2_hi[:, kt, :], u2_lo[:, kt, :]
                        got += [(o_, hi[:, c], xh, kt == 0, False), (o_, hi[:, c], xl, False, False),
                                (o_, lo[:, c], xh, False, kt == KT - 1)]
                    return got

                def needs(half, k0=k0):
                    return (list(bank_free[s]) if k0 == 0 else []) + [t for d in range(per) for t in ready_u2(k0 + d)]
                tiles.append(Tile(src, per, per * TAIL, products, needs))
            job(len(tiles) - 1, lambda: epilogue(s))

        def tail_epilogue(s):
            kiwi = tmp[3][:, 0:T]
            t = tt(kiwi[0:TAIL, :], acc[s][0][0:TAIL, 0, :], rstd_u[0:TAIL, :], ALU.mult,
                   [tile_done[-1], state["rstd2"]] + tmp_free[3])
            evacuated(s, [t])

            def spread():
                t1 = mm(misc[1][:, 0:T], cst[0:IDX_DIM, CST["twice"][0]:CST["twice"][0] + P], kiwi[0:IDX_DIM, :],
                        True, True, [t, misc_free[1]], signal=True)
                for t_ in range(TOK_TILES):
                    t2 = mm(misc[2][:, t_ * IDX_HEADS:(t_ + 1) * IDX_HEADS], kiwi[0:TAIL, t_ * P:(t_ + 1) * P],
                            cst[0:TAIL, IDX_DIM:TAIL], True, True, [t, misc_free[2]], signal=True)
                tmp_free[3] = [t2]
                state["ki"] = misc_free[1] = act(ki[:, :], misc[1][:, 0:T], ACT.Copy, [t1])
                state["wi"] = misc_free[2] = act(wi[:, :, :].rearrange("p t h -> p (t h)"),
                                                 misc[2][:, 0:TOK_TILES * IDX_HEADS], ACT.Copy, [t2],
                                                 scale=IDX_HEADS ** -0.5)
            soon(1, spread)

        def copy_epilogue(dst, j0, key, scale=1.0):
            def go(s):
                got = [stt(dst[:, j0 + 2 * b:j0 + 2 * b + 2, :], acc[s][b][:, :, :], scale, both(rstd_u), ALU.mult,
                           ALU.mult, [tile_done[-1], state["rstd2"]]) for b in range(2)]
                evacuated(s, got)
                state[key] = got[1]
            return go

        def kv_chunk():
            s = chunk_no[0] % 2
            chunk_no[0] += 1
            for i in range(0, KT, 2):
                src = w_in[i * P:(i + 2) * P, C_KV:C_KV + CHUNK].rearrange("(k p) n -> p k n", p=P)

                def products(hi, lo, i=i):
                    got = []
                    for dk in range(2):
                        kt = i + dk
                        xh, xl = u2_hi[:, kt, :], u2_lo[:, kt, :]
                        for j in range(KV_HEADS):
                            c = dk * CHUNK + j * HD
                            o_ = acc[s][0][:, j, :]
                            wh, wl = hi[:, c:c + HD], lo[:, c:c + HD]
                            got += [(o_, wh, xh, kt == 0 and j == 0, False), (o_, wh, xl, False, False),
                                    (o_, wl, xh, False, kt == KT - 1)]
                        for t_ in range(TOK_TILES):
                            c = dk * CHUNK + KV_HEADS * HD
                            o_ = acc[s][1][:, t_, :]
                            tok = slice(t_ * P, (t_ + 1) * P)
                            wh, wl = hi[:, c:c + KV_HEADS * HD], lo[:, c:c + KV_HEADS * HD]
                            got += [(o_, xh[:, tok], wh, kt == 0 and t_ == 0, False), (o_, xl[:, tok], wh, False, False),
                                    (o_, xh[:, tok], wl, False, kt == KT - 1)]
                    return got

                tiles.append(Tile(src, 2, WCOLS, products,
                                  lambda half, i=i: (list(bank_free[s]) if i == 0 else []) + ready_u2(i + half)))

            def epilogue(s=s):
                t1 = tt(k[:, :, :], acc[s][0][:, :, :], both(rstd_u), ALU.mult, [tile_done[-1]])
                for t_ in range(TOK_TILES):
                    t2 = act(v[:, t_, :], acc[s][1][:, t_, :], ACT.Copy, [tile_done[-1], state["rstd2"]],
                             scale=rstd_col[:, t_:t_ + 1])
                evacuated(s, [t1, t2])
                state["k"], state["v"] = t1, t2
            job(len(tiles) - 1, epilogue)

        relu_free = [None, None]
        dots = {}

        def score_banks(n):
            return (1, 2) if n % 2 == 0 else (3, 0)

        def score_dots(n, t_, heads, nk):
            for i, h in enumerate(heads):
                bank = score_banks(n)[h % 2]
                lo_p = (h % 2) * IDX_DIM
                tok = mm(misc[bank][:, i // 2 * nk:(i // 2 + 1) * nk],
                         qi[lo_p:lo_p + IDX_DIM, h // 2, t_ * P:(t_ + 1) * P],
                         ki[lo_p:lo_p + IDX_DIM, 0:nk], True, True, [state["qi"], state["ki"], misc_free[bank]],
                         signal=i == len(heads) - 1)
            dots[n] = tok

        def score_relu(n, t_, heads, nk):
            for odd in range(2):
                bank = score_banks(n)[odd]
                misc_free[bank] = act(relu[n % 2][:, odd * T:(odd + 1) * T], misc[bank][:, 0:T], ACT.Relu,
                                      [dots[n], relu_free[n % 2]])
            dots[n] = misc_free[bank]

        def score_add(n, t_, heads, nk):
            for i, h in enumerate(heads):
                base = ahead if h == 0 else score
                at_ = (h % 2) * T + i // 2 * nk
                tok = stt(score[:, t_, 0:nk], relu[n % 2][:, at_:at_ + nk], wi[:, t_, h:h + 1],
                          base[:, t_, 0:nk], ALU.mult, ALU.add,
                          [dots[n], state["late"], state["wi"], state.get("score")])
                state["score"] = tok
            relu_free[n % 2] = tok

        def topk_round(t_, r, nk):
            src = score[:, t_, 0:nk] if r == 0 else left[:, 0:nk]
            tok = vec_do(lambda e: e.max(top8[:, :], src), [state["score"], state.get("mask")])
            state["score"] = vec_do(lambda e: e.match_replace(left[:, 0:nk], top8[:, :], src, TAKEN), [tok])

        def topk_mask(t_, nk):
            tok = ts(left[:, 0:nk], left[:, 0:nk], 2 * MASKED, UNSELECTED, ALU.is_ge, ALU.mult, [state["score"]])
            state["mask"] = tt(mask[:, t_, 0:nk], left[:, 0:nk], ahead[:, t_, 0:nk], ALU.add, [tok])

        unit = {}

        def a_logits(n, t_, heads, nk):
            for i, h in enumerate(heads):
                o_ = misc[1][:, i * nk:(i + 1) * nk]
                off = (TOK_TILES - 1 - t_) * P
                mm(o_, q[:, h, t_ * P:(t_ + 1) * P], k[:, h // GROUP, 0:nk], True, False,
                   [state["q"], state["k"], misc_free[1]])
                mm(o_, c_of("flip"), bias[:, h, off:off + nk], False, False, [state["bias"]])
                tok = mm(o_, ident_b[:, :], mask[:, t_, 0:nk], False, True, [state["mask"], state["identb"]],
                         signal=i == len(heads) - 1)
            unit[n] = tok

        def a_max(n, t_, heads, nk):
            g = len(heads)
            src = misc[1][:, 0:g * nk].rearrange("p (g k) -> p g k", g=g)
            m_ = row_max[:, n % 2, 0:g]
            tok = vec_do(lambda e: e.reduce_max(m_, src, AX_X), [unit[n]])
            unit[n] = ts(m_, m_, -1.0, None, ALU.mult, None, [tok])

        def a_exp(n, t_, heads, nk):
            for i, h in enumerate(heads):
                tok = act(prob[n % 2][:, i * nk:(i + 1) * nk], misc[1][:, i * nk:(i + 1) * nk], ACT.Exp,
                          [unit[n], unit.get(("prob_free", n % 2))], bias=row_max[:, n % 2, i:i + 1],
                          accum=row_sum[:, n % 2, i:i + 1])
            misc_free[1] = tok
            unit[n] = tok

        def a_norm(n, t_, heads, nk):
            g = len(heads)
            rs = row_sum[:, n % 2, 0:g]
            tok = vec_do(lambda e: e.reciprocal(rs, rs), [unit[n]])
            for i in range(g):
                pr = prob[n % 2][:, i * nk:(i + 1) * nk]
                last = ts(pr, pr, row_sum[:, n % 2, i:i + 1], None, ALU.mult, None, [tok])
            unit[n] = last

        def a_turn(n, t_, heads, nk):
            for b in range(4):
                dst, src = misc[2][:, b * P:(b + 1) * P], prob[n % 2][:, b * P:(b + 1) * P]
                tok = tensor.put(lambda e, dst=dst, src=src: e.transpose(dst, src, c_of("ident")),
                                 [unit[n], misc_free[2]], b == 3)
            unit["prob_free", n % 2] = tok
            unit[n] = tok

        def a_turned(n, t_, heads, nk):
            tok = act(flat(prob_t[n % 2][:, :, :]), misc[2][:, :], ACT.Copy,
                      [unit[n], unit.get(("prob_t_free", n % 2))])
            misc_free[2] = tok
            unit[n] = tok

        def a_values(n, t_, heads, nk):
            kb = nk // P
            for i, h in enumerate(heads):
                g = h // GROUP
                for b in range(kb):
                    tok = mm(misc[3][:, i * P:(i + 1) * P], v[:, b, g * HD:(g + 1) * HD],
                             prob_t[n % 2][:, i * kb + b, :], b == 0, b == kb - 1, [unit[n], state["v"], misc_free[3]],
                             signal=i == len(heads) - 1 and b == kb - 1)
            unit["prob_t_free", n % 2] = tok
            unit[n] = tok

        def a_out_split(n, t_, heads, nk):
            g, h0 = len(heads), heads[0]
            src = misc[3][:, 0:g * P].rearrange("p (g q) -> p g q", g=g)
            hi, lo = (b_[:, h0:h0 + g, t_ * P:(t_ + 1) * P] for b_ in (o_hi, o_lo))
            t1 = act(hi, src, ACT.Copy, [unit[n], state["scores_done"], state["logits_done"]])
            misc_free[3] = tt(lo, src, as32(hi), ALU.subtract, [t1])
            state["attn"] = misc_free[3]

        def plan_attention(step):
            n = 0
            for t_, per, nk in ((0, 4, P), (1, 2, T)):
                for h in range(0, IDX_HEADS, per):
                    hh = list(range(h, h + per))
                    for d, fn in enumerate((score_dots, score_relu, score_add)):
                        job(step + n + d, lambda fn=fn, n=n, t_=t_, hh=hh, nk=nk: fn(n, t_, hh, nk))
                    n += 1
            step += n + 2

            def scored():
                state["scores_done"] = state["score"]
            job(step, scored)
            for t_, nk in ((0, P), (1, T)):
                for r in range(0, TOPK // 8, 2):
                    job(step, lambda t_=t_, r=r, nk=nk: (topk_round(t_, r, nk), topk_round(t_, r + 1, nk)))
                    step += 1
                job(step - 1, lambda t_=t_, nk=nk: topk_mask(t_, nk))
            units = [(0, list(range(h, h + 4)), P) for h in range(0, HEADS, 4)] + \
                    [(1, list(range(h, h + 2)), T) for h in range(0, HEADS, 2)]
            stages = (a_logits, a_max, a_exp, a_norm, a_turn, a_turned, a_values, a_out_split)
            return units, stages, step

        chunk_pair(*((w_in, C_QI + c * CHUNK, u2_hi, u2_lo, ready_u2, copy_epilogue(qi, 4 * c, "qi"), KT)
                     for c in range(2)))

        def make_identb():
            state["identb"] = vec_do(lambda e: e.tensor_copy(ident_b[:, :], c_of("ident")), [(cst_loaded[0], 16)])
        job(len(tiles) - 7, bias_table)
        job(len(tiles) - 5, make_identb)
        job(len(tiles) - 3, bias_rev)
        tail_chunk(tail_epilogue)
        score_step = len(tiles) + 1
        for c in range(2):
            chunk(w_in, C_Q + c * CHUNK, u2_hi, u2_lo, ready_u2, copy_epilogue(q, 4 * c, "q", HD ** -0.5), KT)
        kv_chunk()
        kv_end = len(tiles) - 1
        units, stages, attn_step = plan_attention(score_step)
        attn_step = max(attn_step, kv_end) + 1

        order = [units[2], units[3], units[0], units[4], units[5], units[1]]

        n_units = len(order)
        GAP = 3
        for n, (t_, hh, nk) in enumerate(order):
            for d, fn in enumerate(stages):
                def run(fn=fn, n=n, t_=t_, hh=hh, nk=nk):
                    fn(n, t_, hh, nk)
                if fn is not a_out_split:
                    job(attn_step + GAP * n + d, run)
        for n, (t_, hh, nk) in enumerate(order):
            def run_out(n=n, t_=t_, hh=hh, nk=nk):
                state["logits_done"] = unit["logits", n // 3 * 3 + 2]
                a_out_split(n, t_, hh, nk)
            job(attn_step + GAP * n + 7, run_out)
        for n in (2, 5):
            def keep(n=n):
                unit["logits", n] = unit[n]
            jobs[attn_step + GAP * n].append(keep)

        b_ready = {}

        def pool_epilogue(c):
            def go(s):
                got = [tt(pool_u[:, 2 * b:2 * b + 2, :], acc[s][b][:, :, :], both(rstd_u), ALU.mult,
                          [tile_done[-1], state.get("pool_u_free")]) for b in range(2)]
                evacuated(s, got)
                for g in range(2):
                    soon(3 * g + 1, lambda g=g: window_sums(c, g, got[g]))
                    soon(3 * g + 3, lambda g=g: pool_difference(c, g))
            return go

        window = {}

        def window_sums(c, g, t):
            w_ = POOL_WINDOWS[2 * c + g]
            window["src"], window["t"], window["n"] = pool_u[:, 2 * g:2 * g + 2, :], t, 0

            def double(have):
                n, src, t = window["n"], window["src"], window["t"]
                dst = tmp[n % 2][:, :].rearrange("p (k t) -> p k t", k=2)
                vec_do(lambda e: e.tensor_copy(dst[:, :, 0:have], src[:, :, 0:have]), [t] + tmp_free[n % 2])
                window["t"] = tt(dst[:, :, have:], src[:, :, have:], src[:, :, 0:T - have], ALU.add, [t])
                window["src"], window["n"] = dst, n + 1
            have = 1
            while have < w_:
                soon(0 if have < 4 else 1, lambda have=have: double(have))
                have *= 2

        def pool_difference(c, g):
            gg = 2 * c + g
            src, t, n = window["src"], window["t"], window["n"]
            ic = cst[:, CST["inv_count"][0] + gg * PAD_POOL:CST["inv_count"][0] + (gg + 1) * PAD_POOL]
            mean = tmp[n % 2][:, :].rearrange("p (k t) -> p k t", k=2)
            for d in range(2):
                tt(mean[:, d, 0:PAD_POOL], src[:, d, 0:PAD_POOL], ic, ALU.mult, [t] + tmp_free[n % 2])
            t = stt(mean[:, :, PAD_POOL:], src[:, :, PAD_POOL:], 1.0 / POOL_WINDOWS[gg],
                    pool_u[:, 2 * g:2 * g + 2, PAD_POOL:], ALU.mult, ALU.subtract)
            t = tt(mean[:, :, 0:PAD_POOL], mean[:, :, 0:PAD_POOL], pool_u[:, 2 * g:2 * g + 2, 0:PAD_POOL],
                   ALU.subtract, [t])
            state["pool_u_free"] = t
            tmp_free[(n + 1) % 2] = [t]
            t = split(flat(d_hi[:, 2 * g:2 * g + 2, :]), flat(d_lo[:, 2 * g:2 * g + 2, :]), tmp[n % 2][:, :],
                      [t, state.get("d_free")])
            tmp_free[n % 2] = [t]
            state["d", c, g] = t

        def pool_out_chunk(c):
            s = chunk_no[0] % 2
            chunk_no[0] += 1
            block_tile(pool_w, 2 * c, acc[s], d_hi, d_lo,
                       lambda half: list(bank_free[s]) + [state["d", c, 0], state["d", c, 1]],
                       lambda: pool_out_epilogue(c)(s))

        def pool_out_epilogue(c):
            def go(s):
                state["d_free"] = tile_done[-1]
                got = []
                for b in range(2):
                    bb = tmp[b]
                    for d in range(2):
                        kt = 4 * c + 2 * b + d
                        t = act(bb[:, d * T:(d + 1) * T], acc[s][b][:, d, :], ACT.Copy, [tile_done[-1]] + tmp_free[b],
                                scale=v_of("pool_scale", kt))
                    got.append(t)
                    kt = 4 * c + 2 * b
                    t = split(flat(b_hi[:, kt:kt + 2, :]), flat(b_lo[:, kt:kt + 2, :]), bb[:, :], [t])
                    tmp_free[b] = [t]
                    b_ready[kt // 2] = t
                evacuated(s, got)
            return go

        state["pool_end"] = {}
        for c in range(2):
            chunk(w_in, C_POOL + c * CHUNK, u2_hi, u2_lo, ready_u2, pool_epilogue(c), KT)
            state["pool_end"][c] = len(tiles) - 1

            def uconv_epilogue(s, c=c):
                got = [tt(conv_u[:, 2 * b:2 * b + 2, :], acc[s][b][:, :, :], both(rstd_u), ALU.mult,
                          [tile_done[-1], state.get("conv_u_free")]) for b in range(2)]
                evacuated(s, got)
                state["conv_u"] = got[1]
            if c == 0:
                chunk(w_in, C_UCONV, u2_hi, u2_lo, ready_u2, uconv_epilogue, KT)
                pool_out_chunk(0)

        def cgate_epilogue(c):
            def go(s):
                got = []
                for b in range(2):
                    z_ = conv_z[:, 2 * b:2 * b + 2, :]
                    got.append(tt(z_, acc[s][b][:, :, :], both(rstd_u), ALU.mult,
                                  [tile_done[-1], state["pool_u_free"]]))
                    t = tt(z_, z_, conv_u[:, 2 * b:2 * b + 2, :], ALU.mult, [got[b], state["conv_u"]])
                evacuated(s, got)
                state["conv_u_free"] = t
                soon(1, lambda: conv2(c, (0, 1), t))
                soon(2, lambda: conv2(c, (2, 3), t))
            return go

        def conv2(c, js, t_z):
            toks = {}
            for back in range(CONV2_W):
                for j in js:
                    w_ = v_of("conv_w", (4 * c + j) * CONV2_W + CONV2_W - 1 - back)
                    if back == 0:
                        toks[j] = ts(conv_y[:, j, :], conv_z[:, j, :], w_, None, ALU.mult, None,
                                     [t_z, state["d_free"]])
                    else:
                        toks[j] = stt(conv_y[:, j, back:], conv_z[:, j, 0:T - back], w_, conv_y[:, j, back:],
                                      ALU.mult, ALU.add, [toks[j]])
            state["conv_y"] = toks[js[-1]]

        def bgate_epilogue(c):
            def go(s):
                got = []
                for b in range(2):
                    bb = tmp[b]
                    got.append(tt(bb[:, :].rearrange("p (k t) -> p k t", k=2), acc[s][b][:, :, :], both(rstd_u),
                                  ALU.mult, [tile_done[-1]] + tmp_free[b]))

                def gated(b):
                    bb = tmp[b]
                    kt = HALF // P + 4 * c + 2 * b
                    t = tt(bb[:, :], bb[:, :], flat(conv_y[:, 2 * b:2 * b + 2, :]), ALU.mult,
                           [got[b], state["conv_y"]])
                    t = split(flat(b_hi[:, kt:kt + 2, :]), flat(b_lo[:, kt:kt + 2, :]), bb[:, :], [t])
                    tmp_free[b] = [t]
                    b_ready[kt // 2] = t
                    mix["y_free"] = t
                soon(1, lambda: gated(0))
                soon(2, lambda: gated(1))
                evacuated(s, got)
            return go

        def uconv1(s):
            got = [tt(conv_u[:, 2 * b:2 * b + 2, :], acc[s][b][:, :, :], both(rstd_u), ALU.mult,
                      [tile_done[-1], state["conv_u_free"]]) for b in range(2)]
            evacuated(s, got)
            state["conv_u"] = got[1]

        mix = {}

        def gate_chunk(n, c):
            def go(s):
                got = [tt(gates[:, 2 * b:2 * b + 2, :], acc[s][b][:, :, :], both(rstd_u), ALU.mult,
                          [tile_done[-1], mix.get("gates_free")]) for b in range(2)]
                evacuated(s, got)

                def sigmoids():
                    for j in range(4):
                        t = act(gates[:, j, :], gates[:, j, :], ACT.Sigmoid, [got[j // 2]],
                                bias=v_of("b_gate", n * KT + 4 * c + j))
                    mix["gates"] = t
                soon(1, sigmoids)
            chunk(w_gate, n * D + c * CHUNK, u2_hi, u2_lo, ready_u2, go, KT)

        def up_chunk(n, c, hi, lo, k0, ready):
            def go(s):
                got = []
                for b in range(2):
                    j = 4 * c + 2 * b
                    g = flat(gates[:, 2 * b:2 * b + 2, :])
                    ys = flat(y[:, j:j + 2, :])
                    if n == 0:
                        got.append(tt(ys, flat(acc[s][b][:, :, :]), g, ALU.mult,
                                      [tile_done[-1], mix["gates"], mix["y_free"]]))
                        continue
                    bb = tmp[b]
                    got.append(tt(bb[:, :], flat(acc[s][b][:, :, :]), g, ALU.mult,
                                  [tile_done[-1], mix["gates"]] + tmp_free[b]))
                    t = tt(ys, ys, bb[:, :], ALU.add, [got[b]])
                    tmp_free[b] = [t]
                    if n == 2:
                        split_later(flat(mix_hi[:, j:j + 2, :]), flat(mix_lo[:, j:j + 2, :]), ys, [t],
                                    lambda t, b=b: mix.__setitem__(("mixed", 2 * c + b), t))
                evacuated(s, got)
                mix["gates_free"] = got[1]
            chunk(w_branch[n], c * CHUNK, hi, lo, ready, go, HALF // P, k0=k0)

        gate_chunk(0, 0)
        pool_out_chunk(1)
        for c in range(2):
            if c == 1:
                chunk(w_in, C_UCONV + CHUNK, u2_hi, u2_lo, ready_u2, uconv1, KT)
            chunk(w_in, C_CGATE + c * CHUNK, u2_hi, u2_lo, ready_u2, cgate_epilogue(c), KT)
            chunk(w_in, C_BGATE + c * CHUNK, u2_hi, u2_lo, ready_u2, bgate_epilogue(c), KT)

        def ready_b(kt):
            return [b_ready[kt // 2]]

        sources = [(b_hi, b_lo, 0, ready_b), (b_hi, b_lo, HALF // P, ready_b),
                   (o_hi, o_lo, 0, lambda kt: [state["attn"]])]
        for n in range(3):
            for c in range(4):
                if (n, c) != (0, 0):
                    gate_chunk(n, c)
                up_chunk(n, c, *sources[n][:2], sources[n][2], sources[n][3])
        attn_needed = len(tiles) - 4 * 4 - 3 * 8
        assert attn_step + GAP * n_units + 8 < attn_needed

        def ready_mix(kt):
            return [mix["mixed", kt // 2]]

        for c in range(3):
            chunk(w_out, c * CHUNK, mix_hi, mix_lo, ready_mix, y_epilogue(c, "gain1"), KT)
            if c == 1:
                job(len(tiles) - 1, load_sqrt)
        u3_ready, x_final = {}, {}

        def after_out(t_rstd):
            state["rstd_y3"] = t_rstd
            soon(15, load_gain_row)
            for j in range(KT // 2):
                soon(max(2 * j - 1, 0), lambda j=j: residual3(j))
                soon(min(2 * j + 8, j + 11), lambda j=j: add_squares(flat(x[:, 2 * j:2 * j + 2, :]), [x_final[j]], j == 0))
            soon(KT + 3, lambda: plan_rms_u("rstd3", lambda: square_sums(0, all_squares(), [sq["t"]]),
                                            lambda: [mix["gates"]]))

        def load_gain_row():
            state["gain3_row"] = scalar.put_dma(lambda e: e.dma_start(gain3_row[:, :], gain3_in.broadcast_to([P, D])),
                                                gain_row_in, [tile_done[-1]])
        gain_row_in = [sem("gain_row_in"), 0]

        def residual3(j):
            t = residual_pair(j, state["rstd_y3"], [state["y"]] if j >= 6 else [])
            x_final[j] = t
            gained_split(2 * j, "gain2", u3_hi, u3_lo, [t], u3_ready, 0)
        chunk(w_out, 3 * CHUNK, mix_hi, mix_lo, ready_mix, y_last("gain1", after_out), KT)

        hid_ready = {}

        def up_epilogue(c):
            n0 = 2 * (c % 2)
            buf = tmp[n0:n0 + 2]

            def go(s):
                got = []
                for b in range(2):
                    got.append(stt(buf[b][:, :].rearrange("p (k t) -> p k t", k=2), acc[s][b][:, :, :], 0.0,
                                   both(rstd_u), ALU.max, ALU.mult, [tile_done[-1], state["rstd3"]] + tmp_free[n0 + b]))
                evacuated(s, got)

                low_of = {}

                def hidden():
                    for b in range(2):
                        j = 4 * c + 2 * b
                        t = act(buf[b][:, :], buf[b][:, :], ACT.Square, [got[b]])
                        low_of[b] = act(flat(hid_hi[:, j:j + 2, :]), buf[b][:, :], ACT.Copy, [t])

                def lows():
                    for b in range(2):
                        j = 4 * c + 2 * b
                        t = tt(flat(hid_lo[:, j:j + 2, :]), buf[b][:, :], as32(flat(hid_hi[:, j:j + 2, :])),
                               ALU.subtract, [low_of[b]])
                        tmp_free[n0 + b] = [t]
                        hid_ready[j // 2] = t
                soon(1, hidden)
                soon(2, lows)
            return go

        def turn_x(j):
            bank = 2 + j % 2
            for d in range(2):
                for t_ in range(TOK_TILES):
                    n = d * TOK_TILES + t_
                    t = tensor.put(lambda e, d=d, t_=t_, n=n: e.transpose(
                        misc[bank][:, n * P:(n + 1) * P], x[:, 2 * j + d, t_ * P:(t_ + 1) * P], c_of("ident")),
                        [misc_free[bank], u3_ready[KT - 1]], n == 3)

            def back():
                state["x_turned"] = misc_free[bank] = act(flat(x[:, 2 * j:2 * j + 2, :]), misc[bank][:, :],
                                                          ACT.Copy, [t])
            soon(1, back)

        def y_tok(t_, c):
            kt = t_ * (KT // TOK_TILES) + 2 * c
            return flat(y[:, kt:kt + 2, :])

        def down_chunk(half, c):
            s = chunk_no[0] % 2
            chunk_no[0] += 1
            rows = w_down[half * (MLP // 2):(half + 1) * (MLP // 2), :]
            per = WCOLS // CHUNK
            for i in range(0, hidden_kt, per):
                src = rows[i * P:(i + per) * P, c * CHUNK:(c + 1) * CHUNK].rearrange("(k p) n -> p k n", p=P)

                def products(hi, lo, i=i):
                    got = []
                    order = [(dk, t_) for dk in range(per) for t_ in range(TOK_TILES)]
                    if i + per == hidden_kt:
                        order.sort(key=lambda o: o[1])
                    for dk, t_ in order:
                        kt = i + dk
                        o_ = flat(acc[s][t_][:, :, :])
                        tok = slice(t_ * P, (t_ + 1) * P)
                        xh, xl = hid_hi[:, kt, tok], hid_lo[:, kt, tok]
                        wh, wl = (w_[:, dk * CHUNK:(dk + 1) * CHUNK] for w_ in (hi, lo))
                        got += [(o_, xh, wh, kt == 0, False), (o_, xh, wl, False, False),
                                (o_, xl, wh, False, kt == hidden_kt - 1)]
                    return got

                def needs(half, i=i):
                    return (list(bank_free[s]) if i == half == 0 else []) + \
                        [t for dk in range(per) for t in [hid_ready[(i + dk) // 2]]]
                tiles.append(Tile(src, per, WCOLS, products, needs))
            job(len(tiles) - 1, lambda: (down_epilogue if half == 0 else last_epilogue if c == 3 else
                                         sum_epilogue)(s, c))

        def down_epilogue(s, c):
            got = [act(y_tok(t_, c), flat(acc[s][t_][:, :, :]), ACT.Copy, [tile_done[-1], misc_free[1]])
                   for t_ in range(TOK_TILES)]
            evacuated(s, got)
            mix["half0", c] = got[1]

        def add_half(s, t_, c, after):
            return tt(y_tok(t_, c), flat(acc[s][t_][:, :, :]), y_tok(t_, c), ALU.add, [after, mix["half0", c]])

        def token_squares(t_, c, after):
            t = act(tmp[2 + t_][:, :], y_tok(t_, c), ACT.Square, [after] + tmp_free[2 + t_],
                    accum=chunk_sums[:, c, t_:t_ + 1])
            tmp_free[2 + t_] = [t]
            return t

        def gain_row_times(out_, t_, c, after):
            return tt(out_, y_tok(t_, c), gain3_row[:, c * CHUNK:(c + 1) * CHUNK], ALU.mult,
                      [after, state["gain3_row"]])

        def sum_epilogue(s, c):
            got = [add_half(s, t_, c, tile_done[-1]) for t_ in range(TOK_TILES)]
            evacuated(s, got)

            def squares_and_gain(t_):
                t = token_squares(t_, c, got[t_])
                soon(2, lambda: gain_row_times(y_tok(t_, c), t_, c, t))
                mix["squares", c, t_] = t
            for t_ in range(TOK_TILES):
                soon(t_ + 1, lambda t_=t_: squares_and_gain(t_))

            def add_up():
                t = tt(chunk_sums[:, 0, :], chunk_sums[:, 0, :], chunk_sums[:, 1, :], ALU.add,
                       [mix["squares", 2, 1]])
                t = tt(chunk_sums[:, 0, :], chunk_sums[:, 0, :], chunk_sums[:, 2, :], ALU.add, [t])
                mix["mean"] = ts(chunk_sums[:, 0, :], chunk_sums[:, 0, :], 1.0 / D, EPS, ALU.mult, ALU.add, [t])
            if c == 2:
                soon(5, add_up)

        def last_epilogue(s, c):
            rstd, scaled = {}, {}

            def complete(t_):
                t = add_half(s, t_, c, half_done[0] if t_ == 0 else tile_done[-1])
                t_sq = token_squares(t_, c, t)
                rstd[t_] = act(rstd_col[:, t_:t_ + 1], chunk_sums[:, c, t_:t_ + 1], ACT.Sqrt, [t_sq, mix["mean"]],
                               bias=chunk_sums[:, 0, t_:t_ + 1], scale=1.0 / D)
                scaled[t_] = gain_row_times(tmp[t_][:, :], t_, c, t)

            def invert(t_):
                col = rstd_col[:, t_:t_ + 1]
                rstd[t_] = vec_do(lambda e: e.reciprocal(col, col), [rstd[t_]])

            def finish(t_, c_):
                ys = (tmp[t_][:, :] if c_ == c else y_tok(t_, c_)).rearrange("p (k f) -> p k f", k=4)
                xs = x[:, 4 * c_:4 * c_ + 4, t_ * P:(t_ + 1) * P]
                t = stt(ys, ys, rstd_col[:, t_:t_ + 1], xs, ALU.mult, ALU.add, [rstd[t_], scaled[t_], state["x_turned"]])
                dst = out[t_ * P:(t_ + 1) * P, c_ * CHUNK:(c_ + 1) * CHUNK].rearrange("p (k f) -> p k f", k=4)
                sp_q.put_dma(lambda e: e.dma_start(dst, ys), out_done, [t])
            complete(0)
            invert(0)
            finish(0, 0)
            complete(1)
            finish(0, 1)
            finish(0, 2)
            invert(1)
            finish(0, 3)
            for c_ in range(4):
                finish(1, c_)
            sp_q.items.append((None, [(out_done[0], out_done[1])], None))

        NORM_DELAY = 7
        hidden_kt = MLP // 2 // P
        for half in range(2):
            ups = [(w_up, half * (MLP // 2) + c * CHUNK, u3_hi, u3_lo, lambda kt: [u3_ready[kt]],
                    up_epilogue(c), KT) for c in range(MLP // 2 // CHUNK)]
            if half == 0:
                chunk_pair(*ups[:2], delay=NORM_DELAY)
                chunk(*ups[2], s=2, delay=1)
            for c in range(3 if half == 0 else 0, len(ups)):
                chunk(*ups[c])
            if half == 0:
                for j in range(KT // 2):
                    job(len(tiles) + 2 * j - 2 * KT, lambda j=j: turn_x(j))
            for c in range(4):
                down_chunk(half, c)
                if (half, c) == (1, 1):
                    job(len(tiles), load_sqrt)

        for n in range(0, N_STAGE, 2):
            load_x(n // 2)
            load_tile(n)
            load_tile(n + 1)
        sp_q.put_dma(lambda e: e.dma_start(cst[:, :], cst_in), cst_loaded)
        for j in range(N_STAGE // 2, KT // 2):
            load_x(j)
        for n in range(AHEAD):
            if n % 2 == 0:
                first_gain(n // 2)
            split_tile(n)
        step = 0
        while step < len(tiles) or any(s_ >= step for s_ in jobs):
            if step + AHEAD < len(tiles):
                split_tile(step + AHEAD)
            if step < len(tiles):
                multiply_tile(step)
            now[0] = step
            for fn in jobs.pop(step, []):
                fn()
            step += 1

        block = ctx.enter_context(nc.Block())

        @block.sync
        def _(e):
            sp_q.play(e)

        @block.scalar
        def _(e):
            scalar.play(e)

        @block.vector
        def _(e):
            vector.play(e)

        @block.tensor
        def _(e):
            tensor.play(e)


def kernel(**inputs):
    import numpy as _np
    import concourse.bacc as _bacc
    from concourse import mybir as _mybir
    from concourse.bass_utils import run_bass_kernel_spmd as _run

    get = {k_: _np.asarray(v_) for k_, v_ in inputs.items()}

    def features(a, extra=()):
        a = a.reshape(-1, a.shape[-1] // P, P)
        return _np.ascontiguousarray(a.transpose(2, 1, 0))

    def columns(a):
        return features(a).reshape(P, -1)

    gains = get["norm_gains_2"][0]
    parts = {
        "norm_pre": get["norm_pre"][0], "norm_post": get["norm_post"][0],
        "gain0": gains[0], "gain1": gains[1], "gain2": gains[2],
        "a_conv_w": get["a_conv_w"][0], "a_conv_b": get["a_conv_b"][0],
        "b_r": get["a_b_r"][0].reshape(-1), "b_i": get["a_b_i"][0].reshape(-1), "lam": get["a_lam"][0],
        "pool_scale": get["pool_scale_2"][0], "conv_w": get["conv_w_2"][0],
    }
    packed = [columns(parts[name]) for name, _ in VEC_SIZES[:-1]]
    packed.append(get["b_gate_2"][0].reshape(3, KT, P).transpose(2, 0, 1).reshape(P, -1))
    cst, ahead, onehot = shape_constants()
    w_in = get["w_in_2"][0]
    tail = w_in[:, C_KI:]
    arrays = {
        "x": features(get["x"][0]), "p": features(get["p"][0, 0]).reshape(P, -1),
        "vec": _np.concatenate(packed, axis=1), "cst": cst, "ahead": ahead, "onehot": onehot,
        "table": get["rel_bias_2"],
        "ple_proj": get["ple_w_proj"][0], "ple_gate": get["ple_w_gate"][0], "a_in": get["a_w_in"][0],
        "a_r": get["a_w_r"][0], "a_i": get["a_w_i"][0], "a_out": get["a_w_out"][0], "w_in": w_in,
        "w_tail": tail.reshape(KT, P, TAIL).transpose(1, 0, 2), "pool_w": get["pool_w_2"][0],
        "w_branch": get["w_branch_2"][0], "w_gate": get["w_gate_2"][0], "w_out": get["w_out_2"][0],
        "w_up": get["w_up_2"][0], "w_down": get["w_down_2"][0],
        "gain3": gains[3:4],
    }
    arrays = {f"in_{k_}": _np.ascontiguousarray(v_) for k_, v_ in arrays.items()}
    nc = _bacc.Bacc("TRN2", target_bir_lowering=False, num_devices=1)
    ap = {k_[3:]: nc.dram_tensor(k_, v_.shape, _mybir.dt.from_np(v_.dtype), kind="ExternalInput").ap()
          for k_, v_ in arrays.items()}
    out = nc.dram_tensor("out_dram", (T, D), _mybir.dt.float32, kind="ExternalOutput").ap()
    rev_dram = nc.dram_tensor("rev_dram", (HEADS, REV), _mybir.dt.float32).ap()
    build(nc, ap["x"], ap["p"], ap["vec"], ap["cst"], ap["ahead"], ap["onehot"], ap["table"], rev_dram,
          ap["ple_proj"], ap["ple_gate"], ap["a_in"], ap["a_r"], ap["a_i"], ap["a_out"], ap["w_in"], ap["w_tail"],
          ap["pool_w"], ap["w_branch"], ap["w_gate"], ap["w_out"], ap["w_up"], ap["w_down"],
          ap["gain3"], out)
    got = _run(nc, [arrays], core_ids=[0]).results[0]["out_dram"]
    return _np.ascontiguousarray(got).reshape(1, T, D)
```
